# Optimizing a Trainium2 kernel written in Bass

```python
import jax
import jax.numpy as jnp
from jax import lax
import numpy as np
import jax, jax.numpy as jnp

D_MODEL = 1024
BATCH = 1
SEQ = 256
DEPTH = 2

GRID_W = 64
CTX_LEN = 256

FNET_GROUPS = 4
FNET_GROUP_DIM = 128
FNET_WIDTH = FNET_GROUPS * FNET_GROUP_DIM

NA_HEADS = 8
NA_HEAD_DIM = 64
NA_WIDTH = NA_HEADS * NA_HEAD_DIM
NA_KH = 8
NA_KW = 16
NA_SCALE = NA_HEAD_DIM ** -0.5

MLA_HEADS = 8
MLA_Q_LORA = 256
MLA_KV_LORA = 128
MLA_NOPE_DIM = 64
MLA_ROPE_DIM = 32
MLA_V_DIM = 64
MLA_WIDTH = MLA_HEADS * MLA_V_DIM
MLA_SCALE = (MLA_NOPE_DIM + MLA_ROPE_DIM) ** -0.5
ATTN_BLOCK = 128
ROPE_BASE = 10000.0

N_BRANCH = 3
BRANCH_DIM = 512

FFN_HIDDEN = -(-8 * D_MODEL // (3 * 256)) * 256

NORM_EPS = 1e-5
DEEPNORM_ALPHA = (2 * DEPTH) ** 0.25
DEEPNORM_BETA = (8 * DEPTH) ** -0.25

IN_SIZES = (FNET_WIDTH, NA_WIDTH, NA_WIDTH, NA_WIDTH, MLA_Q_LORA, MLA_KV_LORA, MLA_ROPE_DIM, N_BRANCH * D_MODEL)
IN_DIM = int(sum(IN_SIZES))
IN_OFFSETS = [int(v) for v in np.cumsum(IN_SIZES)[:-1]]


def layer_norm(x, g, b):
    xf = x.astype(jnp.float32)
    mu = jnp.mean(xf, axis=-1, keepdims=True)
    var = jnp.mean(jnp.square(xf - mu), axis=-1, keepdims=True)
    y = (xf - mu) * lax.rsqrt(var + NORM_EPS) * g.astype(jnp.float32) + b.astype(jnp.float32)
    return y.astype(x.dtype)

def rms_norm(x, g):
    xf = x.astype(jnp.float32)
    y = xf * lax.rsqrt(jnp.mean(jnp.square(xf), axis=-1, keepdims=True) + NORM_EPS) * g.astype(jnp.float32)
    return y.astype(x.dtype)

def rope_tables(n):
    t = jnp.arange(n, dtype=jnp.int32)
    rows = (t // GRID_W).astype(jnp.float32)
    cols = (t % GRID_W).astype(jnp.float32)
    n_freq = MLA_ROPE_DIM // 4
    inv_freq = ROPE_BASE ** (-jnp.arange(n_freq, dtype=jnp.float32) / n_freq)
    ang = jnp.concatenate([rows[:, None] * inv_freq, cols[:, None] * inv_freq], axis=-1)
    return jnp.cos(ang), jnp.sin(ang)

def axial_rope(x, cos, sin):
    xf = x.astype(jnp.float32)
    half = x.shape[-1] // 2
    x1, x2 = xf[..., :half], xf[..., half:]
    return jnp.concatenate([x1 * cos - x2 * sin, x2 * cos + x1 * sin], axis=-1).astype(x.dtype)

def split_heads(z, n_heads):
    b, n, w = z.shape
    return z.reshape(b, n, n_heads, w // n_heads)

def fourier_mix(z):
    b, n, _ = z.shape
    zg = z.reshape(b, n, FNET_GROUPS, FNET_GROUP_DIM).astype(jnp.float32)
    y = jnp.fft.fft2(zg, axes=(1, 3), norm='ortho').real
    return y.reshape(b, n, FNET_WIDTH).astype(z.dtype)

def softmax_attend(q, k, v, scale):
    s = jnp.einsum('bqhd,bkhd->bhqk', q, k, preferred_element_type=jnp.float32) * scale
    p = jax.nn.softmax(s, axis=-1).astype(v.dtype)
    return jnp.einsum('bhqk,bkhd->bqhd', p, v)

def blocked_attend(q, k, v, scale):
    b, n, h, dq = q.shape
    qb = q.reshape(b, n // ATTN_BLOCK, ATTN_BLOCK, h, dq).transpose(1, 0, 2, 3, 4)
    out = lax.map(lambda qi: softmax_attend(qi, k, v, scale), qb)
    return out.transpose(1, 0, 2, 3, 4).reshape(b, n, h, v.shape[-1])

def neighbourhood_attention(q, k, v, k_ctx, v_ctx, rpb, n_rows):
    b, n, h, dh = q.shape
    kh = min(NA_KH, n_rows)
    kw = NA_KW
    qg = q.reshape(b, n_rows, GRID_W, h, dh).transpose(1, 0, 2, 3, 4)
    kg = k.reshape(b, n_rows, GRID_W, h, dh)
    vg = v.reshape(b, n_rows, GRID_W, h, dh)
    cols = jnp.arange(GRID_W, dtype=jnp.int32)
    col_start = jnp.clip(cols - kw // 2, 0, GRID_W - kw)
    col_idx = col_start[:, None] + jnp.arange(kw, dtype=jnp.int32)
    dc = col_idx - cols[:, None] + (NA_KW - 1)
    rpb_c = rpb.astype(jnp.float32)[:, :, dc]
    n_loc = kh * kw

    def row_fn(args):
        r, q_r = args
        rs = jnp.clip(r - kh // 2, 0, n_rows - kh)
        k_rows = lax.dynamic_slice_in_dim(kg, rs, kh, axis=1)
        v_rows = lax.dynamic_slice_in_dim(vg, rs, kh, axis=1)
        k_win = k_rows[:, :, col_idx]
        v_win = v_rows[:, :, col_idx]
        dr = rs + jnp.arange(kh, dtype=jnp.int32) - r + (NA_KH - 1)
        bias = jnp.take(rpb_c, dr, axis=1).transpose(0, 2, 1, 3)
        s_loc = jnp.einsum('bwhd,bkwjhd->bhwkj', q_r, k_win, preferred_element_type=jnp.float32) * NA_SCALE + bias[None]
        s_ctx = jnp.einsum('bwhd,bchd->bhwc', q_r, k_ctx, preferred_element_type=jnp.float32) * NA_SCALE
        s = jnp.concatenate([s_loc.reshape(b, h, GRID_W, n_loc), s_ctx], axis=-1)
        p = jax.nn.softmax(s, axis=-1).astype(v.dtype)
        p_loc = p[..., :n_loc].reshape(b, h, GRID_W, kh, kw)
        p_ctx = p[..., n_loc:]
        return (jnp.einsum('bhwkj,bkwjhd->bwhd', p_loc, v_win)
                + jnp.einsum('bhwc,bchd->bwhd', p_ctx, v_ctx))

    out = lax.map(row_fn, (jnp.arange(n_rows, dtype=jnp.int32), qg))
    return out.transpose(1, 0, 2, 3, 4).reshape(b, n, h * dh)

def mla_queries(cq, g_q, w_uq, w_qr, rope):
    b, n, _ = cq.shape
    cq = rms_norm(cq, g_q)
    q_nope = (cq @ w_uq).reshape(b, n, MLA_HEADS, MLA_NOPE_DIM)
    q_rope = (cq @ w_qr).reshape(b, n, MLA_HEADS, MLA_ROPE_DIM)
    if rope is not None:
        q_rope = axial_rope(q_rope, rope[0][:, None, :], rope[1][:, None, :])
    return jnp.concatenate([q_nope, q_rope], axis=-1)

def mla_keys_values(ckv, kr, g_kv, w_uk, w_uv, rope):
    b, n, _ = ckv.shape
    ckv = rms_norm(ckv, g_kv)
    k_nope = (ckv @ w_uk).reshape(b, n, MLA_HEADS, MLA_NOPE_DIM)
    v = (ckv @ w_uv).reshape(b, n, MLA_HEADS, MLA_V_DIM)
    if rope is not None:
        kr = axial_rope(kr, rope[0], rope[1])
    k_rope = jnp.broadcast_to(kr[:, :, None, :], (b, n, MLA_HEADS, MLA_ROPE_DIM))
    return jnp.concatenate([k_nope, k_rope], axis=-1), v

def merge_branches(ys, g, w_branch, w_out):
    b, n, _ = g.shape
    y = jnp.stack(ys, axis=2)
    proj = jnp.einsum('bngi,gio->bngo', y, w_branch)
    gate = jax.nn.sigmoid(g.reshape(b, n, N_BRANCH, D_MODEL).astype(jnp.float32)).astype(proj.dtype)
    return jnp.sum(gate * proj, axis=2) @ w_out

def mixer(h, hc, lp, rope, n_rows, need_ctx):
    b, n, _ = h.shape
    f, nq, nk, nv, cq, ckv, kr, g = jnp.split(h @ lp['w_in'], IN_OFFSETS, axis=-1)
    fc, nqc, nkc, nvc, cqc, ckvc, krc, gc = jnp.split(hc @ lp['w_in'], IN_OFFSETS, axis=-1)
    na_kc, na_vc = split_heads(nkc, NA_HEADS), split_heads(nvc, NA_HEADS)
    mla_kc, mla_vc = mla_keys_values(ckvc, krc, lp['g_kv'], lp['w_uk'], lp['w_uv'], None)
    y_f = fourier_mix(f)
    y_na = neighbourhood_attention(split_heads(nq, NA_HEADS), split_heads(nk, NA_HEADS), split_heads(nv, NA_HEADS),
                                   na_kc, na_vc, lp['rpb'], n_rows)
    mla_k, mla_v = mla_keys_values(ckv, kr, lp['g_kv'], lp['w_uk'], lp['w_uv'], rope)
    mla_q = mla_queries(cq, lp['g_q'], lp['w_uq'], lp['w_qr'], rope)
    y_mla = blocked_attend(mla_q, jnp.concatenate([mla_kc, mla_k], axis=1),
                           jnp.concatenate([mla_vc, mla_v], axis=1), MLA_SCALE).reshape(b, n, MLA_WIDTH)
    out = merge_branches([y_f, y_na, y_mla], g, lp['w_branch'], lp['w_out'])
    if not need_ctx:
        return out, None
    n_ctx = hc.shape[1]
    yc_f = fourier_mix(fc)
    yc_na = softmax_attend(split_heads(nqc, NA_HEADS), na_kc, na_vc, NA_SCALE).reshape(b, n_ctx, NA_WIDTH)
    mla_qc = mla_queries(cqc, lp['g_q'], lp['w_uq'], lp['w_qr'], None)
    yc_mla = softmax_attend(mla_qc, mla_kc, mla_vc, MLA_SCALE).reshape(b, n_ctx, MLA_WIDTH)
    out_c = merge_branches([yc_f, yc_na, yc_mla], gc, lp['w_branch'], lp['w_out'])
    return out, out_c

def swiglu(h, w_gate, w_up, w_down):
    return (jax.nn.silu(h @ w_gate) * (h @ w_up)) @ w_down

def first_inputs(seed: int = 0) -> dict:
    key = jax.random.key(seed)
    ks = jax.random.split(key, 32)

    def nrm(k, shape, scale):
        return jax.random.normal(k, shape, dtype=jnp.float32) * scale

    L, D, F = DEPTH, D_MODEL, FFN_HIDDEN
    return {
        'x': nrm(ks[0], (BATCH, SEQ, D), 1.0),
        'c': nrm(ks[1], (BATCH, D), 1.0),
        'ctx': nrm(ks[2], (BATCH, CTX_LEN, D), 1.0),
        'c_ctx': nrm(ks[3], (D,), 1.0),
        'ln_in_g': 1.0 + nrm(ks[4], (D,), 0.02),
        'ln_in_b': nrm(ks[5], (D,), 0.02),
        'w_mod': nrm(ks[6], (L, D, 6 * D), 0.1 * D ** -0.5),
        'b_mod': nrm(ks[7], (L, 6 * D), 0.02),
        'w_in': nrm(ks[8], (L, D, IN_DIM), D ** -0.5),
        'mla_q_norm_g': 1.0 + nrm(ks[9], (L, MLA_Q_LORA), 0.02),
        'mla_kv_norm_g': 1.0 + nrm(ks[10], (L, MLA_KV_LORA), 0.02),
        'w_uq': nrm(ks[11], (L, MLA_Q_LORA, MLA_HEADS * MLA_NOPE_DIM), MLA_Q_LORA ** -0.5),
        'w_qr': nrm(ks[12], (L, MLA_Q_LORA, MLA_HEADS * MLA_ROPE_DIM), MLA_Q_LORA ** -0.5),
        'w_uk': nrm(ks[13], (L, MLA_KV_LORA, MLA_HEADS * MLA_NOPE_DIM), MLA_KV_LORA ** -0.5),
        'w_uv': nrm(ks[14], (L, MLA_KV_LORA, MLA_HEADS * MLA_V_DIM), MLA_KV_LORA ** -0.5),
        'na_rpb': nrm(ks[15], (L, NA_HEADS, 2 * NA_KH - 1, 2 * NA_KW - 1), 0.1),
        'w_branch': nrm(ks[16], (L, N_BRANCH, BRANCH_DIM, D), BRANCH_DIM ** -0.5),
        'w_out': nrm(ks[17], (L, D, D), DEEPNORM_BETA * D ** -0.5),
        'ln1_g': 1.0 + nrm(ks[18], (L, D), 0.02),
        'ln1_b': nrm(ks[19], (L, D), 0.02),
        'ln2_g': 1.0 + nrm(ks[20], (L, D), 0.02),
        'ln2_b': nrm(ks[21], (L, D), 0.02),
        'w_ffn_gate': nrm(ks[22], (L, D, F), D ** -0.5),
        'w_ffn_up': nrm(ks[23], (L, D, F), D ** -0.5),
        'w_ffn_down': nrm(ks[24], (L, F, D), DEEPNORM_BETA * F ** -0.5),
    }

def first_block(x, c, ctx, c_ctx, ln_in_g, ln_in_b, w_mod, b_mod, w_in, mla_q_norm_g, mla_kv_norm_g,
              w_uq, w_qr, w_uk, w_uv, na_rpb, w_branch, w_out, ln1_g, ln1_b, ln2_g, ln2_b,
              w_ffn_gate, w_ffn_up, w_ffn_down):
    n = x.shape[1]
    n_rows = n // GRID_W
    rope = rope_tables(n)
    x_lat = layer_norm(x, ln_in_g, ln_in_b)
    x_ctx = layer_norm(ctx, ln_in_g, ln_in_b)
    silu_c = jax.nn.silu(c)
    silu_cc = jax.nn.silu(c_ctx)
    for l in range(DEPTH):
        last = l == DEPTH - 1
        lp = {'w_in': w_in[l], 'g_q': mla_q_norm_g[l], 'g_kv': mla_kv_norm_g[l], 'w_uq': w_uq[l],
              'w_qr': w_qr[l], 'w_uk': w_uk[l], 'w_uv': w_uv[l], 'rpb': na_rpb[l],
              'w_branch': w_branch[l], 'w_out': w_out[l]}
        sh1, sc1, g1, sh2, sc2, g2 = [m[:, None, :] for m in jnp.split(silu_c @ w_mod[l] + b_mod[l], 6, axis=-1)]
        csh1, csc1, cg1, csh2, csc2, cg2 = jnp.split(silu_cc @ w_mod[l] + b_mod[l], 6, axis=-1)
        a_lat = x_lat * (1 + sc1) + sh1
        a_ctx = x_ctx * (1 + csc1) + csh1
        m_lat, m_ctx = mixer(a_lat, a_ctx, lp, rope, n_rows, not last)
        x_lat = layer_norm(DEEPNORM_ALPHA * x_lat + (1 + g1) * m_lat, ln1_g[l], ln1_b[l])
        f_lat = swiglu(x_lat * (1 + sc2) + sh2, w_ffn_gate[l], w_ffn_up[l], w_ffn_down[l])
        x_lat = layer_norm(DEEPNORM_ALPHA * x_lat + (1 + g2) * f_lat, ln2_g[l], ln2_b[l])
        if not last:
            x_ctx = layer_norm(DEEPNORM_ALPHA * x_ctx + (1 + cg1) * m_ctx, ln1_g[l], ln1_b[l])
            f_ctx = swiglu(x_ctx * (1 + csc2) + csh2, w_ffn_gate[l], w_ffn_up[l], w_ffn_down[l])
            x_ctx = layer_norm(DEEPNORM_ALPHA * x_ctx + (1 + cg2) * f_ctx, ln2_g[l], ln2_b[l])
    return x_lat


N_MIXERS = 2
N_LAYERS_A = (DEPTH + N_MIXERS - 1) // N_MIXERS
N_LAYERS_B = DEPTH // N_MIXERS
LRU_WIDTH = D_MODEL
LRU_HEADS = 4
LRU_HEAD_DIM = LRU_WIDTH // LRU_HEADS
CONV_WIDTH = 4
LRU_C = 8.0
MIN_RAD = 0.9
MAX_RAD = 0.999
POOL_WINDOWS = (2, 4, 8, 16)
POOL_GROUPS = len(POOL_WINDOWS)
POOL_GROUP_DIM = D_MODEL // POOL_GROUPS
D_FF = 4 * D_MODEL
N_MOD = 6
EPS = 1e-6


def rms_norm_2(x, g):
    xf = x.astype(jnp.float32)
    y = xf * lax.rsqrt(jnp.mean(xf * xf, axis=-1, keepdims=True) + EPS)
    return (y * g.astype(jnp.float32)).astype(x.dtype)

def modulate(h, shift, scale):
    return h * (1.0 + scale[:, None, :]) + shift[:, None, :]

def causal_depthwise_conv(x, w, b):
    s = x.shape[1]
    xp = jnp.pad(x, ((0, 0), (CONV_WIDTH - 1, 0), (0, 0)))
    y = xp[:, 0:s] * w[0]
    for k in range(1, CONV_WIDTH):
        y = y + xp[:, k:k + s] * w[k]
    return y + b

def _lru_combine(left, right):
    a1, b1 = left
    a2, b2 = right
    return a1 * a2, a2 * b1 + b2

def block_diag_linear(x, w, b):
    bsz, s, _ = x.shape
    xh = x.reshape(bsz, s, LRU_HEADS, LRU_HEAD_DIM)
    y = jnp.einsum("bshi,hij->bshj", xh, w) + b
    return y.reshape(bsz, s, LRU_WIDTH)

def rg_lru(x, w_a, b_a, w_x, b_x, lam):
    gate_r = jax.nn.sigmoid(block_diag_linear(x, w_a, b_a)).astype(jnp.float32)
    gate_i = jax.nn.sigmoid(block_diag_linear(x, w_x, b_x)).astype(jnp.float32)
    log_a = LRU_C * gate_r * jax.nn.log_sigmoid(lam.astype(jnp.float32))
    a = jnp.exp(log_a)
    mult = jnp.sqrt(-jnp.expm1(2.0 * log_a))
    u = mult * (gate_i * x.astype(jnp.float32))
    _, h = lax.associative_scan(_lru_combine, (a, u), axis=1)
    return h.astype(x.dtype)

def recurrent_mixer(h, w_y, b_y, w_in, b_in, conv_w, conv_b, w_a, b_a, w_x, b_x, lam, w_out, b_out):
    gate_branch = jax.nn.gelu(jnp.einsum("bsd,dw->bsw", h, w_y) + b_y)
    xr = jnp.einsum("bsd,dw->bsw", h, w_in) + b_in
    xr = causal_depthwise_conv(xr, conv_w, conv_b)
    xr = rg_lru(xr, w_a, b_a, w_x, b_x, lam)
    return jnp.einsum("bsw,wd->bsd", xr * gate_branch, w_out) + b_out

def pool_mixer(h, w_pool, pool_scale):
    bsz, s, _ = h.shape
    hf = h.astype(jnp.float32)
    counts = jnp.arange(1, s + 1, dtype=jnp.float32)
    outs = []
    for g, win in enumerate(POOL_WINDOWS):
        xg = hf[..., g * POOL_GROUP_DIM:(g + 1) * POOL_GROUP_DIM]
        cs = jnp.cumsum(xg, axis=1)
        cs_lag = jnp.pad(cs, ((0, 0), (win, 0), (0, 0)))[:, :s]
        mean = (cs - cs_lag) / jnp.minimum(counts, float(win))[None, :, None]
        outs.append(mean - xg)
    pooled = jnp.stack(outs, axis=2).astype(h.dtype)
    mixed = jnp.einsum("bsgi,gij->bsgj", pooled, w_pool).reshape(bsz, s, D_MODEL)
    return mixed * pool_scale

def sq_relu_mlp(h, w1, w2):
    u = jax.nn.relu(jnp.einsum("bsd,df->bsf", h, w1))
    return jnp.einsum("bsf,fd->bsd", u * u, w2)

def second_inputs(seed: int = 0) -> dict:
    key = jax.random.key(seed)
    ks = jax.random.split(key, 26)
    f32 = jnp.float32
    nrm = lambda k, shape, s: (jax.random.normal(k, shape, f32) * s)
    d, w, hd, na, nb = D_MODEL, LRU_WIDTH, LRU_HEAD_DIM, N_LAYERS_A, N_LAYERS_B
    rad = jnp.sqrt(jax.random.uniform(ks[15], (na, w), f32, MIN_RAD ** 2, MAX_RAD ** 2))
    return {
        "x": nrm(ks[0], (BATCH, SEQ, d), 1.0),
        "c": nrm(ks[1], (BATCH, d), 1.0),
        "w_mod": nrm(ks[2], (DEPTH, d, N_MOD * d), 0.5 * d ** -0.5),
        "b_mod": nrm(ks[3], (DEPTH, N_MOD * d), 0.02),
        "norm_mix_g": 1.0 + nrm(ks[4], (DEPTH, d), 0.05),
        "norm_ffn_g": 1.0 + nrm(ks[5], (DEPTH, d), 0.05),
        "lru_w_y": nrm(ks[6], (na, d, w), d ** -0.5),
        "lru_b_y": nrm(ks[7], (na, w), 0.02),
        "lru_w_in": nrm(ks[8], (na, d, w), d ** -0.5),
        "lru_b_in": nrm(ks[9], (na, w), 0.02),
        "lru_conv_w": nrm(ks[10], (na, CONV_WIDTH, w), CONV_WIDTH ** -0.5),
        "lru_conv_b": nrm(ks[11], (na, w), 0.02),
        "lru_w_a": nrm(ks[12], (na, LRU_HEADS, hd, hd), hd ** -0.5),
        "lru_b_a": nrm(ks[13], (na, LRU_HEADS, hd), 0.02),
        "lru_w_x": nrm(ks[14], (na, LRU_HEADS, hd, hd), hd ** -0.5),
        "lru_b_x": nrm(ks[16], (na, LRU_HEADS, hd), 0.02),
        "lru_lambda": jnp.log(rad) - jnp.log1p(-rad),
        "lru_w_out": nrm(ks[17], (na, w, d), w ** -0.5),
        "lru_b_out": nrm(ks[18], (na, d), 0.02),
        "pool_w": nrm(ks[19], (nb, POOL_GROUPS, POOL_GROUP_DIM, POOL_GROUP_DIM), POOL_GROUP_DIM ** -0.5),
        "pool_scale": 1.0 + nrm(ks[20], (nb, d), 0.1),
        "ffn_w1": nrm(ks[21], (DEPTH, d, D_FF), d ** -0.5),
        "ffn_w2": nrm(ks[22], (DEPTH, D_FF, d), D_FF ** -0.5),
        "final_norm_g": 1.0 + nrm(ks[23], (d,), 0.05),
    }

def second_block(x, c, w_mod, b_mod, norm_mix_g, norm_ffn_g, lru_w_y, lru_b_y, lru_w_in, lru_b_in,
              lru_conv_w, lru_conv_b, lru_w_a, lru_b_a, lru_w_x, lru_b_x, lru_lambda, lru_w_out,
              lru_b_out, pool_w, pool_scale, ffn_w1, ffn_w2, final_norm_g):
    cond = jax.nn.silu(c)
    for i in range(DEPTH):
        mod = jnp.einsum("bd,de->be", cond, w_mod[i]) + b_mod[i]
        sh_m, sc_m, gt_m, sh_f, sc_f, gt_f = jnp.split(mod, N_MOD, axis=-1)
        h = modulate(rms_norm_2(x, norm_mix_g[i]), sh_m, sc_m)
        j = i // N_MIXERS
        if i % N_MIXERS == 0:
            y = recurrent_mixer(h, lru_w_y[j], lru_b_y[j], lru_w_in[j], lru_b_in[j],
                                lru_conv_w[j], lru_conv_b[j], lru_w_a[j], lru_b_a[j],
                                lru_w_x[j], lru_b_x[j], lru_lambda[j], lru_w_out[j], lru_b_out[j])
        else:
            y = pool_mixer(h, pool_w[j], pool_scale[j])
        x = x + gt_m[:, None, :] * y
        h = modulate(rms_norm_2(x, norm_ffn_g[i]), sh_f, sc_f)
        x = x + gt_f[:, None, :] * sq_relu_mlp(h, ffn_w1[i], ffn_w2[i])
    return rms_norm_2(x, final_norm_g)


def setup_inputs(seed=0):
    out = dict(first_inputs(seed))
    for name, value in second_inputs(seed + 1).items():
        if name != "x":
            out[name + "_2"] = value
    return out


def reference(
    x, c, ctx, c_ctx, ln_in_g, ln_in_b, w_mod, b_mod, w_in, mla_q_norm_g, mla_kv_norm_g, w_uq,
    w_qr, w_uk, w_uv, na_rpb, w_branch, w_out, ln1_g, ln1_b, ln2_g, ln2_b, w_ffn_gate, w_ffn_up,
    w_ffn_down, c_2, w_mod_2, b_mod_2, norm_mix_g_2, norm_ffn_g_2, lru_w_y_2, lru_b_y_2,
    lru_w_in_2, lru_b_in_2, lru_conv_w_2, lru_conv_b_2, lru_w_a_2, lru_b_a_2, lru_w_x_2,
    lru_b_x_2, lru_lambda_2, lru_w_out_2, lru_b_out_2, pool_w_2, pool_scale_2, ffn_w1_2,
    ffn_w2_2, final_norm_g_2,
):
    x = first_block(
        x, c, ctx, c_ctx, ln_in_g, ln_in_b, w_mod, b_mod, w_in, mla_q_norm_g, mla_kv_norm_g,
        w_uq, w_qr, w_uk, w_uv, na_rpb, w_branch, w_out, ln1_g, ln1_b, ln2_g, ln2_b, w_ffn_gate,
        w_ffn_up, w_ffn_down,
    )
    return second_block(
        x, c_2, w_mod_2, b_mod_2, norm_mix_g_2, norm_ffn_g_2, lru_w_y_2, lru_b_y_2, lru_w_in_2,
        lru_b_in_2, lru_conv_w_2, lru_conv_b_2, lru_w_a_2, lru_b_a_2, lru_w_x_2, lru_b_x_2,
        lru_lambda_2, lru_w_out_2, lru_b_out_2, pool_w_2, pool_scale_2, ffn_w1_2, ffn_w2_2,
        final_norm_g_2,
    )


_drawn_inputs = setup_inputs


def setup_inputs(seed=0):
    import zlib

    import numpy as np

    out = dict(_drawn_inputs(seed))
    spreads = {}
    factors = {'c_ctx': 3.597,
     'b_mod': 3.173,
     'mla_q_norm_g': 8.0,
     'mla_kv_norm_g': 8.0,
     'w_qr': 4.685,
     'na_rpb': 8.0,
     'norm_mix_g_2': 3.459,
     'lru_b_y_2': 8.0,
     'lru_b_in_2': 6.433,
     'lru_conv_b_2': 5.9,
     'lru_b_a_2': 8.0,
     'lru_b_x_2': 8.0,
     'lru_b_out_2': 22.759,
     'norm_ffn_g_2': 3.703,
     'pool_scale_2': 4.201}
    for name, (base, spread) in spreads.items():
        noise = np.random.default_rng([zlib.crc32(name.encode()), seed]).standard_normal(out[name].shape)
        drawn = base * np.exp(spread * noise) if base else spread * noise
        out[name] = jnp.asarray(drawn.astype(out[name].dtype))
    for name, factor in factors.items():
        out[name] = (out[name] * factor).astype(out[name].dtype)
    return out
```

```python
from contextlib import ExitStack

import numpy as np

import concourse.bass as bass
from concourse import mybir

F32 = mybir.dt.float32
F32R = mybir.dt.float32r
ALU = mybir.AluOpType
ACT = mybir.ActivationFunctionType
AX = mybir.AxisListType

P = 128
D = 1024
KT = D // P
SEQ = 256
CTX = 256
TOK = SEQ + CTX
GRID_W = 64
HEADS = 8
KW = 16
NA_SCALE = 64 ** -0.5
MLA_SCALE = 96 ** -0.5
LN_EPS = 1e-5
RMS_EPS = 1e-6
ALPHA = 4 ** 0.25
FFN = 2816
FFN2 = 4096
RPB_RUN = 5 * 31 + GRID_W

C_ID, C_COS, C_SIN, C_WIN, C_ROT, C_SEL = 0, 128, 384, 640, 704, 736
C_KEEP = 740
C_DFT = C_KEEP
C_POOL = C_DFT + 256 + 512 + 512
C_ALL = C_POOL + 4 * SEQ

VECTORS = [
    ("ln_in_g", 8), ("ln_in_b", 8), ("c", 8), ("c_ctx", 8), ("b_mod", 96), ("c_2", 8), ("b_mod_2", 96),
    ("ln1_g", 16), ("ln1_b", 16), ("ln2_g", 16), ("ln2_b", 16), ("mla_q_norm_g", 4),
    ("mla_kv_norm_g", 2), ("norm_mix_g_2", 16), ("norm_ffn_g_2", 16), ("lru_b_y_2", 8), ("lru_b_in_2", 8),
    ("lru_conv_w_2", 32), ("lru_conv_b_2", 8), ("lru_b_a_2", 8), ("lru_b_x_2", 8), ("lru_lambda_2", 8),
    ("lru_b_out_2", 8), ("pool_scale_2", 8), ("final_norm_g_2", 8),
]

INPUTS = ['x', 'c', 'ctx', 'c_ctx', 'ln_in_g', 'ln_in_b', 'w_mod', 'b_mod', 'w_in', 'mla_q_norm_g', 'mla_kv_norm_g',
          'w_uq', 'w_qr', 'w_uk', 'w_uv', 'na_rpb', 'w_branch', 'w_out', 'ln1_g', 'ln1_b', 'ln2_g', 'ln2_b',
          'w_ffn_gate', 'w_ffn_up', 'w_ffn_down', 'c_2', 'w_mod_2', 'b_mod_2', 'norm_mix_g_2', 'norm_ffn_g_2',
          'lru_w_y_2', 'lru_b_y_2', 'lru_w_in_2', 'lru_b_in_2', 'lru_conv_w_2', 'lru_conv_b_2', 'lru_w_a_2',
          'lru_b_a_2', 'lru_w_x_2', 'lru_b_x_2', 'lru_lambda_2', 'lru_w_out_2', 'lru_b_out_2', 'pool_w_2',
          'pool_scale_2', 'ffn_w1_2', 'ffn_w2_2', 'final_norm_g_2']


def constants():
    t = np.zeros((P, C_ALL), np.float64)
    t[:, C_ID:C_ID + P] = np.eye(P)
    pos = np.arange(SEQ)
    inv = 10000.0 ** (-np.arange(8, dtype=np.float64) / 8)
    ang = np.concatenate([(pos // GRID_W)[:, None] * inv, (pos % GRID_W)[:, None] * inv], 1)
    for half in range(2):
        t[64 + 16 * half:80 + 16 * half, C_COS:C_COS + SEQ] = np.cos(ang).T
        t[64 + 16 * half:80 + 16 * half, C_SIN:C_SIN + SEQ] = np.sin(ang).T
    for j in range(16):
        t[64 + 16 + j, C_ROT + j] = -1.0
        t[64 + j, C_ROT + 16 + j] = 1.0
    col = np.arange(P) % GRID_W
    start = np.clip(col - KW // 2, 0, GRID_W - KW)
    key = np.arange(GRID_W)
    inside = (key >= start[:, None]) & (key < start[:, None] + KW)
    t[:, C_WIN:C_WIN + GRID_W] = np.where(inside, 3.0e38, -1.0e30)
    for g in range(4):
        for v in range(3):
            t[32 * g + v, C_SEL + v] = 1.0
    d = np.arange(P)
    fd = 2 * np.pi * np.outer(d, d) / P
    t[:, C_DFT:C_DFT + P] = np.cos(fd)
    t[:, C_DFT + P:C_DFT + 2 * P] = np.sin(fd)
    n = np.arange(SEQ)
    fn = 2 * np.pi * (np.outer(n, n) % SEQ) / SEQ
    norm = (SEQ * P) ** -0.5
    for half in range(2):
        rows = slice(half * P, half * P + P)
        at = C_DFT + 256 + half * SEQ
        t[:, at:at + SEQ] = np.cos(fn)[rows] * norm
        t[:, at + 512:at + 512 + SEQ] = -np.sin(fn)[rows] * norm
    for g, win in enumerate((2, 4, 8, 16)):
        t[:, C_POOL + g * SEQ:C_POOL + (g + 1) * SEQ] = 1.0 / np.minimum(n + 1, win)
    return t.astype(np.float32)


class Quiet:

    def done(self, *a, **k):
        return self

    activation = tensor_tensor = tensor_scalar = scalar_tensor_tensor = tensor_copy = tensor_reduce = done
    reciprocal = memset = matmul = transpose = dma_start = wait_ge = then_inc = mul = copy = done
    tensor_tensor_scan = done


class Counts:

    def __init__(self, eng, sems, own, dry=False):
        self.eng, self.sems, self.names, self.dry = eng, sems, own, dry
        self.start = {n: 0 for n in sems}
        self.count = {n: 0 for n in own}
        self.turn, self.stride = None, {}
        self.bank = {}

    def s(self, name):
        return self.start[name]

    def value(self, name, value):
        if self.turn is not None and self.stride.get(name):
            assert value > 0, (name, value)
            return self.turn * self.stride[name] + value
        assert value > 0 or self.dry, (name, value)
        return value

    def at(self, name, further=0):
        return self.value(name, self.start[name] + further)

    def own(self, name):
        return self.value(name, self.count[name])

    def up(self, name, by=1):
        assert name in self.names, name
        self.count[name] += by
        return self.sems[name]


OWN = {
    "sp": ["pair0_loaded", "pair1_loaded", "side_loaded", "out_done"],
    "act": ["weight_high", "act_read", "side_row_copied", "act_done", "x_normed", "modulated", "root_done", "exp_done", "turned_copied", "branch_high", "features_copied", "queries_copied", "constants_loaded",
            "tokens_loaded", "rpb_loaded", "latent_w_loaded", "silu_done", "decay_done"],
    "dve": ["weight_low", "dve_read", "side_added", "dve_done", "centred", "input_low", "one_minus_a2", "max_done", "probs_ready", "branch_low", "keys_copied", "hidden_low", "var_done", "rotated_done", 
            "lambda_done", "bias_done", "latent_normed", "copied_out"],
    "pe": ["products", "side_rows", "side_turned", "sums_done", "scores_done", "probs_turned", "values_done", "features_done", "tokens_done", "squares_summed", "qkv_done", "rotary_done", "x_turned", "vectors_turned"],
    "pool": ["pool_done"],
}


def build(nc, A, out, const):
    stack = ExitStack()
    offset = [16512]

    def sb(name, shape, dt=F32, at=None):
        size = 4
        for s in shape[1:]:
            size *= s
        if at is None:
            at = offset[0]
            offset[0] += (size + 31) // 32 * 32
        assert at + size <= 229344, (name, at + size)
        return nc.alloc_sbuf_tensor_at(name, list(shape), dt, offset=at)

    X = sb("X", [P, KT, TOK])
    AH = sb("AH", [P, KT, TOK], F32R)
    AL = sb("AL", [P, KT, TOK], F32R)
    SH = sb("SH", [P, 4, KT, P], F32R)
    SL = sb("SL", [P, 4, KT, P], F32R)
    RAW = [sb(f"RAW{p}", [P, KT, 2 * P]) for p in range(2)]
    SIDE = sb("SIDE", [P, KT, 512])
    YH = sb("YH", [P, 4, TOK], F32R)
    YL = sb("YL", [P, 4, TOK], F32R)
    MACC = sb("MACC", [P, KT, TOK])
    VEC = sb("VEC", [P, 4, P])
    MODT = sb("MODT", [P, 4, 48, 3])
    CC = sb("CC", [P, KT, 32])
    CON = sb("CON", [P, C_KEEP])
    ONES = sb("ONES", [P, P])
    MODROW = sb("MODROW", [P, 512])
    DER = sb("DER", [P, 12, KT])
    SM = sb("SM", [P, 16])
    REG = offset[0]

    def reg(name, at, shape, dt=F32):
        return sb(name, shape, dt, at=REG + 4 * at)

    FT = reg("FT", 0, [P, 4, TOK])
    U = reg("U", 2048, [P, 2, 4, 256])
    DFT = reg("DFT", 4096, [P, 1280])
    NQ = reg("NQ", 0, [P, 4, TOK])
    NK = reg("NK", 2048, [P, 4, TOK])
    NV = reg("NV", 4096, [P, 4, 512])
    BIAS = reg("BIAS", 6144, [P, HEADS, 6, GRID_W])
    RPB = reg("RPB", 10240, [P, HEADS, RPB_RUN])
    Q96 = reg("Q96", 0, [P, HEADS, TOK])
    K96 = reg("K96", 4096, [P, HEADS, TOK])
    MV = reg("MV", 8192, [P, 4, 512])
    SQ3 = reg("SQ3", 8192, [P, 3, TOK])
    RT = reg("RT", 9728, [P, 2, TOK])
    CQ = reg("CQ", 11264, [P, 2, TOK])
    CKV = reg("CKV", 12288, [P, TOK])
    KR = reg("KR", 12800, [P, TOK])
    ROPET = reg("ROPET", 10240, [P, 2, 256])
    PR = reg("PR", 10240, [P, 2, TOK])
    PTS = reg("PTS", 11264, [P, 2, 4, 256])
    GATE = reg("GATE", 11264, [P, 4, TOK])
    HH = reg("HH", 0, [P, KT, TOK], F32R)
    HL = reg("HL", 4096, [P, KT, TOK], F32R)
    SG = reg("SG", 8192, [P, 2, TOK])
    HT = reg("HT", 9216, [P, 2, TOK])
    S1 = reg("S1", 10240, [P, TOK])
    S2 = reg("S2", 10752, [P, TOK])
    SQ = reg("SQ", 11264, [P, TOK])
    MU = reg("MU", 11776, [P, TOK])
    RSTD = reg("RSTD", 12288, [P, TOK])
    VAR = reg("VAR", 12800, [P, TOK])
    NT = reg("NT", 0, [P, 2, TOK])
    A32 = reg("A32", 1024, [P, 2, TOK])
    XIN = nc.alloc_sbuf_tensor_at("XIN", [P, 4, D], F32, offset=16512 + 16384 * 5 + 16384 * 3)
    VROWS = reg("VROWS", 8192, [P, 4, P])
    GB = reg("GB", 0, [P, KT, SEQ])
    XR = reg("XR", 2048, [P, KT, 260])
    XC = reg("XC", 4128, [P, KT, SEQ])
    LA = reg("LA", 6176, [P, KT, SEQ])
    LT = reg("LT", 8224, [P, KT, SEQ])
    GI = reg("GI", 10272, [P, KT, SEQ])
    PA = reg("PA", 2048, [P, KT, SEQ])
    PS1 = reg("PS1", 4096, [P, KT, SEQ + 16])
    PS2 = reg("PS2", 6272, [P, KT, SEQ + 16])
    PINV = reg("PINV", 8448, [P, 4, SEQ])
    OUTT = reg("OUTT", 2048, [P, KT, SEQ])
    OUTS = reg("OUTS", 4096, [P, 2, D])
    assert offset[0] + 53248 <= 229344, offset[0]

    PS = [stack.enter_context(nc.psum_tensor(f"ps{b}", [P, 512], F32)) for b in range(8)]
    sem = {n: stack.enter_context(nc.semaphore(n)) for names in OWN.values() for n in names}

    Y8H, Y8L = (y[:, :, :].rearrange("p a b -> p (a b)").rearrange("p (k n) -> p k n", k=KT) for y in (YH, YL))
    IDENT = CON[:, C_ID:C_ID + P]
    COS = CON[64:96, C_COS:C_COS + SEQ]
    SIN = CON[64:96, C_SIN:C_SIN + SEQ]
    W96 = SIDE[:, 0:3, :].rearrange("p a b -> p (a b)").rearrange("p (k h c) -> p k h c", k=2, h=HEADS)
    WUK = SIDE[:, 3, :]
    WUV = SIDE[:, 4, :]

    place, tile_, row_ = {}, 0, 0
    for name, n in VECTORS:
        if row_ + n > P:
            tile_, row_ = tile_ + 1, 0
        place[name] = (tile_, row_)
        row_ += n

    def vec(name, i, n=1):
        t, r = place[name]
        return VEC[:, t, r + i:r + i + n]

    def mod(mat, chunk, v, k=None):
        if k is None:
            return MODT[:, mat, 8 * chunk:8 * chunk + 8, v]
        return MODT[:, mat, 8 * chunk + k, v:v + 1]

    wmod = [A["w_mod"][0], A["w_mod"][1], A["w_mod_2"][0], A["w_mod_2"][1]]
    bmod = [("b_mod", 0), ("b_mod", 48), ("b_mod_2", 0), ("b_mod_2", 48)]

    def rows(w):
        return w.rearrange("(k p) n -> p k n", p=P)

    class Side:

        def __init__(self, mat, chunk, per_turn=0):
            self.mat, self.chunk, self.per_turn = mat, chunk, per_turn

        def at(self, K):
            return self.chunk if not self.per_turn or K.turn is None else K.turn * self.per_turn + self.chunk

        def sp(self, e, K, j):
            if K.s("side_rows") + j:
                e.wait_ge(sem["side_rows"], K.at("side_rows", j))
            if K.s("qkv_done"):
                e.wait_ge(sem["qkv_done"], K.at("qkv_done"))
            src = rows(wmod[self.mat])
            c = self.at(K)
            s = src[:, :, c * 512:(c + 1) * 512] if K.turn is None or not self.per_turn else src[:, :, bass.ds(c * 512, 512)]
            e.dma_start(SIDE[:, :, :], s).then_inc(K.up("side_loaded", 16), 16)

        def pe_rows(self, e, K, j):
            e.wait_ge(sem["side_loaded"], K.at("side_loaded", 16 * (j + 1)))
            if K.s("side_added") + j:
                e.wait_ge(sem["side_added"], K.at("side_added", j))
            for b in (4, 5):
                reader, count = K.bank[b]
                e.wait_ge(sem[reader], K.value(reader, count))
            for k in range(KT):
                g = k % 4
                ins = e.matmul(PS[4][32 * g:32 * g + 32, :], CC[:, k, :], SIDE[:, k, :], start=k < 4, stop=k >= 4)
            ins.then_inc(K.up("side_rows"), 1)

        def act(self, e, K, j):
            e.wait_ge(sem["side_rows"], K.at("side_rows", j + 1))
            e.activation(MODROW[:, :], PS[4][:, :], ACT.Copy).then_inc(K.up("side_row_copied"), 1)

        def pe_turn(self, e, K, j):
            e.wait_ge(sem["side_row_copied"], K.at("side_row_copied", j + 1))
            for q in range(4):
                ins = e.matmul(PS[5][:, 3 * q:3 * q + 3], MODROW[:, q * P:(q + 1) * P], CON[:, C_SEL:C_SEL + 3],
                               start=True, stop=True)
            ins.then_inc(K.up("side_turned"), 1)
            for b in (4, 5):
                K.bank[b] = ("side_added", K.s("side_added") + j + 1)

        def dve(self, e, K, j):
            e.wait_ge(sem["side_turned"], K.at("side_turned", j + 1))
            c = self.at(K)
            name, first = bmod[self.mat]
            t, r = place[name]
            dyn = K.turn is not None and self.per_turn
            dst = MODT[:, self.mat, bass.ds(4 * c, 4), :] if dyn else MODT[:, self.mat, 4 * c:4 * c + 4, :]
            bias = VEC[:, t, bass.ds(4 * c + (r + first), 4)] if dyn else VEC[:, t, r + first + 4 * c:r + first + 4 * c + 4]
            ps = PS[5][:, 0:12].rearrange("p (q v) -> p q v", v=3)
            e.tensor_tensor(dst, ps, bias.unsqueeze(2).to_broadcast([P, 4, 3]), ALU.add) \
                .then_inc(K.up("side_added"), 1)

    class SideOnly:
        def __init__(self, *side):
            self.sides = side

        def sp(self, e, K):
            for j, s in enumerate(self.sides):
                s.sp(e, K, j)

        def pe(self, e, K):
            for j, s in enumerate(self.sides):
                s.pe_rows(e, K, j)
                s.pe_turn(e, K, j)

        def act(self, e, K):
            for j, s in enumerate(self.sides):
                s.act(e, K, j)

        def dve(self, e, K):
            for j, s in enumerate(self.sides):
                s.dve(e, K, j)

        def pool(self, e, K):
            pass

    class Unit:

        kt = KT
        func = ACT.Copy
        offs = (0, P, 0, P)
        read = "aaaa"
        rhs = (AH, AL)
        tokens = (0, TOK)
        nxt = None
        ready = None
        hold = False

        def __init__(self, w=None, cols=None, tokens=None, offs=None, rhs=None, rhs_count=KT, side=None, ready=None,
                     dst=None, func=None, scale=1.0, layer=0, col=0, h0=0, krow=0, kt=None, per_turn=0, tile0=0, b=0,
                     half=0, u=0, first=True, stats=None, mean=True, bias=None, prep=None):
            self.w, self.cols, self.rhs_count, self.side, self.dst, self.scale = w, cols, rhs_count, side, dst, scale
            self.layer, self.col, self.h0, self.krow, self.per_turn, self.tile0 = layer, col, h0, krow, per_turn, tile0
            self.b, self.half, self.u, self.first, self.mean, self.bias, self.prep = b, half, u, first, mean, bias, prep
            self.tokens = tokens or self.tokens
            self.offs = offs or self.offs
            self.rhs = rhs or self.rhs
            self.ready = ready or self.ready
            self.func = func or self.func
            self.kt = kt or self.kt
            if stats is not None:
                self.stats = stats

        def wide(self, m):
            return self.tokens

        def sp(self, e, K):
            for p in range(2):
                if K.s("products"):
                    e.wait_ge(sem["weight_low"], K.at("weight_low", 2 * p - 6))
                e.dma_start(RAW[p][:, 0:self.kt, :], self.src(K, p)).then_inc(K.up(f"pair{p}_loaded", 16), 16)
            if self.side:
                self.side.sp(e, K, 0)

        def split_act(self, e, K, m, ahead):
            p = m // 2
            e.wait_ge(sem[f"pair{p}_loaded"], K.at(f"pair{p}_loaded", (32 if ahead else 16)))
            kt, o = self.kt, self.offs[m]
            e.activation(SH[:, m, 0:kt, :], RAW[p][:, 0:kt, o:o + P], ACT.Copy).then_inc(K.up("weight_high"), 1)

        def split_dve(self, e, K, m, ahead):
            p = m // 2
            e.wait_ge(sem["weight_high"], K.at("weight_high", m + 1))
            kt, o = self.kt, self.offs[m]
            e.tensor_tensor(SL[:, m, 0:kt, :], RAW[p][:, 0:kt, o:o + P], SH[:, m, 0:kt, :].bitcast(F32),
                            ALU.subtract).then_inc(K.up("weight_low"), 1)

        def pe(self, e, K):
            for m in range(4):
                if m == 1 and self.side:
                    self.side.pe_rows(e, K, 0)
                if m == 2 and self.side:
                    self.side.pe_turn(e, K, 0)
                e.wait_ge(sem["weight_low"], K.at("weight_low", m - 3))
                reader, count = K.bank[m]
                e.wait_ge(sem[reader], K.value(reader, count))
                c0, c1 = self.wide(m)
                ps = PS[m][:, 0:c1 - c0]
                for k in range(self.kt):
                    xh, xl = self.moving(m, k, c0, c1)
                    if m == 0 and self.ready:
                        producer, per_k = self.ready
                        e.wait_ge(sem[producer], K.at(producer, k + 1 - self.rhs_count if per_k else 0))
                    e.matmul(ps, SH[:, m, k, :], xh, start=k == 0, stop=False)
                    e.matmul(ps, SH[:, m, k, :], xl, start=False, stop=False)
                    ins = e.matmul(ps, SL[:, m, k, :], xh, start=False, stop=k == self.kt - 1)
                ins.then_inc(K.up("products"), 1)
            fa, fd = K.s("act_read"), K.s("dve_read")
            for m in range(4):
                if self.read[m] == "a":
                    fa += 1
                    K.bank[m] = ("act_read", fa)
                else:
                    fd += 1
                    K.bank[m] = ("dve_read", fd)

        def moving(self, m, k, c0, c1):
            return self.rhs[0][:, k, c0:c1], self.rhs[1][:, k, c0:c1]

        def freed(self, m):
            return 4 if self.hold else m + 1

        def act(self, e, K):
            for m in range(4):
                e.wait_ge(sem["products"], K.at("products", self.freed(m)))
                if self.nxt:
                    self.nxt.split_act(e, K, m, True)
                self.read_act(e, K, m)
                if m == 1 and self.side:
                    self.side.act(e, K, 0)

        def dve(self, e, K):
            for m in range(4):
                if self.nxt:
                    self.nxt.split_dve(e, K, m, True)
                e.wait_ge(sem["products"], K.at("products", m + 1))
                self.read_dve(e, K, m)
                if m == 2 and self.side:
                    self.side.dve(e, K, 0)

        def pool(self, e, K):
            pass

        def read_act(self, e, K, m):
            pass

        def read_dve(self, e, K, m):
            pass

    class First(SideOnly):

        def __init__(self, unit):
            self.unit = unit

        def sp(self, e, K):
            pass

        pe = pool = sp

        def act(self, e, K):
            for m in range(4):
                self.unit.split_act(e, K, m, False)

        def dve(self, e, K):
            for m in range(4):
                self.unit.split_dve(e, K, m, False)

    class Columns(Unit):

        def src(self, K, p):
            c = self.cols[p]
            if self.per_turn and K.turn is not None:
                return rows(self.w)[:, self.krow:self.krow + self.kt, bass.ds(K.turn * self.per_turn + c, 256)]
            return rows(self.w)[:, self.krow:self.krow + self.kt, c:c + 256]

    class Copied(Columns):

        read = "aaaa"

        def read_act(self, e, K, m):
            c0, c1 = self.wide(m)
            e.activation(self.dst(m), PS[m][:, 0:c1 - c0], self.func, scale=self.scale).then_inc(K.up("act_read"), 1)

    class Compressed(Copied):

        def wide(self, m):
            return self.tokens if m < 2 else (0, TOK)

    class Gelu(Copied):
        def read_act(self, e, K, m):
            i = self.tile0 + m
            e.activation(GB[:, i, :], PS[m][:, 0:SEQ], ACT.Gelu_apprx_tanh, bias=vec("lru_b_y_2", i)) \
                .then_inc(K.up("act_read"), 1)

    class Values(Columns):

        read = "aaaa"
        hold = True

        def pe(self, e, K):
            for m in range(4):
                e.wait_ge(sem["weight_low"], K.at("weight_low", m - 3))
            for t in range(4):
                reader, count = K.bank[t]
                e.wait_ge(sem[reader], K.value(reader, count))
                for k in range(KT):
                    xh, xl = (a[:, k, t * P:(t + 1) * P] for a in (AH, AL))
                    e.matmul(PS[t][:, :], xh, SH[:, :, k, :], start=k == 0, stop=False)
                    e.matmul(PS[t][:, :], xh, SL[:, :, k, :], start=False, stop=False)
                    ins = e.matmul(PS[t][:, :], xl, SH[:, :, k, :], start=False, stop=k == KT - 1)
                ins.then_inc(K.up("products"), 1)
                K.bank[t] = ("act_read", K.s("act_read") + t + 1)
            if self.side:
                self.side.pe_rows(e, K, 0)
                self.side.pe_turn(e, K, 0)

        def read_act(self, e, K, m):
            e.activation(NV[:, m, :], PS[m][:, :], ACT.Copy).then_inc(K.up("act_read"), 1)

    class Branch(Columns):

        kt = 4
        read = "dddd"
        rhs = (YH, YL)

        def read_dve(self, e, K, m):
            c0, c1 = self.tokens
            i = self.half * 4 + m
            acc, gate, ps = MACC[:, i, c0:c1], GATE[:, m, c0:c1], PS[m][:, 0:c1 - c0]
            e.wait_ge(sem["act_read"], K.at("act_read", -4 + m + 1))
            if self.b == 0:
                e.tensor_tensor(acc, ps, gate, ALU.mult).then_inc(K.up("dve_read"), 1)
                return
            tmp = HT[:, m % 2, c0:c1]
            e.tensor_tensor(tmp, ps, gate, ALU.mult).then_inc(K.up("dve_read"), 1)
            e.wait_ge(sem["dve_read"], K.own("dve_read"))
            e.tensor_tensor(acc, acc, tmp, ALU.add).then_inc(K.up("dve_done"), 1)
            e.wait_ge(sem["dve_done"], K.own("dve_done"))
            if self.b == 2:
                e.tensor_copy(HH[:, i, c0:c1], acc).then_inc(K.up("dve_done"), 1)
                e.wait_ge(sem["dve_done"], K.own("dve_done"))
                e.tensor_tensor(HL[:, i, c0:c1], acc, HH[:, i, c0:c1].bitcast(F32), ALU.subtract) \
                    .then_inc(K.up("hidden_low"), 1)

    def stats_pool(e, K, first, tiles, c0, c1, mean, ready):
        for n, k in enumerate(tiles):
            e.wait_ge(sem[ready], K.at(ready, n + 1))
            z = X[:, k, c0:c1]
            if first and n == 0:
                if mean:
                    e.tensor_copy(S1[:, c0:c1], z).then_inc(K.up("pool_done"), 1)
                e.tensor_tensor(S2[:, c0:c1], z, z, ALU.mult).then_inc(K.up("pool_done"), 1)
                e.wait_ge(sem["pool_done"], K.own("pool_done"))
            else:
                if mean:
                    e.tensor_tensor(S1[:, c0:c1], S1[:, c0:c1], z, ALU.add).then_inc(K.up("pool_done"), 1)
                e.tensor_tensor(SQ[:, c0:c1], z, z, ALU.mult).then_inc(K.up("pool_done"), 1)
                e.wait_ge(sem["pool_done"], K.own("pool_done"))
                e.tensor_tensor(S2[:, c0:c1], S2[:, c0:c1], SQ[:, c0:c1], ALU.add).then_inc(K.up("pool_done"), 1)
                e.wait_ge(sem["pool_done"], K.own("pool_done"))

    class Residual(Columns):

        read = "dddd"
        stats = True

        def read_dve(self, e, K, m):
            i = self.tile0 + m
            c0, c1 = self.tokens
            if self.bias:
                tmp = HT[:, m % 2, 0:SEQ]
                e.tensor_scalar(tmp, PS[m][:, 0:SEQ], vec(self.bias, i), self.scale(0, i), ALU.add, ALU.mult) \
                    .then_inc(K.up("dve_done"), 1)
                e.wait_ge(sem["dve_done"], K.own("dve_done"))
                e.tensor_tensor(X[:, i, 0:SEQ], X[:, i, 0:SEQ], tmp, ALU.add).then_inc(K.up("dve_read"), 1)
                return
            for s, c in enumerate(range(c0, c1, SEQ)):
                ins = e.scalar_tensor_tensor(out=X[:, i, c:c + SEQ], in0=PS[m][:, c:c + SEQ], scalar=self.scale(s, i),
                                             in1=X[:, i, c:c + SEQ], op0=ALU.mult, op1=ALU.add)
                ins.then_inc(K.up("dve_read" if c + SEQ == c1 else "dve_done"), 1)

        def dve(self, e, K):
            if self.prep:
                self.prep(e, K)
            super().dve(e, K)

        def pool(self, e, K):
            if self.stats:
                c0, c1 = self.tokens
                stats_pool(e, K, self.first, range(self.tile0, self.tile0 + 4), c0, c1, self.mean,
                           "dve_read")

    class UpGated(Columns):

        read = "aadd"

        def src(self, K, p):
            w = rows(A["w_ffn_gate" if p == 0 else "w_ffn_up"][self.layer])
            if self.per_turn and K.turn is not None:
                return w[:, :, bass.ds(K.turn * self.per_turn + self.col, 256)]
            return w[:, :, self.col:self.col + 256]

        def read_act(self, e, K, m):
            if m < 2:
                c0, c1 = self.tokens
                e.wait_ge(sem["dve_read"], K.at("dve_read", m - 1))
                e.activation(SG[:, m, c0:c1], PS[m][:, 0:c1 - c0], ACT.Silu).then_inc(K.up("act_read"), 1)

        def read_dve(self, e, K, m):
            if m < 2:
                return
            c0, c1 = self.tokens
            j = m - 2
            h = self.h0 + j
            e.wait_ge(sem["act_read"], K.at("act_read", j + 1))
            e.tensor_tensor(HT[:, j, c0:c1], PS[m][:, 0:c1 - c0], SG[:, j, c0:c1], ALU.mult).then_inc(K.up("dve_read"), 1)
            e.wait_ge(sem["dve_read"], K.own("dve_read"))
            e.tensor_copy(HH[:, h, c0:c1], HT[:, j, c0:c1]).then_inc(K.up("dve_done"), 1)
            e.wait_ge(sem["dve_done"], K.own("dve_done"))
            e.tensor_tensor(HL[:, h, c0:c1], HT[:, j, c0:c1], HH[:, h, c0:c1].bitcast(F32), ALU.subtract) \
                .then_inc(K.up("hidden_low"), 1)
            e.wait_ge(sem["hidden_low"], K.own("hidden_low"))

    class UpSquared(Columns):

        read = "dddd"
        tokens = (0, SEQ)

        def read_act(self, e, K, m):
            e.activation(SG4[:, m, :], PS[m][:, 0:SEQ], ACT.Relu).then_inc(K.up("act_read"), 1)

        def read_dve(self, e, K, m):
            h = self.h0 + m
            e.wait_ge(sem["act_read"], K.at("act_read", m + 1))
            ht = HT4[:, m, :]
            e.scalar_tensor_tensor(out=ht, in0=PS[m][:, 0:SEQ], scalar=0.0, in1=SG4[:, m, :], op0=ALU.max,
                                   op1=ALU.mult).then_inc(K.up("dve_read"), 1)
            e.wait_ge(sem["dve_read"], K.own("dve_read"))
            e.tensor_copy(HH[:, h, 0:SEQ], ht).then_inc(K.up("dve_done"), 1)
            e.wait_ge(sem["dve_done"], K.own("dve_done"))
            e.tensor_tensor(HL[:, h, 0:SEQ], ht, HH[:, h, 0:SEQ].bitcast(F32), ALU.subtract).then_inc(K.up("hidden_low"), 1)

    SG4 = SG[:, :, :].rearrange("p a b -> p (a b)").rearrange("p (m n) -> p m n", n=SEQ)
    HT4 = HT[:, :, :].rearrange("p a b -> p (a b)").rearrange("p (m n) -> p m n", n=SEQ)

    class Down(Residual):

        rhs = (HH, HL)
        stats = False
        ready = ("hidden_low", False)

        def src(self, K, p):
            w, c = rows(self.w), self.cols[p]
            if self.per_turn and K.turn is not None:
                return w[:, bass.ds(K.turn * self.per_turn + self.krow, self.kt), c:c + 256]
            return w[:, self.krow:self.krow + self.kt, c:c + 256]

    class Norm:

        def __init__(self, tokens=(0, TOK), mean=True, write_x=True, to="a", eps=LN_EPS, stats=False, prep=None,
                     g=None, b=None, sc=None, sh=None):
            self.tokens, self.mean, self.write_x, self.to, self.eps = tokens, mean, write_x, to, eps
            self.stats = stats
            self.prep, self.g, self.b, self.sc, self.sh = prep, g, b, sc, sh

        def sp(self, e, K):
            pass

        def pe(self, e, K):
            c0, c1 = self.tokens
            e.wait_ge(sem["pool_done"], K.at("pool_done"))
            for b in (4, 5):
                reader, count = K.bank[b]
                e.wait_ge(sem[reader], K.value(reader, count))
            if self.mean:
                e.matmul(PS[4][:, 0:c1 - c0], ONES[:, :], S1[:, c0:c1], start=True, stop=True)
            e.matmul(PS[5][:, 0:c1 - c0], ONES[:, :], S2[:, c0:c1], start=True, stop=True).then_inc(K.up("sums_done"), 1)
            for b in (4, 5):
                K.bank[b] = ("var_done", K.s("var_done") + 1)

        def dve(self, e, K):
            c0, c1 = self.tokens
            n = c1 - c0
            if self.prep:
                self.prep(e, K)
            e.wait_ge(sem["sums_done"], K.at("sums_done", 1))
            var = VAR[:, c0:c1]
            if self.mean:
                e.tensor_scalar(MU[:, c0:c1], PS[4][:, 0:n], 1.0 / D, None, ALU.mult).then_inc(K.up("dve_done"), 1)
                e.wait_ge(sem["dve_done"], K.own("dve_done"))
                e.tensor_tensor(var, MU[:, c0:c1], MU[:, c0:c1], ALU.mult).then_inc(K.up("dve_done"), 1)
                e.wait_ge(sem["dve_done"], K.own("dve_done"))
                e.scalar_tensor_tensor(out=var, in0=PS[5][:, 0:n], scalar=1.0 / D, in1=var, op0=ALU.mult,
                                       op1=ALU.subtract).then_inc(K.up("dve_done"), 1)
                e.wait_ge(sem["dve_done"], K.own("dve_done"))
                e.tensor_scalar(var, var, 0.0, self.eps, ALU.max, ALU.add).then_inc(K.up("var_done"), 1)
            else:
                e.tensor_scalar(var, PS[5][:, 0:n], 1.0 / D, self.eps, ALU.mult, ALU.add).then_inc(K.up("var_done"), 1)
            e.wait_ge(sem["root_done"], K.at("root_done", 1))
            e.reciprocal(RSTD[:, c0:c1], var).then_inc(K.up("dve_done"), 1)
            e.wait_ge(sem["dve_done"], K.own("dve_done"))

            def centre(k):
                t = NT[:, k % 2, c0:c1]
                if k >= 2:
                    r = "x_normed" if self.write_x or self.to != "a" else "modulated"
                    e.wait_ge(sem[r], K.at(r, k - 1))
                if self.mean:
                    e.tensor_tensor(t, X[:, k, c0:c1], MU[:, c0:c1], ALU.subtract).then_inc(K.up("dve_done"), 1)
                    e.wait_ge(sem["dve_done"], K.own("dve_done"))
                    e.tensor_tensor(t, t, RSTD[:, c0:c1], ALU.mult).then_inc(K.up("centred"), 1)
                else:
                    e.tensor_tensor(t, X[:, k, c0:c1], RSTD[:, c0:c1], ALU.mult).then_inc(K.up("centred"), 1)

            centre(0)
            for k in range(KT):
                if k + 1 < KT:
                    centre(k + 1)
                if self.to == "a":
                    e.wait_ge(sem["modulated"], K.at("modulated", k + 1))
                    a = A32[:, k % 2, c0:c1]
                    e.tensor_copy(AH[:, k, c0:c1], a).then_inc(K.up("dve_done"), 1)
                    e.wait_ge(sem["dve_done"], K.own("dve_done"))
                    e.tensor_tensor(AL[:, k, c0:c1], a, AH[:, k, c0:c1].bitcast(F32), ALU.subtract) \
                        .then_inc(K.up("input_low"), 1)

        def act(self, e, K):
            c0, c1 = self.tokens
            e.wait_ge(sem["var_done"], K.at("var_done", 1))
            e.activation(VAR[:, c0:c1], VAR[:, c0:c1], ACT.Sqrt).then_inc(K.up("root_done"), 1)
            for k in range(KT):
                e.wait_ge(sem["centred"], K.at("centred", k + 1))
                t = NT[:, k % 2, c0:c1]
                if self.write_x:
                    e.activation(X[:, k, c0:c1], t, ACT.Identity, bias=self.b(k), scale=self.g(k)) \
                        .then_inc(K.up("x_normed"), 1)
                if self.to == "a":
                    if k >= 2:
                        e.wait_ge(sem["input_low"], K.at("input_low", k - 1))
                    src = t
                    if self.write_x:
                        e.wait_ge(sem["x_normed"], K.own("x_normed"))
                        src = X[:, k, c0:c1]
                    for s, c in enumerate(range(c0, c1, SEQ)):
                        last = c + SEQ == c1
                        at = c - c0
                        e.activation(A32[:, k % 2, c:c + SEQ], src[:, at:at + SEQ], ACT.Identity,
                                     bias=self.sh(s, k), scale=self.sc(s, k)) \
                            .then_inc(K.up("modulated" if last else "act_done"), 1)
                if self.to == "pool":
                    e.activation(PA[:, k, :], t, ACT.Identity, bias=self.sh(0, k), scale=self.sc(0, k)) \
                        .then_inc(K.up("x_normed"), 1)
                if self.to == "out":
                    e.activation(OUTT[:, k, :], t, ACT.Copy, scale=self.g(k)).then_inc(K.up("x_normed"), 1)

        def pool(self, e, K):
            if self.stats:
                c0, c1 = self.tokens
                e.wait_ge(sem["sums_done"], K.at("sums_done", 1))
                stats_pool(e, K, True, range(KT), c0, c1, False, "x_normed")

    class Load:

        def sp(self, e, K):
            pass

        pe = dve = pool = sp

    class LoadTransform(Load):
        def act(self, e, K):
            e.wait_ge(sem["input_low"], K.at("input_low"))
            if K.s("products"):
                e.wait_ge(sem["products"], K.at("products"))
                e.wait_ge(sem["hidden_low"], K.at("hidden_low"))
            e.dma_start(DFT[:, :], const[:, C_DFT:C_DFT + 1280]).then_inc(K.up("constants_loaded", 16), 16)

    class LoadRpb(Load):

        def __init__(self, layer):
            self.layer = layer

        def act(self, e, K):
            e.wait_ge(sem["dve_read"], K.at("dve_read"))
            e.wait_ge(sem["products"], K.at("products"))
            flat = A["na_rpb"].rearrange("l h a b -> (l h a b)")
            for r in range(2):
                first = flat.offset + self.layer * 3720 + 464 - (10 - r) * 31 - 15 - 63
                src = bass.AP(flat.tensor, first, [[1, GRID_W], [465, HEADS], [1, RPB_RUN]])
                e.dma_start(RPB[64 * r:64 * r + 64, :, :], src).then_inc(K.up("rpb_loaded", 16), 16)

    class LoadLatentWeights(Load):

        def __init__(self, layer):
            self.layer = layer

        def act(self, e, K):
            e.wait_ge(sem["side_rows"], K.at("side_rows"))
            w_uq, w_qr = (A[n][self.layer].rearrange("(k p) (h c) -> p k h c", p=P, h=HEADS) for n in ("w_uq", "w_qr"))
            for k in range(2):
                e.dma_start(W96[:, k, :, 0:64], w_uq[:, k]).then_inc(K.up("latent_w_loaded", 16), 16)
                e.dma_start(W96[:, k, :, 64:96], w_qr[:, k]).then_inc(K.up("latent_w_loaded", 16), 16)
            e.dma_start(WUK, A["w_uk"][self.layer]).then_inc(K.up("latent_w_loaded", 16), 16)
            e.dma_start(WUV, A["w_uv"][self.layer]).then_inc(K.up("latent_w_loaded", 16), 16)

    class LoadWindows(Load):
        def act(self, e, K):
            e.wait_ge(sem["dve_read"], K.at("dve_read"))
            e.wait_ge(sem["products"], K.at("products"))
            e.wait_ge(sem["hidden_low"], K.at("hidden_low"))
            src = const[:, C_POOL:C_ALL].rearrange("p (g n) -> p g n", g=4)
            e.dma_start(PINV[:, :, :], src).then_inc(K.up("constants_loaded", 16), 16)

    class Fourier:

        def __init__(self, streams):
            self.streams = streams

        def sp(self, e, K):
            pass

        pool = sp

        def pe(self, e, K):
            e.wait_ge(sem["act_read"], K.at("act_read"))
            e.wait_ge(sem["constants_loaded"], K.at("constants_loaded"))
            for b in (4, 5, 6, 7):
                reader, count = K.bank[b]
                e.wait_ge(sem[reader], K.value(reader, count))
            for s in range(self.streams):
                for tt in range(2):
                    for gp in range(2):
                        b = 2 * tt + gp
                        if s:
                            e.wait_ge(sem["branch_low"], K.at("branch_low", 2 * (s - 1) + 2))
                            e.wait_ge(sem["features_copied"], K.at("features_copied", 4 * s))
                        for g in range(2):
                            ins = e.matmul(PS[4 + b][:, 256 * g:256 * g + 256],
                                           FT[:, 2 * gp + g, s * SEQ + tt * P:s * SEQ + tt * P + P],
                                           DFT[:, 0:256], start=True, stop=True)
                        ins.then_inc(K.up("features_done"), 1)
                for gp in range(2):
                    e.wait_ge(sem["features_copied"], K.at("features_copied", 4 * s + 4))
                    for g in range(2):
                        for tt in range(2):
                            u = U[:, tt, 2 * gp + g, :]
                            y = PS[4 + gp][:, 256 * g:256 * g + 256]
                            e.matmul(y, u[:, 0:P], DFT[:, 256 + tt * SEQ:256 + (tt + 1) * SEQ], start=tt == 0, stop=False)
                            ins = e.matmul(y, u[:, P:2 * P], DFT[:, 768 + tt * SEQ:768 + (tt + 1) * SEQ],
                                           start=False, stop=tt == 1)
                    ins.then_inc(K.up("tokens_done"), 1)
            for b in (4, 5):
                K.bank[b] = ("branch_low", K.s("branch_low") + 2 * self.streams)
            for b in (6, 7):
                K.bank[b] = ("features_copied", K.s("features_copied") + 4 * self.streams)

        def act(self, e, K):
            for s in range(self.streams):
                for tt in range(2):
                    for gp in range(2):
                        n = 4 * s + 2 * tt + gp
                        e.wait_ge(sem["features_done"], K.at("features_done", n + 1))
                        if s:
                            e.wait_ge(sem["tokens_done"], K.at("tokens_done", 2 * s))
                        e.activation(U[:, tt, 2 * gp:2 * gp + 2, :], PS[4 + 2 * tt + gp][:, :].rearrange(
                      "p (g n) -> p g n", g=2), ACT.Copy).then_inc(K.up("features_copied"), 1)
                for gp in range(2):
                    e.wait_ge(sem["tokens_done"], K.at("tokens_done", 2 * s + gp + 1))
                    e.activation(YH[:, 2 * gp:2 * gp + 2, s * SEQ:(s + 1) * SEQ],
                                 PS[4 + gp][:, :].rearrange("p (g n) -> p g n", g=2), ACT.Copy) \
                        .then_inc(K.up("branch_high"), 1)

        def dve(self, e, K):
            for s in range(self.streams):
                for gp in range(2):
                    e.wait_ge(sem["branch_high"], K.at("branch_high", 2 * s + gp + 1))
                    y = slice(2 * gp, 2 * gp + 2), slice(s * SEQ, (s + 1) * SEQ)
                    e.tensor_tensor(YL[:, y[0], y[1]], PS[4 + gp][:, :].rearrange("p (g n) -> p g n", g=2),
                                    YH[:, y[0], y[1]].bitcast(F32), ALU.subtract).then_inc(K.up("branch_low"), 1)

    class Bias:

        def sp(self, e, K):
            pass

        pe = act = pool = sp

        def dve(self, e, K):
            e.wait_ge(sem["rpb_loaded"], K.at("rpb_loaded"))
            e.wait_ge(sem["act_read"], K.at("act_read"))
            for h in range(HEADS):
                base = RPB[:, h, 0:RPB_RUN]
                skew = bass.AP(base.tensor, base.offset + RPB_RUN - 1, [list(base.ap[0]), [-31, 6], [-1, GRID_W]])
                win = CON[:, C_WIN:C_WIN + GRID_W].unsqueeze(1).to_broadcast([P, 6, GRID_W])
                e.tensor_tensor(BIAS[:, h, :, :], skew, win, ALU.min).then_inc(K.up("bias_done"), 1)

    class Attention:

        def __init__(self, kind, streams):
            self.kind = kind
            self.steps = [(s, h, qt) for s in range(streams) for h in range(HEADS) for qt in range(2)]

        def sp(self, e, K):
            pass

        pool = sp

        def keys(self, s):
            return (0, TOK) if s == 0 else (SEQ, TOK)

        def qk(self, s, h, qt):
            c0, c1 = self.keys(s)
            q0 = s * SEQ + qt * P
            if self.kind == "na":
                b = 64 * (h % 2)
                return NQ[b:b + 64, h // 2, q0:q0 + P], NK[b:b + 64, h // 2, c0:c1]
            return Q96[0:96, h, q0:q0 + P], K96[0:96, h, c0:c1]

        def pe(self, e, K):
            V = NV if self.kind == "na" else MV
            e.wait_ge(sem["act_read"], K.at("act_read"))
            if self.kind == "mla":
                e.wait_ge(sem["queries_copied"], K.at("queries_copied"))
                e.wait_ge(sem["rotated_done"], K.at("rotated_done"))
            for b in (4, 5, 6, 7):
                reader, count = K.bank[b]
                e.wait_ge(sem[reader], K.value(reader, count))
            n_steps = len(self.steps)

            def scores(n):
                s, h, qt = self.steps[n]
                if n >= 2:
                    e.wait_ge(sem["exp_done"], K.at("exp_done", n - 1))
                q, k = self.qk(s, h, qt)
                c0, c1 = self.keys(s)
                e.matmul(PS[6 + n % 2][:, 0:c1 - c0], q, k, start=True, stop=True).then_inc(K.up("scores_done"), 1)

            def turn(n):
                s, h, qt = self.steps[n]
                c0, c1 = self.keys(s)
                e.wait_ge(sem["probs_ready"], K.at("probs_ready", n + 1))
                if n:
                    e.wait_ge(sem["turned_copied"], K.at("turned_copied", n))
                for j in range((c1 - c0) // P):
                    ins = e.transpose(PS[5][:, j * P:(j + 1) * P], PR[:, n % 2, j * P:(j + 1) * P], IDENT)
                ins.then_inc(K.up("probs_turned"), 1)

            def values(g):
                s, h, _ = self.steps[2 * g]
                c0, c1 = self.keys(s)
                e.wait_ge(sem["turned_copied"], K.at("turned_copied", 2 * g + 2))
                pair = g // 2
                if h % 2 == 0 and pair >= 2:
                    e.wait_ge(sem["branch_low"], K.at("branch_low", pair - 1))
                o = PS[4][64 * (h % 2):64 * (h % 2) + 64, 256 * (pair % 2):256 * (pair % 2) + 256]
                tiles = (c1 - c0) // P
                for j in range(tiles):
                    ins = e.matmul(o, V[:, c0 // P + j, 64 * h:64 * h + 64], PTS[:, g % 2, j, :], start=j == 0,
                                   stop=j == tiles - 1)
                ins.then_inc(K.up("values_done"), 1)

            scores(0)
            scores(1)
            for n in range(n_steps):
                if n + 2 < n_steps:
                    scores(n + 2)
                turn(n)
                if n >= 2 and n % 2 == 0:
                    values(n // 2 - 1)
            values(n_steps // 2 - 1)
            K.bank[4] = ("branch_low", K.s("branch_low") + n_steps // 4)
            K.bank[5] = ("turned_copied", K.s("turned_copied") + n_steps)
            K.bank[6] = K.bank[7] = ("exp_done", K.s("exp_done") + n_steps)

        def outputs(self, pair):
            s = self.steps[4 * pair][0]
            return pair % 4, slice(s * SEQ, (s + 1) * SEQ), slice(256 * (pair % 2), 256 * (pair % 2) + 256)

        def act(self, e, K):
            n_steps = len(self.steps)

            def exp(n):
                s, h, qt = self.steps[n]
                c0, c1 = self.keys(s)
                e.wait_ge(sem["max_done"], K.at("max_done", n + 1))
                if n >= 2:
                    e.wait_ge(sem["probs_turned"], K.at("probs_turned", n - 1))
                e.activation(PR[:, n % 2, 0:c1 - c0], PS[6 + n % 2][:, 0:c1 - c0], ACT.Exp,
                             bias=SM[:, n % 2:n % 2 + 1], accum_out=SM[:, 2 + n % 2:3 + n % 2]) \
                    .then_inc(K.up("exp_done"), 1)

            def turned(n):
                s, h, qt = self.steps[n]
                c0, c1 = self.keys(s)
                g, w = n // 2, c1 - c0
                e.wait_ge(sem["probs_turned"], K.at("probs_turned", n + 1))
                if g >= 2:
                    e.wait_ge(sem["values_done"], K.at("values_done", g - 1))
                e.activation(PTS[:, g % 2, 0:w // P, qt * P:(qt + 1) * P],
                             PS[5][:, 0:w].rearrange("p (j q) -> p j q", q=P), ACT.Copy).then_inc(K.up("turned_copied"), 1)

            def out(pair):
                t, tok, cols = self.outputs(pair)
                e.wait_ge(sem["values_done"], K.at("values_done", 2 * pair + 2))
                e.activation(YH[:, t, tok], PS[4][:, cols], ACT.Copy).then_inc(K.up("branch_high"), 1)

            for n in range(n_steps + 1):
                if n < n_steps:
                    exp(n)
                if n >= 1:
                    turned(n - 1)
                if n >= 5 and (n - 5) % 4 == 0:
                    out((n - 5) // 4)
            out(n_steps // 4 - 1)

        def dve(self, e, K):
            n_steps = len(self.steps)

            def maximum(n):
                s, h, qt = self.steps[n]
                c0, c1 = self.keys(s)
                e.wait_ge(sem["scores_done"], K.at("scores_done", n + 1))
                ps = PS[6 + n % 2]
                if self.kind == "na" and s == 0:
                    loc = ps[:, 0:SEQ].rearrange("p (r c) -> p r c", c=GRID_W)
                    e.tensor_tensor(loc, loc, BIAS[:, h, 2 - 2 * qt:6 - 2 * qt, :], ALU.add) \
                        .then_inc(K.up("dve_done"), 1)
                    e.wait_ge(sem["dve_done"], K.own("dve_done"))
                e.tensor_reduce(SM[:, n % 2:n % 2 + 1], ps[:, 0:c1 - c0], AX.X, ALU.max, negate=True) \
                    .then_inc(K.up("max_done"), 1)

            def normalise(n):
                s, h, qt = self.steps[n]
                c0, c1 = self.keys(s)
                e.wait_ge(sem["exp_done"], K.at("exp_done", n + 1))
                e.reciprocal(SM[:, 4 + n % 2:5 + n % 2], SM[:, 2 + n % 2:3 + n % 2]).then_inc(K.up("dve_done"), 1)
                e.wait_ge(sem["dve_done"], K.own("dve_done"))
                pr = PR[:, n % 2, 0:c1 - c0]
                e.tensor_scalar(pr, pr, SM[:, 4 + n % 2:5 + n % 2], None, ALU.mult).then_inc(K.up("probs_ready"), 1)

            def out(pair):
                t, tok, cols = self.outputs(pair)
                e.wait_ge(sem["branch_high"], K.at("branch_high", pair + 1))
                e.tensor_tensor(YL[:, t, tok], PS[4][:, cols], YH[:, t, tok].bitcast(F32), ALU.subtract) \
                    .then_inc(K.up("branch_low"), 1)

            e.wait_ge(sem["bias_done"], K.own("bias_done"))
            for n in range(n_steps + 1):
                if n < n_steps:
                    maximum(n)
                if n >= 1:
                    normalise(n - 1)
                if n >= 6 and (n - 6) % 4 == 0:
                    out((n - 6) // 4)
            for pair in range((n_steps - 6) // 4 + 1, n_steps // 4):
                out(pair)

    class Latent:

        def __init__(self, layer, nq):
            self.layer, self.nq = layer, nq

        def sp(self, e, K):
            pass

        pool = sp

        def pe(self, e, K):
            nq = self.nq
            for b in (4, 5, 6, 7):
                reader, count = K.bank[b]
                e.wait_ge(sem[reader], K.value(reader, count))
            e.wait_ge(sem["act_done"], K.at("act_done", 3))
            e.matmul(PS[4][:, 0:nq], ONES[:, :], SQ3[:, 0, 0:nq], start=True, stop=False)
            e.matmul(PS[4][:, 0:nq], ONES[:, :], SQ3[:, 1, 0:nq], start=False, stop=True)
            e.matmul(PS[5][:, :], ONES[:, :], SQ3[:, 2, :], start=True, stop=True).then_inc(K.up("squares_summed"), 1)
            e.matmul(PS[6][64:96, 0:SEQ], CON[64:96, C_ROT:C_ROT + 32], KR[64:96, 0:SEQ], start=True, stop=True) \
                .then_inc(K.up("rotary_done"), 1)
            e.wait_ge(sem["latent_normed"], K.at("latent_normed", 3))
            e.wait_ge(sem["latent_w_loaded"], K.at("latent_w_loaded"))
            e.wait_ge(sem["rotated_done"], K.at("rotated_done", 1))
            e.wait_ge(sem["root_done"], K.at("root_done", 2))
            for h in range(HEADS):
                b = 4 + 2 * (h % 2)
                if h >= 2:
                    e.wait_ge(sem["queries_copied"], K.at("queries_copied", h - 1))
                for k in range(2):
                    ins = e.matmul(PS[b][0:96, 0:nq], W96[:, k, h, :], CQ[:, k, 0:nq], start=k == 0, stop=k == 1)
                ins.then_inc(K.up("qkv_done"), 1)
                if h >= 2:
                    e.wait_ge(sem["keys_copied"], K.at("keys_copied", h - 1))
                e.matmul(PS[b + 1][0:64, :], WUK[:, 64 * h:64 * h + 64], CKV[:, :], start=True, stop=True) \
                    .then_inc(K.up("qkv_done"), 1)
            for t in range(4):
                b = 4 + 2 * (t % 2)
                e.wait_ge(sem["queries_copied"], K.at("queries_copied", 7 + t))
                e.matmul(PS[b][:, :], CKV[:, t * P:(t + 1) * P], WUV, start=True, stop=True).then_inc(K.up("qkv_done"), 1)
            e.wait_ge(sem["queries_copied"], K.at("queries_copied", 8))
            for j in range(4):
                b = 5 + 2 * (j % 2)
                if j < 2:
                    e.wait_ge(sem["keys_copied"], K.at("keys_copied", 8))
                else:
                    e.wait_ge(sem["rotated_done"], K.at("rotated_done", 1 + j - 1))
                e.matmul(PS[b][64:96, :], CON[64:96, C_ROT:C_ROT + 32], Q96[64:96, 2 * j:2 * j + 2, 0:SEQ],
                         start=True, stop=True).then_inc(K.up("rotary_done"), 1)
            K.bank[4] = K.bank[6] = ("queries_copied", K.s("queries_copied") + 12)
            K.bank[5] = K.bank[7] = ("rotated_done", K.s("rotated_done") + 5)

        def act(self, e, K):
            nq = self.nq
            e.wait_ge(sem["act_read"], K.own("act_read"))
            for t in range(2):
                e.activation(SQ3[:, t, 0:nq], CQ[:, t, 0:nq], ACT.Square).then_inc(K.up("act_done"), 1)
            e.activation(SQ3[:, 2, :], CKV[:, :], ACT.Square).then_inc(K.up("act_done"), 1)
            e.wait_ge(sem["var_done"], K.at("var_done", 1))
            e.activation(RT[:, 0, 0:nq], RT[:, 0, 0:nq], ACT.Sqrt).then_inc(K.up("root_done"), 1)
            e.activation(RT[:, 1, :], RT[:, 1, :], ACT.Sqrt).then_inc(K.up("root_done"), 1)
            for h in range(HEADS):
                e.wait_ge(sem["qkv_done"], K.at("qkv_done", 2 * h + 1))
                e.activation(Q96[0:96, h, 0:nq], PS[4 + 2 * (h % 2)][0:96, 0:nq], ACT.Copy, scale=MLA_SCALE) \
                    .then_inc(K.up("queries_copied"), 1)
            for t in range(4):
                e.wait_ge(sem["qkv_done"], K.at("qkv_done", 17 + t))
                if t == 0:
                    e.wait_ge(sem["squares_summed"], K.at("squares_summed", 1))
                    e.wait_ge(sem["latent_normed"], K.at("latent_normed", 3))
                e.activation(MV[:, t, :], PS[4 + 2 * (t % 2)][:, :], ACT.Copy).then_inc(K.up("queries_copied"), 1)

        def dve(self, e, K):
            nq, l = self.nq, self.layer
            e.wait_ge(sem["squares_summed"], K.at("squares_summed", 1))
            e.tensor_scalar(RT[:, 0, 0:nq], PS[4][:, 0:nq], 1.0 / 256, LN_EPS, ALU.mult, ALU.add) \
                .then_inc(K.up("dve_done"), 1)
            e.tensor_scalar(RT[:, 1, :], PS[5][:, :], 1.0 / 128, LN_EPS, ALU.mult, ALU.add).then_inc(K.up("var_done"), 1)
            e.wait_ge(sem["rotary_done"], K.at("rotary_done", 1))
            e.wait_ge(sem["act_read"], K.at("act_read"))
            e.tensor_tensor(SM_ROPE[64:96, 0, :], PS[6][64:96, 0:SEQ], SIN, ALU.mult).then_inc(K.up("dve_done"), 1)
            e.wait_ge(sem["dve_done"], K.own("dve_done"))
            e.tensor_tensor(KR[64:96, 0:SEQ], KR[64:96, 0:SEQ], COS, ALU.mult).then_inc(K.up("dve_done"), 1)
            e.wait_ge(sem["dve_done"], K.own("dve_done"))
            e.tensor_tensor(KR[64:96, 0:SEQ], KR[64:96, 0:SEQ], SM_ROPE[64:96, 0, :], ALU.add) \
                .then_inc(K.up("dve_done"), 1)
            e.wait_ge(sem["dve_done"], K.own("dve_done"))
            e.tensor_copy(K96[64:96, :, :], KR[64:96, :].unsqueeze(1).to_broadcast([32, HEADS, TOK])) \
                .then_inc(K.up("rotated_done"), 1)
            e.wait_ge(sem["root_done"], K.at("root_done", 2))
            e.reciprocal(RT[:, 0, 0:nq], RT[:, 0, 0:nq]).then_inc(K.up("dve_done"), 1)
            e.reciprocal(RT[:, 1, :], RT[:, 1, :]).then_inc(K.up("dve_done"), 1)
            e.wait_ge(sem["dve_done"], K.own("dve_done"))
            for t in range(2):
                e.scalar_tensor_tensor(out=CQ[:, t, 0:nq], in0=CQ[:, t, 0:nq], scalar=vec("mla_q_norm_g", 2 * l + t),
                                       in1=RT[:, 0, 0:nq], op0=ALU.mult, op1=ALU.mult).then_inc(K.up("latent_normed"), 1)
            e.scalar_tensor_tensor(out=CKV[:, :], in0=CKV[:, :], scalar=vec("mla_kv_norm_g", l), in1=RT[:, 1, :],
                                   op0=ALU.mult, op1=ALU.mult).then_inc(K.up("latent_normed"), 1)
            for h in range(HEADS):
                e.wait_ge(sem["qkv_done"], K.at("qkv_done", 2 * h + 2))
                e.tensor_copy(K96[0:64, h, :], PS[5 + 2 * (h % 2)][0:64, :]).then_inc(K.up("keys_copied"), 1)
            e.wait_ge(sem["keys_copied"], K.own("keys_copied"))
            for j in range(4):
                e.wait_ge(sem["rotary_done"], K.at("rotary_done", 2 + j))
                q = Q96[64:96, 2 * j:2 * j + 2, 0:SEQ]
                t = SM_ROPE[64:96, :, :]
                sin, cos = (a.unsqueeze(1).to_broadcast([32, 2, SEQ]) for a in (SIN, COS))
                e.tensor_tensor(t, PS[5 + 2 * (j % 2)][64:96, :].rearrange("p (h n) -> p h n", h=2), sin, ALU.mult) \
                    .then_inc(K.up("dve_done"), 1)
                e.wait_ge(sem["dve_done"], K.own("dve_done"))
                e.tensor_tensor(q, q, cos, ALU.mult).then_inc(K.up("dve_done"), 1)
                e.wait_ge(sem["dve_done"], K.own("dve_done"))
                e.tensor_tensor(q, q, t, ALU.add).then_inc(K.up("rotated_done"), 1)
                e.wait_ge(sem["rotated_done"], K.own("rotated_done"))

    SM_ROPE = reg("ROPE_T", 10752, [P, 2, SEQ])

    class Start:

        def sp(self, e, K):
            pass

        def act(self, e, K):
            e.dma_start(CON[:, :], const[:, 0:C_KEEP]).then_inc(K.up("constants_loaded", 16), 16)
            e.wait_ge(sem["dve_done"], K.at("dve_done", 1))
            for name, n in VECTORS:
                t, r = place[name]
                src = A[name].rearrange(DIMS[len(A[name].shape)]).rearrange("(n p) -> n p", p=P)
                e.dma_start(VROWS[r:r + n, t, :], src).then_inc(K.up("constants_loaded", 16), 16)
            e.dma_start(XIN[:, 0:2, :], A["x"][0].rearrange("(t p) d -> p t d", p=P)).then_inc(K.up("tokens_loaded", 16), 16)
            e.dma_start(XIN[:, 2:4, :], A["ctx"][0].rearrange("(t p) d -> p t d", p=P)) \
                .then_inc(K.up("tokens_loaded", 16), 16)
            e.wait_ge(sem["copied_out"], K.at("copied_out", 1))
            e.wait_ge(sem["dve_done"], K.at("dve_done", 4))
            for v, name in enumerate(("c", "c_ctx", "c_2")):
                e.activation(CC[:, :, v], vec(name, 0, 8), ACT.Silu).then_inc(K.up("silu_done"), 1)

        def dve(self, e, K):
            e.memset(VROWS[:, :, :], 0.0).then_inc(K.up("dve_done"), 1)
            e.wait_ge(sem["dve_done"], K.own("dve_done"))
            e.memset(ONES[:, :], 1.0).then_inc(K.up("dve_done"), 1)
            e.memset(SM[:, :], 0.0).then_inc(K.up("dve_done"), 1)
            e.memset(CC[:, :, :], 0.0).then_inc(K.up("dve_done"), 1)
            e.wait_ge(sem["vectors_turned"], K.at("vectors_turned", 1))
            e.tensor_copy(VEC[:, :, :], PS[6][:, :].rearrange("p (t r) -> p t r", t=4)).then_inc(K.up("copied_out"), 1)
            for k in range(KT):
                e.wait_ge(sem["x_turned"], K.at("x_turned", k + 1))
                e.tensor_copy(X[:, k, :], PS[k % 4][:, :]).then_inc(K.up("dve_read"), 1)

        def pe(self, e, K):
            e.wait_ge(sem["constants_loaded"], 16 * (1 + len(VECTORS)))
            for t in range(4):
                ins = e.transpose(PS[6][:, t * P:(t + 1) * P], VROWS[:, t, :], IDENT)
            ins.then_inc(K.up("vectors_turned"), 1)
            e.wait_ge(sem["tokens_loaded"], 32)
            for k in range(KT):
                if k >= 4:
                    e.wait_ge(sem["dve_read"], K.at("dve_read", k - 3))
                for t in range(4):
                    ins = e.transpose(PS[k % 4][:, t * P:(t + 1) * P], XIN[:, t, k * P:(k + 1) * P], IDENT)
                ins.then_inc(K.up("x_turned"), 1)
            for b in range(4):
                K.bank[b] = ("dve_read", K.s("dve_read") + 5 + b)
            for b in range(4, 8):
                K.bank[b] = ("copied_out", K.s("copied_out") + 1)
            e.wait_ge(sem["silu_done"], K.at("silu_done", 3))

        def pool(self, e, K):
            stats_pool(e, K, True, range(KT), 0, TOK, True, "dve_read")

    DIMS = {1: "a -> a", 2: "a b -> (a b)", 3: "a b c -> (a b c)"}

    class Lru:

        def sp(self, e, K):
            pass

        pe = pool = sp

        def act(self, e, K):
            e.wait_ge(sem["lambda_done"], K.at("lambda_done"))
            e.wait_ge(sem["act_read"], K.own("act_read"))
            for k in range(KT):
                e.activation(LT[:, k, :], LA[:, k, :], ACT.Tanh, scale=DER[:, 7, k:k + 1]).then_inc(K.up("act_done"), 1)
            e.wait_ge(sem["act_done"], K.own("act_done"))
            for k in range(KT):
                e.activation(LA[:, k, :], LA[:, k, :], ACT.Exp, scale=DER[:, 6, k:k + 1]).then_inc(K.up("decay_done"), 1)
            e.wait_ge(sem["one_minus_a2"], K.at("one_minus_a2", 1))
            e.activation(LT[:, :, :], LT[:, :, :], ACT.Sqrt).then_inc(K.up("decay_done"), 1)

        def dve(self, e, K):
            e.wait_ge(sem["act_read"], K.at("act_read"))
            e.tensor_tensor(GI[:, :, :], GI[:, :, :], XC[:, :, :], ALU.mult).then_inc(K.up("dve_done"), 1)
            e.wait_ge(sem["dve_done"], K.own("dve_done"))
            e.wait_ge(sem["decay_done"], K.at("decay_done", KT))
            e.tensor_tensor(XC[:, :, :], LA[:, :, :], LA[:, :, :], ALU.mult).then_inc(K.up("dve_done"), 1)
            e.wait_ge(sem["dve_done"], K.own("dve_done"))
            e.scalar_tensor_tensor(out=LT[:, :, :], in0=XC[:, :, :], scalar=1.0, in1=LT[:, :, :], op0=ALU.add,
                                   op1=ALU.mult).then_inc(K.up("one_minus_a2"), 1)
            e.wait_ge(sem["one_minus_a2"], K.own("one_minus_a2"))
            e.wait_ge(sem["decay_done"], K.at("decay_done", KT + 1))
            e.tensor_tensor(GI[:, :, :], GI[:, :, :], LT[:, :, :], ALU.mult).then_inc(K.up("dve_done"), 1)
            e.wait_ge(sem["dve_done"], K.own("dve_done"))
            for k in range(KT):
                e.tensor_tensor_scan(XC[:, k, :], LA[:, k, :], GI[:, k, :], 0.0, ALU.mult, ALU.add) \
                    .then_inc(K.up("dve_done"), 1)
            e.wait_ge(sem["dve_done"], K.own("dve_done"))
            e.tensor_tensor(XC[:, :, :], XC[:, :, :], GB[:, :, :], ALU.mult).then_inc(K.up("dve_done"), 1)
            e.wait_ge(sem["dve_done"], K.own("dve_done"))
            e.tensor_copy(AH[:, :, 0:SEQ], XC[:, :, :]).then_inc(K.up("dve_done"), 1)
            e.wait_ge(sem["dve_done"], K.own("dve_done"))
            for k in range(KT):
                e.tensor_tensor(AL[:, k, 0:SEQ], XC[:, k, :], AH[:, k, 0:SEQ].bitcast(F32), ALU.subtract) \
                    .then_inc(K.up("input_low"), 1)

    class Conv(Copied):

        def read_act(self, e, K, m):
            i = self.tile0 + m
            e.activation(XR[:, i, 3:3 + SEQ], PS[m][:, 0:SEQ], ACT.Identity, bias=vec("lru_b_in_2", i)) \
                .then_inc(K.up("act_read"), 1)

        def read_dve(self, e, K, m):
            i = self.tile0 + m
            if i == 0:
                e.memset(XR[:, :, 0:3], 0.0).then_inc(K.up("dve_done"), 1)
                e.wait_ge(sem["dve_done"], K.own("dve_done"))
            e.wait_ge(sem["act_read"], K.at("act_read", m + 1))
            xc = XC[:, i, :]
            e.tensor_scalar(xc, XR[:, i, 0:SEQ], vec("lru_conv_w_2", i), vec("lru_conv_b_2", i), ALU.mult, ALU.add) \
                .then_inc(K.up("dve_done"), 1)
            e.wait_ge(sem["dve_done"], K.own("dve_done"))
            for t in range(1, 4):
                e.scalar_tensor_tensor(out=xc, in0=XR[:, i, t:t + SEQ], scalar=vec("lru_conv_w_2", 8 * t + i),
                                       in1=xc, op0=ALU.mult, op1=ALU.add).then_inc(K.up("dve_done"), 1)
                e.wait_ge(sem["dve_done"], K.own("dve_done"))
            e.tensor_copy(Y8H[:, i, :], xc).then_inc(K.up("dve_done"), 1)
            e.wait_ge(sem["dve_done"], K.own("dve_done"))
            e.tensor_tensor(Y8L[:, i, :], xc, Y8H[:, i, :].bitcast(F32), ALU.subtract).then_inc(K.up("hidden_low"), 1)

    class Blocks(Columns):

        kt = 2
        tokens = (0, SEQ)
        ready = ("hidden_low", False)

        def src(self, K, p):
            return rows(self.w[2 * self.u + p])

        def moving(self, m, k, c0, c1):
            i = 2 * (2 * self.u + m // 2) + k
            return Y8H[:, i, :], Y8L[:, i, :]

    class GateBlocks(Blocks):
        def read_act(self, e, K, m):
            i = 4 * self.u + m
            e.activation(self.dst[:, i, :], PS[m][:, 0:SEQ], ACT.Sigmoid, bias=vec(self.bias, i)) \
                .then_inc(K.up("act_read"), 1)

    class PoolBlocks(Blocks, Residual):
        read = "dddd"
        src = Blocks.src

    class Pooling:

        def sp(self, e, K):
            pass

        pe = pool = act = sp

        def dve(self, e, K):
            e.memset(PS1[:, :, 0:16], 0.0).then_inc(K.up("dve_done"), 1)
            e.wait_ge(sem["dve_done"], K.own("dve_done"))
            e.memset(PS2[:, :, 0:16], 0.0).then_inc(K.up("dve_done"), 1)
            e.wait_ge(sem["dve_done"], K.own("dve_done"))
            e.wait_ge(sem["x_normed"], K.at("x_normed"))
            e.wait_ge(sem["constants_loaded"], K.at("constants_loaded"))
            last = 16 + SEQ
            src = None
            for g in range(4):
                lag, lo = 1 << g, 2 * g
                a = PA if g == 0 else (PS1, PS2)[(g + 1) % 2]
                o = (PS1, PS2)[g % 2]
                if g == 0:
                    e.tensor_copy(PS2[:, :, 16:last], PA[:, :, :]).then_inc(K.up("dve_done"), 1)
                    e.wait_ge(sem["dve_done"], K.own("dve_done"))
                    a = PS2
                e.tensor_tensor(o[:, lo:8, 16:last], a[:, lo:8, 16:last], a[:, lo:8, 16 - lag:last - lag],
                                ALU.add).then_inc(K.up("dve_done"), 1)
                e.wait_ge(sem["dve_done"], K.own("dve_done"))
                inv = PINV[:, g, :].unsqueeze(1).to_broadcast([P, 2, SEQ])
                e.tensor_tensor(o[:, lo:lo + 2, 16:last], o[:, lo:lo + 2, 16:last], inv, ALU.mult) \
                    .then_inc(K.up("dve_done"), 1)
                e.wait_ge(sem["dve_done"], K.own("dve_done"))
                e.tensor_tensor(PA[:, lo:lo + 2, :], o[:, lo:lo + 2, 16:last], PA[:, lo:lo + 2, :],
                                ALU.subtract).then_inc(K.up("dve_done"), 1)
                e.wait_ge(sem["dve_done"], K.own("dve_done"))
                e.tensor_copy(Y8H[:, lo:lo + 2, :], PA[:, lo:lo + 2, :]).then_inc(K.up("dve_done"), 1)
                e.wait_ge(sem["dve_done"], K.own("dve_done"))
                e.tensor_tensor(Y8L[:, lo:lo + 2, :], PA[:, lo:lo + 2, :], Y8H[:, lo:lo + 2, :].bitcast(F32),
                                ALU.subtract).then_inc(K.up("hidden_low"), 1)
                e.wait_ge(sem["hidden_low"], K.own("hidden_low"))

    class Finish:

        def pool(self, e, K):
            pass

        def pe(self, e, K):
            for b in range(4):
                reader, count = K.bank[b]
                e.wait_ge(sem[reader], K.value(reader, count))
            e.wait_ge(sem["x_normed"], K.at("x_normed"))
            for t in range(2):
                for half in range(2):
                    for j in range(4):
                        ins = e.transpose(PS[2 * t + half][:, j * P:(j + 1) * P],
                                          OUTT[:, 4 * half + j, t * P:(t + 1) * P], IDENT)
                    ins.then_inc(K.up("x_turned"), 1)

        def dve(self, e, K):
            for n in range(0, 4, 2):
                e.wait_ge(sem["x_turned"], K.at("x_turned", n + 1))
                e.tensor_copy(OUTS[:, n // 2, 0:512], PS[n][:, :]).then_inc(K.up("copied_out"), 1)

        def act(self, e, K):
            for n in range(1, 4, 2):
                e.wait_ge(sem["x_turned"], K.at("x_turned", n + 1))
                e.activation(OUTS[:, n // 2, 512:1024], PS[n][:, :], ACT.Copy).then_inc(K.up("act_done"), 1)

        def sp(self, e, K):
            for t in range(2):
                e.wait_ge(sem["copied_out"], K.at("copied_out", t + 1))
                e.wait_ge(sem["act_done"], K.at("act_done", t + 1))
                e.dma_start(out[0].rearrange("(t p) d -> p t d", p=P)[:, t, :], OUTS[:, t, :]) \
                    .then_inc(K.up("out_done", 16), 16)
            e.wait_ge(sem["out_done"], K.at("out_done", 32))

    class LruConst:

        def sp(self, e, K):
            pass

        pe = pool = sp

        def dve(self, e, K):
            lam = vec("lru_lambda_2", 0, 8)
            w, z, y, q, m = (DER[:, j, :] for j in (8, 9, 10, 11, 5))
            
            def st(ins):
                ins.then_inc(K.up("dve_done"), 1)
                e.wait_ge(sem["dve_done"], K.own("dve_done"))

            st(e.tensor_scalar(w, lam, -1.0, None, ALU.mult))
            e.tensor_tensor(w, w, lam, ALU.max).then_inc(K.up("lambda_done"), 1)
            e.wait_ge(sem["silu_done"], K.at("silu_done", 1))
            st(e.tensor_scalar(z, w, 2.0, None, ALU.add))
            st(e.reciprocal(z, z))
            st(e.tensor_tensor(z, z, w, ALU.mult))
            st(e.tensor_tensor(y, z, z, ALU.mult))
            st(e.memset(q, 1.0 / 17))
            for n in (15, 13, 11, 9, 7, 5, 3, 1):
                st(e.tensor_tensor(q, q, y, ALU.mult))
                st(e.tensor_scalar(q, q, 1.0 / n, None, ALU.add))
            st(e.tensor_tensor(z, z, q, ALU.mult))
            st(e.tensor_scalar(m, lam, 0.0, None, ALU.min))
            st(e.scalar_tensor_tensor(out=z, in0=z, scalar=-2.0, in1=m, op0=ALU.mult, op1=ALU.add))
            st(e.tensor_scalar(DER[:, 6, :], z, 8.0, None, ALU.mult))
            e.tensor_scalar(DER[:, 7, :], z, -8.0, None, ALU.mult).then_inc(K.up("lambda_done"), 1)
            e.wait_ge(sem["lambda_done"], K.own("lambda_done"))

        def act(self, e, K):
            e.wait_ge(sem["lambda_done"], K.at("lambda_done", 1))
            e.activation(DER[:, 8, :], DER[:, 8, :], ACT.Exp, scale=-1.0).then_inc(K.up("silu_done"), 1)

    def prep_ln(gname, bname, row, alpha, mat, chunk_sc, streams):
        def f(e, K):
            e.tensor_scalar(DER[:, 0, :], vec(gname, row, 8), alpha, None, ALU.mult).then_inc(K.up("dve_done"), 1)
            e.tensor_scalar(DER[:, 1, :], vec(bname, row, 8), alpha, None, ALU.mult).then_inc(K.up("dve_done"), 1)
            if mat is not None:
                e.wait_ge(sem["side_added"], K.own("side_added"))
                for s in range(streams):
                    e.tensor_scalar(DER[:, 2 + s, :], mod(mat, chunk_sc, s), 1.0, 1.0 / alpha, ALU.add, ALU.mult) \
                        .then_inc(K.up("dve_done"), 1)
        return f

    def prep_gain(mat, chunk, streams):
        def f(e, K):
            e.wait_ge(sem["side_added"], K.own("side_added"))
            for s in range(streams):
                e.tensor_scalar(DER[:, 4 + s, :], mod(mat, chunk, s), 1.0, None, ALU.add).then_inc(K.up("dve_done"), 1)
                e.wait_ge(sem["dve_done"], K.own("dve_done"))
        return f

    def prep_rms(gname, row, mat, chunk_sc):
        def f(e, K):
            e.wait_ge(sem["side_added"], K.own("side_added"))
            e.scalar_tensor_tensor(out=DER[:, 2, :], in0=mod(mat, chunk_sc, 2), scalar=1.0,
                                   in1=vec(gname, row, 8), op0=ALU.add, op1=ALU.mult).then_inc(K.up("dve_done"), 1)
            e.wait_ge(sem["dve_done"], K.own("dve_done"))
        return f

    def prep_pool(e, K):
        e.wait_ge(sem["side_added"], K.own("side_added"))
        e.tensor_tensor(DER[:, 3, :], mod(3, 2, 2), vec("pool_scale_2", 0, 8), ALU.mult).then_inc(K.up("dve_done"), 1)
        e.wait_ge(sem["dve_done"], K.own("dve_done"))

    seq = []
    wi = [A["w_in"][l] for l in range(2)]

    def sides(layer):
        return iter(SIDES[layer])

    SIDES = {
        0: [(0, c) for c in range(4, 12)] + [(2, c) for c in range(4)],
        1: [(2, c) for c in range(9, 12)] + [(3, c) for c in range(9)],
    }

    def up_gated(l, tokens, col, h0, per, side):
        return UpGated(layer=l, tokens=tokens, col=col, h0=h0, per_turn=per, side=side, ready=("input_low", True))

    def next_side(it):
        s = next(it, None)
        return Side(*s) if s else None

    start = Start()
    seq.append(start)
    seq.append(SideOnly(Side(0, 0)))
    seq.append(("loop", 3, [SideOnly(Side(0, 1, 1))]))

    for l in range(2):
        N = TOK if l == 0 else SEQ
        streams = N // SEQ
        tok = (0, N)
        it = sides(l)
        if l == 0:
            seq.append(Norm(tokens=tok, g=lambda k: DER[:, 0, k:k + 1], b=lambda k: DER[:, 1, k:k + 1],
                            sc=lambda s, k: DER[:, 2 + s, k:k + 1], sh=lambda s, k: mod(0, 0, s, k),
                            prep=prep_ln("ln_in_g", "ln_in_b", 0, ALPHA, 0, 1, 2)))
        seq.append(LoadTransform())
        seq.append(Copied(w=wi[l], cols=(0, 256), tokens=tok, side=next_side(it), ready=("input_low", True),
                          dst=lambda m, N=N: FT[:, m, 0:N]))
        if l == 0:
            first_unit = seq[-1]
        seq.append(Fourier(streams))

        def merge(b):
            for half in range(2):
                g0 = 2464 + b * D + half * 512
                seq.append(Copied(w=wi[l], cols=(g0, g0 + 256), tokens=tok, side=next_side(it), func=ACT.Sigmoid,
                                  dst=lambda m, N=N: GATE[:, m, 0:N]))
                seq.append(Branch(w=A["w_branch"][l][b], cols=(half * 512, half * 512 + 256), tokens=tok, b=b,
                                  half=half, ready=("branch_low", False)))

        merge(0)
        seq.append(Copied(w=wi[l], cols=(512, 768), tokens=tok, side=next_side(it), scale=NA_SCALE,
                          dst=lambda m, N=N: NQ[:, m, 0:N]))
        seq.append(Copied(w=wi[l], cols=(1024, 1280), side=next_side(it), dst=lambda m: NK[:, m, :]))
        seq.append(LoadRpb(l))
        seq.append(Values(w=wi[l], cols=(1536, 1792), side=next_side(it)))
        seq.append(Bias())
        seq.append(Attention("na", streams))
        merge(1)
        small = Compressed(w=wi[l], cols=(2048, 2304), offs=(0, P, 0, 64), tokens=tok,
                       dst=lambda m, N=N: (CQ[:, 0, 0:N], CQ[:, 1, 0:N], CKV[:, :], KR[:, :])[m])
        seq.append(LoadLatentWeights(l))
        seq.append(small)
        seq.append(Latent(l, N))
        seq.append(Attention("mla", streams))
        merge(2)
        for half in range(2):
            seq.append(Residual(w=A["w_out"][l], cols=(half * 512, half * 512 + 256), tokens=tok, rhs=(HH, HL),
                                ready=("hidden_low", False), side=next_side(it), tile0=4 * half, first=half == 0,
                                scale=lambda s, i: DER[:, 4 + s, i:i + 1], prep=prep_gain(l, 2, streams) if half == 0 else None))
        seq.append(Norm(tokens=tok, g=lambda k: DER[:, 0, k:k + 1], b=lambda k: DER[:, 1, k:k + 1],
                        sc=lambda s, k: DER[:, 2 + s, k:k + 1], sh=lambda s, k, l=l: mod(l, 3, s, k),
                        prep=prep_ln("ln1_g", "ln1_b", 8 * l, ALPHA, l, 4, streams)))
        assert next(it, None) is None, "a modulation chunk has no place"

        def down(krow, kt, half, per, side, last):
            return Down(w=A["w_ffn_down"][l], cols=(half * 512, half * 512 + 256), tokens=tok, krow=krow, kt=kt,
                        rhs_count=kt, per_turn=per, side=side, tile0=4 * half, first=half == 0, stats=last,
                        scale=lambda s, i: DER[:, 4 + s, i:i + 1],
                        prep=prep_gain(l, 5, streams) if half == 0 else None)

        body = [up_gated(l, tok, 256 * u, 2 * u, 1024, None) for u in range(4)]
        body += [down(0, 8, half, 8, None, False) for half in range(2)]
        if l == 0:
            for u in range(6):
                body[u].side = Side(1, u, 6)
        seq.append(("loop", 2, body))
        last = [(2, c) for c in range(4, 9)] if l == 0 else [(3, 9), (3, 10), (3, 11)]
        tail_sides = [Side(*c) for c in last] + [None] * (5 - len(last))
        seq += [up_gated(l, tok, 2048 + 256 * u, 2 * u, 0, tail_sides[u]) for u in range(3)]
        seq += [down(16, 6, half, 0, tail_sides[3 + half], True) for half in range(2)]
        final = l == 1
        seq.append(Norm(tokens=tok, g=lambda k: DER[:, 0, k:k + 1], b=lambda k: DER[:, 1, k:k + 1],
                        sc=lambda s, k: DER[:, 2 + s, k:k + 1], sh=lambda s, k: mod(1, 0, s, k),
                        to=None if final else "a", stats=final,
                        prep=prep_ln("ln2_g", "ln2_b", 8 * l, 1.0 if final else ALPHA, None if final else 1, 1, 2)))

    lat = (0, SEQ)

    def rms(gname, row, mat, chunk, **kw):
        return Norm(tokens=lat, mean=False, write_x=False, eps=RMS_EPS, sc=lambda s, k: DER[:, 2, k:k + 1],
                    sh=lambda s, k: mod(mat, chunk, 2, k), prep=prep_rms(gname, row, mat, chunk + 1), **kw)

    def mlp(layer):
        w1, w2 = A["ffn_w1_2"][layer], A["ffn_w2_2"][layer]

        def part(base, per, last):
            units = [UpSquared(w=w1, cols=(base * P + 512 * u, base * P + 512 * u + 256), per_turn=per * P, h0=4 * u,
                               ready=("input_low", True)) for u in range(2)]
            units += [Down(w=w2, cols=(half * 512, half * 512 + 256), tokens=lat, krow=base, kt=8, per_turn=per,
                           tile0=4 * half, first=half == 0, stats=last, mean=False,
                           scale=lambda s, i: mod(2 + layer, 5, 2, i)) for half in range(2)]
            return units

        seq.append(("loop", 3, part(0, 8, False)))
        seq.extend(part(24, 0, True))

    seq.append(rms("norm_mix_g_2", 0, 2, 0))
    for half in range(2):
        seq.append(Gelu(w=A["lru_w_y_2"][0], cols=(half * 512, half * 512 + 256), tokens=lat, ready=("input_low", True),
                        tile0=4 * half))
    seq += [Conv(w=A["lru_w_in_2"][0], cols=(half * 512, half * 512 + 256), tokens=lat, tile0=4 * half) for half in range(2)]
    seq += [GateBlocks(w=A["lru_w_a_2"][0], u=u, dst=LA, bias="lru_b_a_2") for u in range(2)]
    seq += [GateBlocks(w=A["lru_w_x_2"][0], u=u, dst=GI, bias="lru_b_x_2") for u in range(2)]
    seq.append(LruConst())
    seq.append(Lru())
    seq += [Residual(w=A["lru_w_out_2"][0], cols=(half * 512, half * 512 + 256), tokens=lat, tile0=4 * half,
                     first=half == 0, mean=False, bias="lru_b_out_2", ready=("input_low", True),
                     scale=lambda s, i: mod(2, 2, 2, i)) for half in range(2)]
    seq.append(rms("norm_ffn_g_2", 0, 2, 3))
    mlp(0)
    seq.append(rms("norm_mix_g_2", 8, 3, 0, to="pool"))
    seq.append(LoadWindows())
    seq.append(Pooling())
    pool_units = [PoolBlocks(w=A["pool_w_2"][0], u=u, tile0=4 * u, first=u == 0, mean=False, prep=prep_pool if u == 0 else None,
                             scale=lambda s, i: DER[:, 3, i:i + 1]) for u in range(2)]
    seq += pool_units
    seq.append(rms("norm_ffn_g_2", 8, 3, 3))
    mlp(1)
    seq.append(Norm(tokens=lat, mean=False, write_x=False, eps=RMS_EPS, to="out", g=lambda k: vec("final_norm_g_2", k)))
    seq.append(Finish())

    groups = []
    for s in seq:
        if isinstance(s, tuple):
            groups.append((s[1], s[2]) if s[0] == "loop" else (1, s[1]))
        else:
            groups.append((1, [s]))
    units = [s for turns, g in groups for s in g if isinstance(s, Unit)]
    for a, b in zip(units, units[1:]):
        a.nxt = b
    groups.insert(3, (1, [First(first_unit)]))
    write_programs(groups, sem, nc, stack)


ENGINES = ("sp", "act", "dve", "pe", "pool")


def program_of(section, engine):
    return {"sp": section.sp, "act": section.act, "dve": section.dve, "pe": section.pe, "pool": section.pool}[engine]


def after_turns(bank, begin, stride, turns):
    return {b: (reader, v + stride[reader] * (turns - 1) if v > begin[reader] else v)
            for b, (reader, v) in bank.items()}


def count_signals(groups, sems):
    dry = {n: Counts(Quiet(), sems, OWN[n], True) for n in ENGINES}
    now = {n: 0 for n in sems}
    starts, strides, banks = {}, [], []
    for gi, (turns, sections) in enumerate(groups):
        begin = dict(now)
        for si, section in enumerate(sections):
            starts[gi, si] = dict(now)
            for engine in ENGINES:
                dry[engine].start = starts[gi, si]
                program_of(section, engine)(dry[engine].eng, dry[engine])
            now = {n: dry[engine].count[n] for engine in ENGINES for n in OWN[engine]}
        stride = {n: now[n] - begin[n] for n in now}
        strides.append(stride)
        banks.append(dict(dry["pe"].bank))
        now = {n: begin[n] + stride[n] * turns for n in now}
        for engine in ENGINES:
            dry[engine].count = {n: now[n] for n in OWN[engine]}
        dry["pe"].bank = after_turns(dry["pe"].bank, begin, stride, turns)
    return starts, strides, banks


def write_programs(groups, sems, nc, stack):
    starts, strides, banks = count_signals(groups, sems)

    def program(engine, eng):
        K = Counts(eng, sems, OWN[engine])
        for gi, (turns, sections) in enumerate(groups):
            begin, stride = starts[gi, 0], strides[gi]
            if turns == 1:
                for si, section in enumerate(sections):
                    K.start = starts[gi, si]
                    program_of(section, engine)(eng, K)
            elif any(stride[n] for n in K.names):
                if engine == "pe":
                    for b, (reader, v) in sorted(banks[gi].items()):
                        if v > begin[reader]:
                            before, count = K.bank[b]
                            eng.wait_ge(sems[before], count)
                            K.bank[b] = (reader, v - stride[reader])
                with eng.Fori(0, turns) as turn:
                    K.turn, K.stride = turn, stride
                    for si, section in enumerate(sections):
                        K.start = starts[gi, si]
                        program_of(section, engine)(eng, K)
                    K.turn, K.stride = None, {}
                K.count = {n: begin[n] + stride[n] * turns for n in K.names}
                K.bank = after_turns(K.bank, begin, stride, turns)

    block = stack.enter_context(nc.Block())

    @block.sync
    def _(sp):
        program("sp", sp)

    @block.scalar
    def _(act):
        program("act", act)

    @block.vector
    def _(dve):
        program("dve", dve)

    @block.tensor
    def _(pe):
        program("pe", pe)

    @block.gpsimd
    def _(pool):
        program("pool", pool)

    stack.close()


def kernel(**inputs):
    import concourse.bacc as bacc
    from concourse.bass_utils import run_bass_kernel_spmd

    nc = bacc.Bacc("TRN2", target_bir_lowering=False, num_devices=1)
    arrays, aps = {}, {}
    for name in INPUTS:
        a = np.asarray(inputs[name])
        if name == "na_rpb":
            a = a[:, :, ::-1, ::-1]
        a = np.ascontiguousarray(a)
        arrays[f"in_{name}"] = a
        aps[name] = nc.dram_tensor(f"in_{name}", a.shape, mybir.dt.from_np(a.dtype), kind="ExternalInput").ap()
    arrays["in_constants"] = constants()
    const = nc.dram_tensor("in_constants", (P, C_ALL), F32, kind="ExternalInput").ap()
    out = nc.dram_tensor("out", (1, SEQ, D), F32, kind="ExternalOutput").ap()
    build(nc, aps, out, const)
    r = run_bass_kernel_spmd(nc, [arrays], core_ids=[0])
    return np.asarray(r.results[0]["out"])
```

```python
from contextlib import ExitStack

import numpy as np

import concourse.bass as bass
from concourse import mybir

F32 = mybir.dt.float32
F32R = mybir.dt.float32r
ALU = mybir.AluOpType
ACT = mybir.ActivationFunctionType
AX = mybir.AxisListType

P = 128
D = 1024
KT = D // P
SEQ = 256
CTX = 256
TOK = SEQ + CTX
GRID_W = 64
HEADS = 8
KW = 16
NA_SCALE = 64 ** -0.5
MLA_SCALE = 96 ** -0.5
LN_EPS = 1e-5
RMS_EPS = 1e-6
ALPHA = 4 ** 0.25
FFN = 2816
FFN2 = 4096
RPB_RUN = 5 * 31 + GRID_W

C_ID, C_COS, C_SIN, C_WIN, C_ROT, C_SEL = 0, 128, 384, 640, 704, 736
C_KEEP = 740
C_DFT = C_KEEP
C_POOL = C_DFT + 256 + 512 + 512
C_ALL = C_POOL + 4 * SEQ

VECTORS = [
    ("ln_in_g", 8), ("ln_in_b", 8), ("c", 8), ("c_ctx", 8), ("b_mod", 96), ("c_2", 8), ("b_mod_2", 96),
    ("ln1_g", 16), ("ln1_b", 16), ("ln2_g", 16), ("ln2_b", 16), ("mla_q_norm_g", 4),
    ("mla_kv_norm_g", 2), ("norm_mix_g_2", 16), ("norm_ffn_g_2", 16), ("lru_b_y_2", 8), ("lru_b_in_2", 8),
    ("lru_conv_w_2", 32), ("lru_conv_b_2", 8), ("lru_b_a_2", 8), ("lru_b_x_2", 8), ("lru_lambda_2", 8),
    ("lru_b_out_2", 8), ("pool_scale_2", 8), ("final_norm_g_2", 8),
]

INPUTS = ['x', 'c', 'ctx', 'c_ctx', 'ln_in_g', 'ln_in_b', 'w_mod', 'b_mod', 'w_in', 'mla_q_norm_g', 'mla_kv_norm_g',
          'w_uq', 'w_qr', 'w_uk', 'w_uv', 'na_rpb', 'w_branch', 'w_out', 'ln1_g', 'ln1_b', 'ln2_g', 'ln2_b',
          'w_ffn_gate', 'w_ffn_up', 'w_ffn_down', 'c_2', 'w_mod_2', 'b_mod_2', 'norm_mix_g_2', 'norm_ffn_g_2',
          'lru_w_y_2', 'lru_b_y_2', 'lru_w_in_2', 'lru_b_in_2', 'lru_conv_w_2', 'lru_conv_b_2', 'lru_w_a_2',
          'lru_b_a_2', 'lru_w_x_2', 'lru_b_x_2', 'lru_lambda_2', 'lru_w_out_2', 'lru_b_out_2', 'pool_w_2',
          'pool_scale_2', 'ffn_w1_2', 'ffn_w2_2', 'final_norm_g_2']


def constants():
    t = np.zeros((P, C_ALL), np.float64)
    t[:, C_ID:C_ID + P] = np.eye(P)
    pos = np.arange(SEQ)
    inv = 10000.0 ** (-np.arange(8, dtype=np.float64) / 8)
    ang = np.concatenate([(pos // GRID_W)[:, None] * inv, (pos % GRID_W)[:, None] * inv], 1)
    for half in range(2):
        t[64 + 16 * half:80 + 16 * half, C_COS:C_COS + SEQ] = np.cos(ang).T
        t[64 + 16 * half:80 + 16 * half, C_SIN:C_SIN + SEQ] = np.sin(ang).T
    for j in range(16):
        t[64 + 16 + j, C_ROT + j] = -1.0
        t[64 + j, C_ROT + 16 + j] = 1.0
    col = np.arange(P) % GRID_W
    start = np.clip(col - KW // 2, 0, GRID_W - KW)
    key = np.arange(GRID_W)
    inside = (key >= start[:, None]) & (key < start[:, None] + KW)
    t[:, C_WIN:C_WIN + GRID_W] = np.where(inside, 3.0e38, -1.0e30)
    for g in range(4):
        for v in range(3):
            t[32 * g + v, C_SEL + v] = 1.0
    d = np.arange(P)
    fd = 2 * np.pi * np.outer(d, d) / P
    t[:, C_DFT:C_DFT + P] = np.cos(fd)
    t[:, C_DFT + P:C_DFT + 2 * P] = np.sin(fd)
    n = np.arange(SEQ)
    fn = 2 * np.pi * (np.outer(n, n) % SEQ) / SEQ
    norm = (SEQ * P) ** -0.5
    for half in range(2):
        rows = slice(half * P, half * P + P)
        at = C_DFT + 256 + half * SEQ
        t[:, at:at + SEQ] = np.cos(fn)[rows] * norm
        t[:, at + 512:at + 512 + SEQ] = -np.sin(fn)[rows] * norm
    for g, win in enumerate((2, 4, 8, 16)):
        t[:, C_POOL + g * SEQ:C_POOL + (g + 1) * SEQ] = 1.0 / np.minimum(n + 1, win)
    return t.astype(np.float32)


class Quiet:

    def done(self, *a, **k):
        return self

    activation = tensor_tensor = tensor_scalar = scalar_tensor_tensor = tensor_copy = tensor_reduce = done
    reciprocal = memset = matmul = transpose = dma_start = wait_ge = then_inc = mul = copy = done
    tensor_tensor_scan = done


class Counts:

    def __init__(self, eng, sems, own, dry=False):
        self.eng, self.sems, self.names, self.dry = eng, sems, own, dry
        self.start = {n: 0 for n in sems}
        self.count = {n: 0 for n in own}
        self.turn, self.stride = None, {}
        self.bank = {}

    def s(self, name):
        return self.start[name]

    def value(self, name, value):
        if self.turn is not None and self.stride.get(name):
            assert value > 0, (name, value)
            return self.turn * self.stride[name] + value
        assert value > 0 or self.dry, (name, value)
        return value

    def at(self, name, further=0):
        return self.value(name, self.start[name] + further)

    def own(self, name):
        return self.value(name, self.count[name])

    def up(self, name, by=1):
        assert name in self.names, name
        self.count[name] += by
        return self.sems[name]


OWN = {
    "sp": ["pair0_loaded", "pair1_loaded", "tokens_loaded", "vectors_loaded", "chunk0_loaded", "chunk1_loaded",
           "chunk2_loaded", "chunk3_loaded", "side_loaded", "out_done"],
    "act": ["weight_high", "act_read", "side_row_copied", "act_done", "x_normed", "modulated", "root_done",
            "exp_done", "turned_copied", "branch_high", "features_copied", "queries_copied", "constants_loaded",
            "rpb_loaded", "latent_w_loaded", "silu_done", "last_squared", "normed_squared", "decay_done",
            "decay_squared"],
    "dve": ["weight_low", "dve_read", "side_added", "dve_done", "centred", "input_low", "one_minus_a2", "scanned",
            "pooled", "max_done", "probs_ready", "branch_low", "keys_copied", "hidden_low", "var_done",
            "rotary_copied", "rotated_done", "lambda_done", "bias_done", "latent_normed", "copied_out"],
    "pe": ["products", "squares_added", "side_rows", "side_turned", "sums_done", "scores_done", "probs_turned",
           "values_done", "features_done", "tokens_done", "squares_summed", "qkv_done", "rotary_done", "x_turned",
           "vectors_turned"],
    "pool": ["pool_done", "gated_done", "pooled_last"],
}


def build(nc, A, out, const):
    stack = ExitStack()
    offset = [16512]

    def sb(name, shape, dt=F32, at=None):
        size = 4
        for s in shape[1:]:
            size *= s
        if at is None:
            at = offset[0]
            offset[0] += (size + 31) // 32 * 32
        assert at + size <= 229344, (name, at + size)
        return nc.alloc_sbuf_tensor_at(name, list(shape), dt, offset=at)

    X = sb("X", [P, KT, TOK])
    AH_AT = offset[0]
    AH = sb("AH", [P, KT, TOK], F32R)
    AL_AT = offset[0]
    AL = sb("AL", [P, KT, TOK], F32R)
    SH = sb("SH", [P, 4, KT, P], F32R)
    SL = sb("SL", [P, 4, KT, P], F32R)
    RAW = [sb(f"RAW{p}", [P, KT, 2 * P]) for p in range(2)]
    SIDE = sb("SIDE", [P, KT, 512])
    YH_AT = offset[0]
    YH = sb("YH", [P, 4, TOK], F32R)
    YL = sb("YL", [P, 4, TOK], F32R)
    MACC = sb("MACC", [P, KT, TOK])
    VEC = sb("VEC", [P, 4, P])
    MODT = sb("MODT", [P, 4, 48, 3])
    CC = sb("CC", [P, KT, 32])
    CON = sb("CON", [P, C_KEEP])
    ONES = sb("ONES", [P, P])
    MODROW = sb("MODROW", [P, 512])
    DER = sb("DER", [P, 12, KT])
    SM = sb("SM", [P, 16])
    REG = offset[0]

    def reg(name, at, shape, dt=F32):
        return sb(name, shape, dt, at=REG + 4 * at)

    FT = reg("FT", 0, [P, 4, TOK])
    U = reg("U", 2048, [P, 2, 4, 256])
    DFT = reg("DFT", 4096, [P, 1280])
    NQ = reg("NQ", 0, [P, 4, TOK])
    NK = reg("NK", 2048, [P, 4, TOK])
    NV = reg("NV", 4096, [P, 4, 512])
    BIAS = reg("BIAS", 6144, [P, HEADS, 6, GRID_W])
    RPB = reg("RPB", 10240, [P, HEADS, RPB_RUN])
    Q96 = reg("Q96", 0, [P, HEADS, TOK])
    K96 = reg("K96", 4096, [P, HEADS, TOK])
    MV = reg("MV", 8192, [P, 4, 512])
    SQ3 = reg("SQ3", 8192, [P, 3, TOK])
    RT = reg("RT", 9728, [P, 2, TOK])
    CQ = reg("CQ", 11264, [P, 2, TOK])
    CKV = reg("CKV", 12288, [P, TOK])
    KR = reg("KR", 12800, [P, TOK])
    ROPET = reg("ROPET", 10240, [P, 2, 256])
    PR = reg("PR", 10240, [P, 2, TOK])
    PTS = reg("PTS", 11264, [P, 2, 4, 256])
    GATE = reg("GATE", 11264, [P, 4, TOK])
    HH = reg("HH", 0, [P, KT, TOK], F32R)
    HL = reg("HL", 4096, [P, KT, TOK], F32R)
    SG = reg("SG", 8192, [P, 2, TOK])
    HT = reg("HT", 9216, [P, 2, TOK])
    S1 = reg("S1", 10240, [P, TOK])
    S2 = reg("S2", 10752, [P, TOK])
    SQ = reg("SQ", 11264, [P, TOK])
    MU = reg("MU", 11776, [P, TOK])
    RSTD = reg("RSTD", 12288, [P, TOK])
    VAR = reg("VAR", 12800, [P, TOK])
    NT = reg("NT", 0, [P, 2, TOK])
    A32 = reg("A32", 1024, [P, 2, TOK])
    XIN = nc.alloc_sbuf_tensor_at("XIN", [P, 4, D], F32, offset=16512 + 16384 * 5 + 16384 * 3)
    EARLY1, EARLY2, EARLY3 = (sb(f"EARLY{j + 1}", [P, KT, 512], at=at)
                              for j, at in enumerate((AH_AT, AL_AT, YH_AT)))
    VROWS = reg("VROWS", 8192, [P, 4, P])
    GB = reg("GB", 0, [P, KT, SEQ])
    XR = reg("XR", 2048, [P, KT, 260])
    XC = reg("XC", 4128, [P, KT, SEQ])
    LA = reg("LA", 6176, [P, KT, SEQ])
    LT = reg("LT", 8224, [P, KT, SEQ])
    GI = reg("GI", 10272, [P, KT, SEQ])
    PA = reg("PA", 2048, [P, KT, 16 + SEQ])
    PS1 = reg("PS1", 4224, [P, KT, 16 + SEQ])
    PS2 = reg("PS2", 6400, [P, KT, 16 + SEQ])
    PINV = reg("PINV", 8576, [P, 4, SEQ])
    OUTT = reg("OUTT", 2048, [P, KT, SEQ])
    OUTS = reg("OUTS", 4096, [P, 2, D])
    assert offset[0] + 53248 <= 229344, offset[0]

    PS = [stack.enter_context(nc.psum_tensor(f"ps{b}", [P, 512], F32)) for b in range(8)]
    sem = {n: stack.enter_context(nc.semaphore(n)) for names in OWN.values() for n in names}

    Y8H, Y8L = (y[:, :, :].rearrange("p a b -> p (a b)").rearrange("p (k n) -> p k n", k=KT) for y in (YH, YL))
    IDENT = CON[:, C_ID:C_ID + P]
    COS = CON[64:96, C_COS:C_COS + SEQ]
    SIN = CON[64:96, C_SIN:C_SIN + SEQ]
    W96 = SIDE[:, 0:3, :].rearrange("p a b -> p (a b)").rearrange("p (k h c) -> p k h c", k=2, h=HEADS)
    WUK = SIDE[:, 3, :]
    WUV = SIDE[:, 4, :]

    place, tile_, row_ = {}, 0, 0
    for name, n in VECTORS:
        if row_ + n > P:
            tile_, row_ = tile_ + 1, 0
        place[name] = (tile_, row_)
        row_ += n

    def vec(name, i, n=1):
        t, r = place[name]
        return VEC[:, t, r + i:r + i + n]

    def mod(mat, chunk, v, k=None):
        if k is None:
            return MODT[:, mat, 8 * chunk:8 * chunk + 8, v]
        return MODT[:, mat, 8 * chunk + k, v:v + 1]

    wmod = [A["w_mod"][0], A["w_mod"][1], A["w_mod_2"][0], A["w_mod_2"][1]]
    bmod = [("b_mod", 0), ("b_mod", 48), ("b_mod_2", 0), ("b_mod_2", 48)]

    def rows(w):
        return w.rearrange("(k p) n -> p k n", p=P)

    class Side:

        def __init__(self, mat, chunk, per_turn=0):
            self.mat, self.chunk, self.per_turn = mat, chunk, per_turn

        def at(self, K):
            return self.chunk if not self.per_turn or K.turn is None else K.turn * self.per_turn + self.chunk

        def sp(self, e, K, j):
            if K.s("side_rows") + j:
                e.wait_ge(sem["side_rows"], K.at("side_rows", j))
            if K.s("qkv_done"):
                e.wait_ge(sem["qkv_done"], K.at("qkv_done"))
            src = rows(wmod[self.mat])
            c = self.at(K)
            dyn = K.turn is not None and self.per_turn
            s = src[:, :, bass.ds(c * 512, 512)] if dyn else src[:, :, c * 512:(c + 1) * 512]
            e.dma_start(SIDE[:, :, :], s).then_inc(K.up("side_loaded", 16), 16)

        def pe_rows(self, e, K, j):
            e.wait_ge(sem["side_loaded"], K.at("side_loaded", 16 * (j + 1)))
            if K.s("side_added") + j:
                e.wait_ge(sem["side_added"], K.at("side_added", j))
            for b in (4, 5):
                reader, count = K.bank[b]
                e.wait_ge(sem[reader], K.value(reader, count))
            for k in range(KT):
                g = k % 4
                ins = e.matmul(PS[4][32 * g:32 * g + 32, :], CC[:, k, :], SIDE[:, k, :], start=k < 4, stop=k >= 4)
            ins.then_inc(K.up("side_rows"), 1)

        def act(self, e, K, j):
            e.wait_ge(sem["side_rows"], K.at("side_rows", j + 1))
            e.activation(MODROW[:, :], PS[4][:, :], ACT.Copy).then_inc(K.up("side_row_copied"), 1)

        def pe_turn(self, e, K, j):
            e.wait_ge(sem["side_row_copied"], K.at("side_row_copied", j + 1))
            for q in range(4):
                ins = e.matmul(PS[5][:, 3 * q:3 * q + 3], MODROW[:, q * P:(q + 1) * P], CON[:, C_SEL:C_SEL + 3],
                               start=True, stop=True)
            ins.then_inc(K.up("side_turned"), 1)
            for b in (4, 5):
                K.bank[b] = ("side_added", K.s("side_added") + j + 1)

        def dve(self, e, K, j):
            e.wait_ge(sem["side_turned"], K.at("side_turned", j + 1))
            c = self.at(K)
            name, first = bmod[self.mat]
            t, r = place[name]
            dyn = K.turn is not None and self.per_turn
            dst = MODT[:, self.mat, bass.ds(4 * c, 4), :] if dyn else MODT[:, self.mat, 4 * c:4 * c + 4, :]
            bias = VEC[:, t, bass.ds(4 * c + (r + first), 4)] if dyn else VEC[:, t, r + first + 4 * c:r + first + 4 * c + 4]
            ps = PS[5][:, 0:12].rearrange("p (q v) -> p q v", v=3)
            e.tensor_tensor(dst, ps, bias.unsqueeze(2).to_broadcast([P, 4, 3]), ALU.add) \
                .then_inc(K.up("side_added"), 1)

    class Unit:

        kt = KT
        func = ACT.Copy
        offs = (0, P, 0, P)
        read = "aaaa"
        rhs = (AH, AL)
        tokens = (0, TOK)
        nxt = None
        loaded = False
        ready = None
        hold = False

        def __init__(self, w=None, cols=None, tokens=None, offs=None, rhs=None, rhs_count=KT, side=None, ready=None,
                     dst=None, func=None, scale=1.0, layer=0, col=0, h0=0, krow=0, kt=None, per_turn=0, tile0=0, b=0,
                     half=0, u=0, first=True, stats=None, mean=True, bias=None, prep=None,
                     by_k=False, late=0):
            self.w, self.cols, self.rhs_count, self.side, self.dst, self.scale = w, cols, rhs_count, side, dst, scale
            self.layer, self.col, self.h0, self.krow, self.per_turn, self.tile0 = layer, col, h0, krow, per_turn, tile0
            self.b, self.half, self.u, self.first, self.mean, self.bias, self.prep = b, half, u, first, mean, bias, prep
            self.tokens = tokens or self.tokens
            self.offs = offs or self.offs
            self.rhs = rhs or self.rhs
            self.ready = ready or self.ready
            self.func = func or self.func
            self.kt = kt or self.kt
            self.by_k, self.late = by_k, late
            if stats is not None:
                self.stats = stats

        def wide(self, m):
            return self.tokens

        def sp(self, e, K):
            if not self.loaded:
                self.load(e, K)
            if self.side:
                self.side.sp(e, K, 0)

        def load(self, e, K):
            for p in range(2):
                if K.s("products"):
                    e.wait_ge(sem["weight_low"], K.at("weight_low", 2 * p - 6))
                e.dma_start(RAW[p][:, 0:self.kt, :], self.src(K, p)).then_inc(K.up(f"pair{p}_loaded", 16), 16)

        def split_act(self, e, K, m, loads):
            p = m // 2
            e.wait_ge(sem[f"pair{p}_loaded"], K.at(f"pair{p}_loaded", 16 * loads))
            kt, o = self.kt, self.offs[m]
            e.activation(SH[:, m, 0:kt, :], RAW[p][:, 0:kt, o:o + P], ACT.Copy).then_inc(K.up("weight_high"), 1)

        def split_dve(self, e, K, m):
            p = m // 2
            e.wait_ge(sem["weight_high"], K.at("weight_high", m + 1))
            kt, o = self.kt, self.offs[m]
            e.tensor_tensor(SL[:, m, 0:kt, :], RAW[p][:, 0:kt, o:o + P], SH[:, m, 0:kt, :].bitcast(F32),
                            ALU.subtract).then_inc(K.up("weight_low"), 1)

        def order(self):
            first = 4 if self.by_k else 2 if self.late else 0
            early = 0 if self.by_k else self.kt - self.late
            steps = [(m, k) for m in range(first) for k in range(early)]
            if self.by_k:
                steps += [(m, k) for k in range(early, self.kt) for m in range(first)]
            else:
                steps += [(m, k) for m in range(first) for k in range(early, self.kt)]
            return steps + [(m, k) for m in range(first, 4) for k in range(self.kt)]

        def pe(self, e, K):
            waited = -1
            if self.side and self.by_k:
                self.side.pe_rows(e, K, 0)
            for m, k in self.order():
                if self.side and (m, k) == (3, 0) and not self.by_k:
                    self.side.pe_rows(e, K, 0)
                c0, c1 = self.wide(m)
                ps = PS[m][:, 0:c1 - c0]
                xh, xl = self.moving(m, k, c0, c1)
                if k == 0:
                    e.wait_ge(sem["weight_low"], K.at("weight_low", m - 3))
                    reader, count = K.bank[m]
                    e.wait_ge(sem[reader], K.value(reader, count))
                part = self.part(m, k)
                if part > waited and self.ready:
                    producer, per_k = self.ready
                    e.wait_ge(sem[producer], K.at(producer, part + 1 - self.rhs_count if per_k else 0))
                    waited = part
                e.matmul(ps, SH[:, m, k, :], xh, start=k == 0, stop=False)
                e.matmul(ps, SH[:, m, k, :], xl, start=False, stop=False)
                ins = e.matmul(ps, SL[:, m, k, :], xh, start=False, stop=k == self.kt - 1)
                if k == self.kt - 1:
                    ins.then_inc(K.up("products"), 1)
            if self.side:
                self.side.pe_turn(e, K, 0)
            fa, fd = K.s("act_read"), K.s("dve_read")
            for m in range(4):
                if self.read[m] == "a":
                    fa += 1
                    K.bank[m] = ("act_read", fa)
                else:
                    fd += 1
                    K.bank[m] = ("dve_read", fd)

        def part(self, m, k):
            return k

        def moving(self, m, k, c0, c1):
            return self.rhs[0][:, k, c0:c1], self.rhs[1][:, k, c0:c1]

        def freed(self, m):
            return 4 if self.hold else m + 1

        def act(self, e, K):
            for m in range(4):
                if self.side and m == (0 if self.by_k or self.hold else 3):
                    self.side.act(e, K, 0)
                e.wait_ge(sem["products"], K.at("products", self.freed(m)))
                if self.nxt:
                    self.nxt.split_act(e, K, m, 1 if self.loaded else 2)
                self.read_act(e, K, m)

        def dve(self, e, K):
            for m in range(4):
                if self.nxt:
                    self.nxt.split_dve(e, K, m)
                e.wait_ge(sem["products"], K.at("products", m + 1))
                self.read_dve(e, K, m)
                if m == 3 and self.side:
                    self.side.dve(e, K, 0)

        def pool(self, e, K):
            pass

        def read_act(self, e, K, m):
            pass

        def read_dve(self, e, K, m):
            pass

    class First:

        def __init__(self, unit):
            self.unit = unit
            unit.loaded = True

        def sp(self, e, K):
            self.unit.load(e, K)

        def pe(self, e, K):
            pass

        pool = pe

        def act(self, e, K):
            for m in range(4):
                self.unit.split_act(e, K, m, 1)

        def dve(self, e, K):
            for m in range(4):
                self.unit.split_dve(e, K, m)

    class Columns(Unit):

        def src(self, K, p):
            c = self.cols[p]
            if self.per_turn and K.turn is not None:
                return rows(self.w)[:, self.krow:self.krow + self.kt, bass.ds(K.turn * self.per_turn + c, 256)]
            return rows(self.w)[:, self.krow:self.krow + self.kt, c:c + 256]

    class Copied(Columns):

        read = "aaaa"

        def read_act(self, e, K, m):
            c0, c1 = self.wide(m)
            e.activation(self.dst(m), PS[m][:, 0:c1 - c0], self.func, scale=self.scale).then_inc(K.up("act_read"), 1)

    class Compressed(Copied):

        def wide(self, m):
            return self.tokens if m < 2 else (0, TOK)

    class Gelu(Copied):
        def read_act(self, e, K, m):
            i = self.tile0 + m
            e.activation(GB[:, i, :], PS[m][:, 0:SEQ], ACT.Gelu_apprx_tanh, bias=vec("lru_b_y_2", i)) \
                .then_inc(K.up("act_read"), 1)

    class Values(Columns):

        read = "aaaa"
        hold = True

        def pe(self, e, K):
            for m in range(4):
                e.wait_ge(sem["weight_low"], K.at("weight_low", m - 3))
            for t in range(4):
                if t == 2 and self.side:
                    self.side.pe_rows(e, K, 0)
                reader, count = K.bank[t]
                e.wait_ge(sem[reader], K.value(reader, count))
                for k in range(KT):
                    xh, xl = (a[:, k, t * P:(t + 1) * P] for a in (AH, AL))
                    e.matmul(PS[t][:, :], xh, SH[:, :, k, :], start=k == 0, stop=False)
                    e.matmul(PS[t][:, :], xh, SL[:, :, k, :], start=False, stop=False)
                    ins = e.matmul(PS[t][:, :], xl, SH[:, :, k, :], start=False, stop=k == KT - 1)
                ins.then_inc(K.up("products"), 1)
                K.bank[t] = ("act_read", K.s("act_read") + t + 1)
            if self.side:
                self.side.pe_turn(e, K, 0)

        def act(self, e, K):
            if self.side:
                self.side.act(e, K, 0)
            for m in range(4):
                e.wait_ge(sem["products"], K.at("products", m + 1))
                self.read_act(e, K, m)
            for m in range(4):
                self.nxt.split_act(e, K, m, 2)

        def read_act(self, e, K, m):
            e.activation(NV[:, m, :], PS[m][:, :], ACT.Copy).then_inc(K.up("act_read"), 1)

    class Branch(Columns):

        kt = 4
        read = "dddd"
        rhs = (YH, YL)

        def read_dve(self, e, K, m):
            c0, c1 = self.tokens
            i = self.half * 4 + m
            acc, gate, ps = MACC[:, i, c0:c1], GATE[:, m, c0:c1], PS[m][:, 0:c1 - c0]
            e.wait_ge(sem["act_read"], K.at("act_read", -4 + m + 1))
            if self.b == 0:
                e.tensor_tensor(acc, ps, gate, ALU.mult).then_inc(K.up("dve_read"), 1)
                return
            tmp = HT[:, m % 2, c0:c1]
            e.tensor_tensor(tmp, ps, gate, ALU.mult).then_inc(K.up("dve_read"), 1)
            e.wait_ge(sem["dve_read"], K.own("dve_read"))
            e.tensor_tensor(acc, acc, tmp, ALU.add).then_inc(K.up("dve_done"), 1)
            e.wait_ge(sem["dve_done"], K.own("dve_done"))
            if self.b == 2:
                e.tensor_copy(HH[:, i, c0:c1], acc).then_inc(K.up("dve_done"), 1)
                e.wait_ge(sem["dve_done"], K.own("dve_done"))
                e.tensor_tensor(HL[:, i, c0:c1], acc, HH[:, i, c0:c1].bitcast(F32), ALU.subtract) \
                    .then_inc(K.up("hidden_low"), 1)

    def stats_pool(e, K, first, tiles, c0, c1, mean, ready):
        for n, k in enumerate(tiles):
            e.wait_ge(sem[ready], K.at(ready, n + 1))
            z = X[:, k, c0:c1]
            if first and n == 0:
                e.tensor_tensor(S2[:, c0:c1], z, z, ALU.mult).then_inc(K.up("pool_done"), 1)
                e.wait_ge(sem["pool_done"], K.own("pool_done"))
            else:
                if mean:
                    before = X[:, 0, c0:c1] if first and n == 1 else S1[:, c0:c1]
                    e.tensor_tensor(S1[:, c0:c1], before, z, ALU.add).then_inc(K.up("pool_done"), 1)
                e.tensor_tensor(SQ[:, c0:c1], z, z, ALU.mult).then_inc(K.up("pool_done"), 1)
                e.wait_ge(sem["pool_done"], K.own("pool_done"))
                e.tensor_tensor(S2[:, c0:c1], S2[:, c0:c1], SQ[:, c0:c1], ALU.add).then_inc(K.up("pool_done"), 1)
                e.wait_ge(sem["pool_done"], K.own("pool_done"))

    class Residual(Columns):

        read = "dddd"
        stats = True

        def read_dve(self, e, K, m):
            i = self.tile0 + m
            c0, c1 = self.tokens
            if self.bias:
                tmp = HT[:, m % 2, 0:SEQ]
                e.tensor_scalar(tmp, PS[m][:, 0:SEQ], vec(self.bias, i), self.scale(0, i), ALU.add, ALU.mult) \
                    .then_inc(K.up("dve_done"), 1)
                e.wait_ge(sem["dve_done"], K.own("dve_done"))
                e.tensor_tensor(X[:, i, 0:SEQ], X[:, i, 0:SEQ], tmp, ALU.add).then_inc(K.up("dve_read"), 1)
                return
            for s, c in enumerate(range(c0, c1, SEQ)):
                ins = e.scalar_tensor_tensor(out=X[:, i, c:c + SEQ], in0=PS[m][:, c:c + SEQ], scalar=self.scale(s, i),
                                             in1=X[:, i, c:c + SEQ], op0=ALU.mult, op1=ALU.add)
                ins.then_inc(K.up("dve_read" if c + SEQ == c1 else "dve_done"), 1)

        def dve(self, e, K):
            if self.first and self.stats and K.turn is not None:
                e.wait_ge(sem["pool_done"], K.at("pool_done"))
            if self.prep:
                self.prep(e, K)
            super().dve(e, K)

        def pool(self, e, K):
            if self.stats:
                c0, c1 = self.tokens
                stats_pool(e, K, self.first, range(self.tile0, min(self.tile0 + 4, KT - 1)), c0, c1, self.mean,
                           "dve_read")

    class UpGated(Columns):

        read = "aadd"

        def src(self, K, p):
            w = rows(A["w_ffn_gate" if p == 0 else "w_ffn_up"][self.layer])
            if self.per_turn and K.turn is not None:
                return w[:, :, bass.ds(K.turn * self.per_turn + self.col, 256)]
            return w[:, :, self.col:self.col + 256]

        def read_act(self, e, K, m):
            if m < 2:
                c0, c1 = self.tokens
                e.wait_ge(sem["dve_read"], K.at("dve_read", m - 1))
                e.activation(SG[:, m, c0:c1], PS[m][:, 0:c1 - c0], ACT.Silu).then_inc(K.up("act_read"), 1)

        def read_dve(self, e, K, m):
            if m < 2:
                return
            c0, c1 = self.tokens
            j = m - 2
            h = self.h0 + j
            e.wait_ge(sem["act_read"], K.at("act_read", j + 1))
            e.tensor_tensor(HT[:, j, c0:c1], PS[m][:, 0:c1 - c0], SG[:, j, c0:c1], ALU.mult) \
                .then_inc(K.up("dve_read"), 1)
            e.wait_ge(sem["dve_read"], K.own("dve_read"))
            e.tensor_copy(HH[:, h, c0:c1], HT[:, j, c0:c1]).then_inc(K.up("dve_done"), 1)
            e.wait_ge(sem["dve_done"], K.own("dve_done"))
            e.tensor_tensor(HL[:, h, c0:c1], HT[:, j, c0:c1], HH[:, h, c0:c1].bitcast(F32), ALU.subtract) \
                .then_inc(K.up("hidden_low"), 1)
            e.wait_ge(sem["hidden_low"], K.own("hidden_low"))

    class UpSquared(Columns):

        read = "dddd"
        tokens = (0, SEQ)

        def read_act(self, e, K, m):
            e.activation(SG4[:, m, :], PS[m][:, 0:SEQ], ACT.Relu).then_inc(K.up("act_read"), 1)

        def read_dve(self, e, K, m):
            h = self.h0 + m
            e.wait_ge(sem["act_read"], K.at("act_read", m + 1))
            ht = HT4[:, m, :]
            e.scalar_tensor_tensor(out=ht, in0=PS[m][:, 0:SEQ], scalar=0.0, in1=SG4[:, m, :], op0=ALU.max,
                                   op1=ALU.mult).then_inc(K.up("dve_read"), 1)
            e.wait_ge(sem["dve_read"], K.own("dve_read"))
            e.tensor_copy(HH[:, h, 0:SEQ], ht).then_inc(K.up("dve_done"), 1)
            e.wait_ge(sem["dve_done"], K.own("dve_done"))
            e.tensor_tensor(HL[:, h, 0:SEQ], ht, HH[:, h, 0:SEQ].bitcast(F32), ALU.subtract) \
                .then_inc(K.up("hidden_low"), 1)

    SG4 = SG[:, :, :].rearrange("p a b -> p (a b)").rearrange("p (m n) -> p m n", n=SEQ)
    HT4 = HT[:, :, :].rearrange("p a b -> p (a b)").rearrange("p (m n) -> p m n", n=SEQ)

    class Down(Residual):

        rhs = (HH, HL)
        stats = False
        ready = ("hidden_low", True)

        def src(self, K, p):
            w, c = rows(self.w), self.cols[p]
            if self.per_turn and K.turn is not None:
                return w[:, bass.ds(K.turn * self.per_turn + self.krow, self.kt), c:c + 256]
            return w[:, self.krow:self.krow + self.kt, c:c + 256]

    class Norm:

        def __init__(self, tokens=(0, TOK), mean=True, write_x=True, to="a", eps=LN_EPS, stats=False, prep=None,
                     g=None, b=None, sc=None, sh=None, split=False,
                     summed=False):
            self.tokens, self.mean, self.write_x, self.to, self.eps = tokens, mean, write_x, to, eps
            self.stats = stats
            self.summed = summed
            self.prep, self.g, self.b, self.sc, self.sh = prep, g, b, sc, sh
            self.split = split

        def sp(self, e, K):
            pass

        def pe(self, e, K):
            if self.summed:
                K.bank[6] = ("var_done", K.s("var_done") + 1)
            elif not self.split:
                self.pe_sums(e, K)
            if self.stats:
                c0, c1 = self.tokens
                reader, count = K.bank[6]
                e.wait_ge(sem[reader], K.value(reader, count))
                for k in range(KT):
                    e.wait_ge(sem["normed_squared"], K.at("normed_squared", k + 1))
                    e.matmul(PS[6][:, 0:c1 - c0], ONES[:, :], A32[:, k % 2, c0:c1], start=k == 0, stop=k == KT - 1) \
                        .then_inc(K.up("squares_added"), 1)

        def pe_sums(self, e, K):
            c0, c1 = self.tokens
            if K.s("pool_done"):
                e.wait_ge(sem["pool_done"], K.at("pool_done"))
            else:
                e.wait_ge(sem["dve_done"], K.at("dve_done"))
            for b in (4, 5):
                reader, count = K.bank[b]
                e.wait_ge(sem[reader], K.value(reader, count))
            n, whole = c1 - c0, self.split
            if self.mean:
                e.matmul(PS[4][:, 0:n], ONES[:, :], S1[:, c0:c1], start=True, stop=whole)
            ins = e.matmul(PS[5][:, 0:n], ONES[:, :], S2[:, c0:c1], start=True, stop=whole)
            if not whole:
                e.wait_ge(sem["last_squared"], K.at("last_squared", 1))
                if self.mean:
                    e.matmul(PS[4][:, 0:n], ONES[:, :], X[:, KT - 1, c0:c1], start=False, stop=True)
                ins = e.matmul(PS[5][:, 0:n], ONES[:, :], NT[:, 1, c0:c1], start=False, stop=True)
            ins.then_inc(K.up("sums_done"), 1)
            for b in (4, 5):
                K.bank[b] = ("var_done", K.s("var_done") + 1)

        def dve_spread(self, e, K):
            c0, c1 = self.tokens
            n = c1 - c0
            if self.summed:
                e.wait_ge(sem["squares_added"], K.at("squares_added"))
            else:
                e.wait_ge(sem["sums_done"], K.at("sums_done", 1))
            var = VAR[:, c0:c1]
            if self.mean:
                e.tensor_scalar(MU[:, c0:c1], PS[4][:, 0:n], 1.0 / D, None, ALU.mult).then_inc(K.up("dve_done"), 1)
                e.wait_ge(sem["dve_done"], K.own("dve_done"))
                e.tensor_tensor(var, MU[:, c0:c1], MU[:, c0:c1], ALU.mult).then_inc(K.up("dve_done"), 1)
                e.wait_ge(sem["dve_done"], K.own("dve_done"))
                e.scalar_tensor_tensor(out=var, in0=PS[5][:, 0:n], scalar=1.0 / D, in1=var, op0=ALU.mult,
                                       op1=ALU.subtract).then_inc(K.up("dve_done"), 1)
                e.wait_ge(sem["dve_done"], K.own("dve_done"))
                e.tensor_scalar(var, var, 0.0, self.eps, ALU.max, ALU.add).then_inc(K.up("var_done"), 1)
            else:
                sums = PS[6 if self.summed else 5]
                e.tensor_scalar(var, sums[:, 0:n], 1.0 / D, self.eps, ALU.mult, ALU.add).then_inc(K.up("var_done"), 1)
            if self.mean and not self.split:
                for k in range(2):
                    e.tensor_tensor(NT[:, k, c0:c1], X[:, k, c0:c1], MU[:, c0:c1], ALU.subtract) \
                        .then_inc(K.up("dve_done"), 1)
            e.wait_ge(sem["root_done"], K.at("root_done", 1))
            e.reciprocal(RSTD[:, c0:c1], var).then_inc(K.up("dve_done"), 1)

        def dve(self, e, K):
            c0, c1 = self.tokens
            if self.prep:
                self.prep(e, K)
            if not self.split:
                self.dve_spread(e, K)
            e.wait_ge(sem["dve_done"], K.own("dve_done"))

            def centre(k):
                t = NT[:, k % 2, c0:c1]
                if k >= 2:
                    r = "x_normed" if self.write_x or self.to != "a" else "modulated"
                    e.wait_ge(sem[r], K.at(r, k - 1))
                if self.mean:
                    if k >= 2 or self.split:
                        e.tensor_tensor(t, X[:, k, c0:c1], MU[:, c0:c1], ALU.subtract).then_inc(K.up("dve_done"), 1)
                        e.wait_ge(sem["dve_done"], K.own("dve_done"))
                    e.tensor_tensor(t, t, RSTD[:, c0:c1], ALU.mult).then_inc(K.up("centred"), 1)
                else:
                    e.tensor_tensor(t, X[:, k, c0:c1], RSTD[:, c0:c1], ALU.mult).then_inc(K.up("centred"), 1)

            centre(0)
            for k in range(KT):
                if k + 1 < KT:
                    centre(k + 1)
                if self.to == "a":
                    e.wait_ge(sem["modulated"], K.at("modulated", k + 1))
                    a = A32[:, k % 2, c0:c1]
                    e.tensor_copy(AH[:, k, c0:c1], a).then_inc(K.up("dve_done"), 1)
                    e.wait_ge(sem["dve_done"], K.own("dve_done"))
                    e.tensor_tensor(AL[:, k, c0:c1], a, AH[:, k, c0:c1].bitcast(F32), ALU.subtract) \
                        .then_inc(K.up("input_low"), 1)

        def act_root(self, e, K):
            c0, c1 = self.tokens
            if not self.split and not self.summed:
                e.wait_ge(sem["dve_read"], K.at("dve_read"))
                e.activation(NT[:, 1, c0:c1], X[:, KT - 1, c0:c1], ACT.Square).then_inc(K.up("last_squared"), 1)
            e.activation(SM[:, 8:9], ONES[:, 0:1], ACT.Sqrt).then_inc(K.up("act_done"), 1)
            e.wait_ge(sem["var_done"], K.at("var_done", 1))
            e.activation(VAR[:, c0:c1], VAR[:, c0:c1], ACT.Sqrt).then_inc(K.up("root_done"), 1)

        def act(self, e, K):
            c0, c1 = self.tokens
            if not self.split:
                self.act_root(e, K)
            for k in range(KT):
                e.wait_ge(sem["centred"], K.at("centred", k + 1))
                t = NT[:, k % 2, c0:c1]
                if self.write_x:
                    e.activation(X[:, k, c0:c1], t, ACT.Identity, bias=self.b(k), scale=self.g(k)) \
                        .then_inc(K.up("x_normed"), 1)
                if self.stats:
                    if k >= 2:
                        e.wait_ge(sem["squares_added"], K.at("squares_added", k - 1))
                    e.wait_ge(sem["x_normed"], K.own("x_normed"))
                    e.activation(A32[:, k % 2, c0:c1], X[:, k, c0:c1], ACT.Square).then_inc(K.up("normed_squared"), 1)
                if self.to == "a":
                    if k >= 2:
                        e.wait_ge(sem["input_low"], K.at("input_low", k - 1))
                    src = t
                    if self.write_x:
                        e.wait_ge(sem["x_normed"], K.own("x_normed"))
                        src = X[:, k, c0:c1]
                    for s, c in enumerate(range(c0, c1, SEQ)):
                        last = c + SEQ == c1
                        at = c - c0
                        e.activation(A32[:, k % 2, c:c + SEQ], src[:, at:at + SEQ], ACT.Identity,
                                     bias=self.sh(s, k), scale=self.sc(s, k)) \
                            .then_inc(K.up("modulated" if last else "act_done"), 1)
                if self.to == "pool":
                    e.activation(PA[:, k, 16:16 + SEQ], t, ACT.Identity, bias=self.sh(0, k), scale=self.sc(0, k)) \
                        .then_inc(K.up("x_normed"), 1)
                if self.to == "out":
                    e.activation(OUTT[:, k, :], t, ACT.Copy, scale=self.g(k)).then_inc(K.up("x_normed"), 1)

        def pool(self, e, K):
            pass

    class Spread:

        def __init__(self, norm):
            self.norm = norm

        def sp(self, e, K):
            pass

        pool = sp

        def pe(self, e, K):
            self.norm.pe_sums(e, K)

        def act(self, e, K):
            self.norm.act_root(e, K)

        def dve(self, e, K):
            self.norm.dve_spread(e, K)

    class Load:

        def sp(self, e, K):
            pass

        pe = dve = pool = sp

    class LoadTransform(Load):
        def act(self, e, K):
            e.wait_ge(sem["input_low"], K.at("input_low"))
            if K.s("products"):
                e.wait_ge(sem["products"], K.at("products"))
                e.wait_ge(sem["hidden_low"], K.at("hidden_low"))
            e.dma_start(DFT[:, :], const[:, C_DFT:C_DFT + 1280]).then_inc(K.up("constants_loaded", 16), 16)

    class LoadRpb(Load):

        def __init__(self, layer):
            self.layer = layer

        def act(self, e, K):
            e.wait_ge(sem["dve_read"], K.at("dve_read"))
            e.wait_ge(sem["products"], K.at("products"))
            flat = A["na_rpb"].rearrange("l h a b -> (l h a b)")
            for r in range(2):
                first = flat.offset + self.layer * 3720 + 464 - (10 - r) * 31 - 15 - 63
                src = bass.AP(flat.tensor, first, [[1, GRID_W], [465, HEADS], [1, RPB_RUN]])
                e.dma_start(RPB[64 * r:64 * r + 64, :, :], src).then_inc(K.up("rpb_loaded", 16), 16)

    class LoadLatentWeights(Load):

        def __init__(self, layer):
            self.layer = layer

        def act(self, e, K):
            e.wait_ge(sem["side_rows"], K.at("side_rows"))
            w_uq, w_qr = (A[n][self.layer].rearrange("(k p) (h c) -> p k h c", p=P, h=HEADS) for n in ("w_uq", "w_qr"))
            for k in range(2):
                e.dma_start(W96[:, k, :, 0:64], w_uq[:, k]).then_inc(K.up("latent_w_loaded", 16), 16)
                e.dma_start(W96[:, k, :, 64:96], w_qr[:, k]).then_inc(K.up("latent_w_loaded", 16), 16)
            e.dma_start(WUK, A["w_uk"][self.layer]).then_inc(K.up("latent_w_loaded", 16), 16)
            e.dma_start(WUV, A["w_uv"][self.layer]).then_inc(K.up("latent_w_loaded", 16), 16)

    class LoadWindows(Load):
        def act(self, e, K):
            e.wait_ge(sem["dve_read"], K.at("dve_read"))
            e.wait_ge(sem["products"], K.at("products"))
            e.wait_ge(sem["hidden_low"], K.at("hidden_low"))
            src = const[:, C_POOL:C_ALL].rearrange("p (g n) -> p g n", g=4)
            e.dma_start(PINV[:, :, :], src).then_inc(K.up("constants_loaded", 16), 16)

    class Fourier:

        def __init__(self, streams):
            self.streams = streams

        def sp(self, e, K):
            pass

        pool = sp

        def pe(self, e, K):
            e.wait_ge(sem["act_read"], K.at("act_read", -4))
            e.wait_ge(sem["constants_loaded"], K.at("constants_loaded"))
            for b in (4, 5, 6, 7):
                reader, count = K.bank[b]
                e.wait_ge(sem[reader], K.value(reader, count))
            for s in range(self.streams):
                for tt in range(2):
                    for gp in range(2):
                        b = 2 * tt + gp
                        if s:
                            e.wait_ge(sem["branch_low"], K.at("branch_low", 2 * (s - 1) + 2))
                            e.wait_ge(sem["features_copied"], K.at("features_copied", 4 * s))
                        for g in range(2):
                            ins = e.matmul(PS[4 + b][:, 256 * g:256 * g + 256],
                                           FT[:, 2 * gp + g, s * SEQ + tt * P:s * SEQ + tt * P + P],
                                           DFT[:, 0:256], start=True, stop=True)
                        ins.then_inc(K.up("features_done"), 1)
                for gp in range(2):
                    e.wait_ge(sem["features_copied"], K.at("features_copied", 4 * s + 4))
                    for g in range(2):
                        for tt in range(2):
                            u = U[:, tt, 2 * gp + g, :]
                            y = PS[4 + gp][:, 256 * g:256 * g + 256]
                            e.matmul(y, u[:, 0:P], DFT[:, 256 + tt * SEQ:256 + (tt + 1) * SEQ], start=tt == 0, stop=False)
                            ins = e.matmul(y, u[:, P:2 * P], DFT[:, 768 + tt * SEQ:768 + (tt + 1) * SEQ],
                                           start=False, stop=tt == 1)
                    ins.then_inc(K.up("tokens_done"), 1)
            for b in (4, 5):
                K.bank[b] = ("branch_low", K.s("branch_low") + 2 * self.streams)
            for b in (6, 7):
                K.bank[b] = ("features_copied", K.s("features_copied") + 4 * self.streams)

        def act(self, e, K):
            for s in range(self.streams):
                for tt in range(2):
                    for gp in range(2):
                        n = 4 * s + 2 * tt + gp
                        e.wait_ge(sem["features_done"], K.at("features_done", n + 1))
                        if s:
                            e.wait_ge(sem["tokens_done"], K.at("tokens_done", 2 * s))
                        e.activation(U[:, tt, 2 * gp:2 * gp + 2, :], PS[4 + 2 * tt + gp][:, :].rearrange(
                      "p (g n) -> p g n", g=2), ACT.Copy).then_inc(K.up("features_copied"), 1)
                for gp in range(2):
                    e.wait_ge(sem["tokens_done"], K.at("tokens_done", 2 * s + gp + 1))
                    e.activation(YH[:, 2 * gp:2 * gp + 2, s * SEQ:(s + 1) * SEQ],
                                 PS[4 + gp][:, :].rearrange("p (g n) -> p g n", g=2), ACT.Copy) \
                        .then_inc(K.up("branch_high"), 1)

        def dve(self, e, K):
            for s in range(self.streams):
                for gp in range(2):
                    e.wait_ge(sem["branch_high"], K.at("branch_high", 2 * s + gp + 1))
                    y = slice(2 * gp, 2 * gp + 2), slice(s * SEQ, (s + 1) * SEQ)
                    e.tensor_tensor(YL[:, y[0], y[1]], PS[4 + gp][:, :].rearrange("p (g n) -> p g n", g=2),
                                    YH[:, y[0], y[1]].bitcast(F32), ALU.subtract).then_inc(K.up("branch_low"), 1)

    class Bias:

        def sp(self, e, K):
            pass

        pe = act = pool = sp

        def dve(self, e, K):
            e.wait_ge(sem["rpb_loaded"], K.at("rpb_loaded"))
            e.wait_ge(sem["act_read"], K.at("act_read"))
            for h in range(HEADS):
                base = RPB[:, h, 0:RPB_RUN]
                skew = bass.AP(base.tensor, base.offset + RPB_RUN - 1, [list(base.ap[0]), [-31, 6], [-1, GRID_W]])
                win = CON[:, C_WIN:C_WIN + GRID_W].unsqueeze(1).to_broadcast([P, 6, GRID_W])
                e.tensor_tensor(BIAS[:, h, :, :], skew, win, ALU.min).then_inc(K.up("bias_done"), 1)

    class Attention:

        def __init__(self, kind, streams):
            self.kind = kind
            self.steps = [(s, h, qt) for s in range(streams) for h in range(HEADS) for qt in range(2)]

        def sp(self, e, K):
            pass

        pool = sp

        def keys(self, s):
            return (0, TOK) if s == 0 else (SEQ, TOK)

        def qk(self, s, h, qt):
            c0, c1 = self.keys(s)
            q0 = s * SEQ + qt * P
            if self.kind == "na":
                b = 64 * (h % 2)
                return NQ[b:b + 64, h // 2, q0:q0 + P], NK[b:b + 64, h // 2, c0:c1]
            return Q96[0:96, h, q0:q0 + P], K96[0:96, h, c0:c1]

        def pe(self, e, K):
            V = NV if self.kind == "na" else MV
            e.wait_ge(sem["act_read"], K.at("act_read"))
            if self.kind == "mla":
                e.wait_ge(sem["queries_copied"], K.at("queries_copied"))
                e.wait_ge(sem["rotated_done"], K.at("rotated_done"))
                e.wait_ge(sem["keys_copied"], K.at("keys_copied"))
            for b in (4, 5, 6, 7):
                reader, count = K.bank[b]
                e.wait_ge(sem[reader], K.value(reader, count))
            n_steps = len(self.steps)

            def scores(n):
                s, h, qt = self.steps[n]
                if n >= 2:
                    e.wait_ge(sem["exp_done"], K.at("exp_done", n - 1))
                q, k = self.qk(s, h, qt)
                c0, c1 = self.keys(s)
                e.matmul(PS[6 + n % 2][:, 0:c1 - c0], q, k, start=True, stop=True).then_inc(K.up("scores_done"), 1)

            def turn(n):
                s, h, qt = self.steps[n]
                c0, c1 = self.keys(s)
                e.wait_ge(sem["probs_ready"], K.at("probs_ready", n + 1))
                if n:
                    e.wait_ge(sem["turned_copied"], K.at("turned_copied", n))
                for j in range((c1 - c0) // P):
                    ins = e.transpose(PS[5][:, j * P:(j + 1) * P], PR[:, n % 2, j * P:(j + 1) * P], IDENT)
                ins.then_inc(K.up("probs_turned"), 1)

            def values(g):
                s, h, _ = self.steps[2 * g]
                c0, c1 = self.keys(s)
                e.wait_ge(sem["turned_copied"], K.at("turned_copied", 2 * g + 2))
                pair = g // 2
                if h % 2 == 0 and pair >= 2:
                    e.wait_ge(sem["branch_low"], K.at("branch_low", pair - 1))
                o = PS[4][64 * (h % 2):64 * (h % 2) + 64, 256 * (pair % 2):256 * (pair % 2) + 256]
                tiles = (c1 - c0) // P
                for j in range(tiles):
                    ins = e.matmul(o, V[:, c0 // P + j, 64 * h:64 * h + 64], PTS[:, g % 2, j, :], start=j == 0,
                                   stop=j == tiles - 1)
                ins.then_inc(K.up("values_done"), 1)

            scores(0)
            scores(1)
            for n in range(n_steps):
                if n + 2 < n_steps:
                    scores(n + 2)
                turn(n)
                if n >= 2 and n % 2 == 0:
                    values(n // 2 - 1)
            values(n_steps // 2 - 1)
            K.bank[4] = ("branch_low", K.s("branch_low") + n_steps // 4)
            K.bank[5] = ("turned_copied", K.s("turned_copied") + n_steps)
            K.bank[6] = K.bank[7] = ("exp_done", K.s("exp_done") + n_steps)

        def outputs(self, pair):
            s = self.steps[4 * pair][0]
            return pair % 4, slice(s * SEQ, (s + 1) * SEQ), slice(256 * (pair % 2), 256 * (pair % 2) + 256)

        def act(self, e, K):
            n_steps = len(self.steps)

            def exp(n):
                s, h, qt = self.steps[n]
                c0, c1 = self.keys(s)
                e.wait_ge(sem["max_done"], K.at("max_done", n + 1))
                if n >= 2:
                    e.wait_ge(sem["probs_turned"], K.at("probs_turned", n - 1))
                e.activation(PR[:, n % 2, 0:c1 - c0], PS[6 + n % 2][:, 0:c1 - c0], ACT.Exp,
                             bias=SM[:, n % 2:n % 2 + 1], accum_out=SM[:, 2 + n % 2:3 + n % 2]) \
                    .then_inc(K.up("exp_done"), 1)

            def turned(n):
                s, h, qt = self.steps[n]
                c0, c1 = self.keys(s)
                g, w = n // 2, c1 - c0
                e.wait_ge(sem["probs_turned"], K.at("probs_turned", n + 1))
                if g >= 2:
                    e.wait_ge(sem["values_done"], K.at("values_done", g - 1))
                e.activation(PTS[:, g % 2, 0:w // P, qt * P:(qt + 1) * P],
                             PS[5][:, 0:w].rearrange("p (j q) -> p j q", q=P), ACT.Copy).then_inc(K.up("turned_copied"), 1)

            def out(pair):
                t, tok, cols = self.outputs(pair)
                e.wait_ge(sem["values_done"], K.at("values_done", 2 * pair + 2))
                e.activation(YH[:, t, tok], PS[4][:, cols], ACT.Copy).then_inc(K.up("branch_high"), 1)

            for n in range(n_steps + 1):
                if n < n_steps:
                    exp(n)
                if n >= 1:
                    turned(n - 1)
                if n >= 5 and (n - 5) % 4 == 0:
                    out((n - 5) // 4)
            out(n_steps // 4 - 1)

        def dve(self, e, K):
            n_steps = len(self.steps)

            def maximum(n):
                s, h, qt = self.steps[n]
                c0, c1 = self.keys(s)
                e.wait_ge(sem["scores_done"], K.at("scores_done", n + 1))
                ps = PS[6 + n % 2]
                if self.kind == "na" and s == 0:
                    loc = ps[:, 0:SEQ].rearrange("p (r c) -> p r c", c=GRID_W)
                    e.tensor_tensor(loc, loc, BIAS[:, h, 2 - 2 * qt:6 - 2 * qt, :], ALU.add) \
                        .then_inc(K.up("dve_done"), 1)
                    e.wait_ge(sem["dve_done"], K.own("dve_done"))
                e.tensor_reduce(SM[:, n % 2:n % 2 + 1], ps[:, 0:c1 - c0], AX.X, ALU.max, negate=True) \
                    .then_inc(K.up("max_done"), 1)

            def normalise(n):
                s, h, qt = self.steps[n]
                c0, c1 = self.keys(s)
                e.wait_ge(sem["exp_done"], K.at("exp_done", n + 1))
                e.reciprocal(SM[:, 4 + n % 2:5 + n % 2], SM[:, 2 + n % 2:3 + n % 2]).then_inc(K.up("dve_done"), 1)
                e.wait_ge(sem["dve_done"], K.own("dve_done"))
                pr = PR[:, n % 2, 0:c1 - c0]
                e.tensor_scalar(pr, pr, SM[:, 4 + n % 2:5 + n % 2], None, ALU.mult).then_inc(K.up("probs_ready"), 1)

            def out(pair):
                t, tok, cols = self.outputs(pair)
                e.wait_ge(sem["branch_high"], K.at("branch_high", pair + 1))
                e.tensor_tensor(YL[:, t, tok], PS[4][:, cols], YH[:, t, tok].bitcast(F32), ALU.subtract) \
                    .then_inc(K.up("branch_low"), 1)

            e.wait_ge(sem["bias_done"], K.own("bias_done"))
            for n in range(n_steps + 1):
                if n < n_steps:
                    maximum(n)
                if n >= 1:
                    normalise(n - 1)
                if n >= 6 and (n - 6) % 4 == 0:
                    out((n - 6) // 4)
            for pair in range((n_steps - 6) // 4 + 1, n_steps // 4):
                out(pair)

    class Latent:

        def __init__(self, layer, nq):
            self.layer, self.nq = layer, nq

        def sp(self, e, K):
            pass

        pool = sp

        def pe(self, e, K):
            nq = self.nq
            for b in (4, 5, 6, 7):
                reader, count = K.bank[b]
                e.wait_ge(sem[reader], K.value(reader, count))
            e.wait_ge(sem["act_done"], K.at("act_done", 4))
            e.matmul(PS[4][:, 0:nq], ONES[:, :], SQ3[:, 0, 0:nq], start=True, stop=False)
            e.matmul(PS[4][:, 0:nq], ONES[:, :], SQ3[:, 1, 0:nq], start=False, stop=True)
            e.matmul(PS[5][:, :], ONES[:, :], SQ3[:, 2, :], start=True, stop=True).then_inc(K.up("squares_summed"), 1)
            e.matmul(PS[6][64:96, 0:SEQ], CON[64:96, C_ROT:C_ROT + 32], KR[64:96, 0:SEQ], start=True, stop=True) \
                .then_inc(K.up("rotary_done"), 1)
            e.wait_ge(sem["latent_w_loaded"], K.at("latent_w_loaded"))
            e.wait_ge(sem["latent_normed"], K.at("latent_normed", 2))
            def rotate(j):
                if j < 2:
                    reader, count = K.bank[j]
                    e.wait_ge(sem[reader], K.value(reader, count))
                else:
                    e.wait_ge(sem["rotated_done"], K.at("rotated_done", j))
                e.wait_ge(sem["queries_copied"], K.at("queries_copied", 2 * j + 2))
                e.matmul(PS[j % 2][64:96, :], CON[64:96, C_ROT:C_ROT + 32], Q96[64:96, 2 * j:2 * j + 2, 0:SEQ],
                         start=True, stop=True).then_inc(K.up("rotary_done"), 1)

            for h in range(HEADS):
                b = 4 + 2 * (h % 2)
                if h == 1:
                    e.wait_ge(sem["rotated_done"], K.at("rotated_done", 1))
                if h >= 2:
                    e.wait_ge(sem["queries_copied"], K.at("queries_copied", h - 1))
                for k in range(2):
                    ins = e.matmul(PS[b][0:96, 0:nq], W96[:, k, h, :], CQ[:, k, 0:nq], start=k == 0, stop=k == 1)
                ins.then_inc(K.up("qkv_done"), 1)
                if h == 0:
                    e.wait_ge(sem["latent_normed"], K.at("latent_normed", 3))
                if h >= 2:
                    e.wait_ge(sem["keys_copied"], K.at("keys_copied", h - 1))
                e.matmul(PS[b + 1][0:64, :], WUK[:, 64 * h:64 * h + 64], CKV[:, :], start=True, stop=True) \
                    .then_inc(K.up("qkv_done"), 1)
                if h % 2 and h > 1:
                    rotate(h // 2 - 1)
            for t in range(4):
                b = 4 + 2 * (t % 2)
                e.wait_ge(sem["queries_copied"], K.at("queries_copied", 7 + t))
                e.matmul(PS[b][:, :], CKV[:, t * P:(t + 1) * P], WUV, start=True, stop=True) \
                    .then_inc(K.up("qkv_done"), 1)
                if t == 0:
                    rotate(3)
            K.bank[4] = K.bank[6] = ("queries_copied", K.s("queries_copied") + 12)
            K.bank[5] = K.bank[7] = ("keys_copied", K.s("keys_copied") + 8)
            K.bank[0] = K.bank[1] = ("rotated_done", K.s("rotated_done") + 5)

        def act(self, e, K):
            nq = self.nq
            e.activation(SM[:, 8:9], ONES[:, 0:1], ACT.Sqrt).then_inc(K.up("act_done"), 1)
            e.wait_ge(sem["act_read"], K.own("act_read"))
            for t in range(2):
                e.activation(SQ3[:, t, 0:nq], CQ[:, t, 0:nq], ACT.Square).then_inc(K.up("act_done"), 1)
            e.activation(SQ3[:, 2, :], CKV[:, :], ACT.Square).then_inc(K.up("act_done"), 1)
            e.wait_ge(sem["var_done"], K.at("var_done", 1))
            e.activation(RT[:, 0, 0:nq], RT[:, 0, 0:nq], ACT.Sqrt).then_inc(K.up("root_done"), 1)
            e.activation(RT[:, 1, :], RT[:, 1, :], ACT.Sqrt).then_inc(K.up("root_done"), 1)
            for h in range(HEADS):
                e.wait_ge(sem["qkv_done"], K.at("qkv_done", 2 * h + 1))
                e.activation(Q96[0:96, h, 0:nq], PS[4 + 2 * (h % 2)][0:96, 0:nq], ACT.Copy, scale=MLA_SCALE) \
                    .then_inc(K.up("queries_copied"), 1)
            for t in range(4):
                e.wait_ge(sem["qkv_done"], K.at("qkv_done", 17 + t))
                if t == 0:
                    e.wait_ge(sem["squares_summed"], K.at("squares_summed", 1))
                    e.wait_ge(sem["latent_normed"], K.at("latent_normed", 3))
                e.activation(MV[:, t, :], PS[4 + 2 * (t % 2)][:, :], ACT.Copy).then_inc(K.up("queries_copied"), 1)

        def dve(self, e, K):
            nq, l = self.nq, self.layer
            e.wait_ge(sem["squares_summed"], K.at("squares_summed", 1))
            e.tensor_scalar(RT[:, 0, 0:nq], PS[4][:, 0:nq], 1.0 / 256, LN_EPS, ALU.mult, ALU.add) \
                .then_inc(K.up("dve_done"), 1)
            e.tensor_scalar(RT[:, 1, :], PS[5][:, :], 1.0 / 128, LN_EPS, ALU.mult, ALU.add) \
                .then_inc(K.up("var_done"), 1)
            e.wait_ge(sem["rotary_done"], K.at("rotary_done", 1))
            e.wait_ge(sem["act_read"], K.at("act_read"))
            e.tensor_tensor(SM_ROPE[64:96, 0, :], PS[6][64:96, 0:SEQ], SIN, ALU.mult).then_inc(K.up("dve_done"), 1)
            e.wait_ge(sem["dve_done"], K.own("dve_done"))
            e.tensor_tensor(KR[64:96, 0:SEQ], KR[64:96, 0:SEQ], COS, ALU.mult).then_inc(K.up("dve_done"), 1)
            e.wait_ge(sem["dve_done"], K.own("dve_done"))
            e.tensor_tensor(KR[64:96, 0:SEQ], KR[64:96, 0:SEQ], SM_ROPE[64:96, 0, :], ALU.add) \
                .then_inc(K.up("rotated_done"), 1)
            e.wait_ge(sem["root_done"], K.at("root_done", 1))
            e.reciprocal(RT[:, 0, 0:nq], RT[:, 0, 0:nq]).then_inc(K.up("dve_done"), 1)
            e.wait_ge(sem["dve_done"], K.own("dve_done"))
            for t in range(2):
                e.scalar_tensor_tensor(out=CQ[:, t, 0:nq], in0=CQ[:, t, 0:nq], scalar=vec("mla_q_norm_g", 2 * l + t),
                                       in1=RT[:, 0, 0:nq], op0=ALU.mult, op1=ALU.mult) \
                    .then_inc(K.up("latent_normed"), 1)
            e.wait_ge(sem["root_done"], K.at("root_done", 2))
            e.reciprocal(RT[:, 1, :], RT[:, 1, :]).then_inc(K.up("dve_done"), 1)
            e.wait_ge(sem["dve_done"], K.own("dve_done"))
            e.scalar_tensor_tensor(out=CKV[:, :], in0=CKV[:, :], scalar=vec("mla_kv_norm_g", l), in1=RT[:, 1, :],
                                   op0=ALU.mult, op1=ALU.mult).then_inc(K.up("latent_normed"), 1)
            e.wait_ge(sem["rotated_done"], K.own("rotated_done"))
            def rope(j):
                e.wait_ge(sem["rotary_done"], K.at("rotary_done", 2 + j))
                q = Q96[64:96, 2 * j:2 * j + 2, 0:SEQ]
                t = SM_ROPE[64:96, :, :]
                sin, cos = (a.unsqueeze(1).to_broadcast([32, 2, SEQ]) for a in (SIN, COS))
                rotated = PS[j % 2][64:96, :].rearrange("p (h n) -> p h n", h=2)
                e.tensor_tensor(t, rotated, sin, ALU.mult).then_inc(K.up("dve_done"), 1)
                e.tensor_tensor(q, q, cos, ALU.mult).then_inc(K.up("dve_done"), 1)
                e.wait_ge(sem["dve_done"], K.own("dve_done"))
                e.tensor_tensor(q, q, t, ALU.add).then_inc(K.up("rotated_done"), 1)
                e.wait_ge(sem["rotated_done"], K.own("rotated_done"))

            for h in range(HEADS):
                e.tensor_copy(K96[64:96, h, :], KR[64:96, :]).then_inc(K.up("rotary_copied"), 1)
                e.wait_ge(sem["qkv_done"], K.at("qkv_done", 2 * h + 2))
                e.tensor_copy(K96[0:64, h, :], PS[5 + 2 * (h % 2)][0:64, :]).then_inc(K.up("keys_copied"), 1)
                if h % 2 and h > 1:
                    rope(h // 2 - 1)
            rope(3)

    SM_ROPE = reg("ROPE_T", 10752, [P, 2, SEQ])

    class Start:

        def vectors(self, e, K, names, signal):
            for name, n in names:
                t, r = place[name]
                src = A[name].rearrange(DIMS[len(A[name].shape)]).rearrange("(n p) -> n p", p=P)
                e.dma_start(VROWS[r:r + n, t, :], src).then_inc(K.up(signal, 16), 16)

        def sp(self, e, K):
            e.dma_start(XIN[:, 0:2, :], A["x"][0].rearrange("(t p) d -> p t d", p=P)) \
                .then_inc(K.up("tokens_loaded", 16), 16)
            e.dma_start(XIN[:, 2:4, :], A["ctx"][0].rearrange("(t p) d -> p t d", p=P)) \
                .then_inc(K.up("tokens_loaded", 16), 16)
            e.wait_ge(sem["dve_done"], K.at("dve_done", 1))
            self.vectors(e, K, VECTORS[13:], "vectors_loaded")

        def act(self, e, K):
            e.dma_start(CON[:, :], const[:, 0:C_KEEP]).then_inc(K.up("constants_loaded", 16), 16)
            e.wait_ge(sem["dve_done"], K.at("dve_done", 1))
            self.vectors(e, K, VECTORS[:13], "constants_loaded")
            for k in range(KT):
                e.wait_ge(sem["dve_read"], K.at("dve_read", k + 1))
                if k >= 2:
                    e.wait_ge(sem["dve_done"], K.at("dve_done", 4 + 2 * k - 3))
                e.activation(NT[:, k % 2, :], X[:, k, :], ACT.Square).then_inc(K.up("act_done"), 1)
            e.wait_ge(sem["copied_out"], K.at("copied_out", 1))
            for v, name in enumerate(("c", "c_ctx", "c_2")):
                e.activation(CC[:, :, v], vec(name, 0, 8), ACT.Silu).then_inc(K.up("silu_done"), 1)

        def dve(self, e, K):
            e.memset(VROWS[:, :, :], 0.0).then_inc(K.up("dve_done"), 1)
            e.memset(ONES[:, :], 1.0).then_inc(K.up("dve_done"), 1)
            e.memset(SM[:, :], 0.0).then_inc(K.up("dve_done"), 1)
            e.memset(CC[:, :, :], 0.0).then_inc(K.up("dve_done"), 1)

            def add(k):
                if k:
                    e.wait_ge(sem["dve_done"], K.own("dve_done"))
                e.wait_ge(sem["dve_read"], K.at("dve_read", k + 1))
                if k:
                    e.tensor_tensor(S1[:, :], S1[:, :], X[:, k, :], ALU.add).then_inc(K.up("dve_done"), 1)
                else:
                    e.tensor_copy(S1[:, :], X[:, k, :]).then_inc(K.up("dve_done"), 1)
                e.wait_ge(sem["act_done"], K.at("act_done", k + 1))
                square = NT[:, k % 2, :]
                if k:
                    e.tensor_tensor(S2[:, :], S2[:, :], square, ALU.add).then_inc(K.up("dve_done"), 1)
                else:
                    e.tensor_copy(S2[:, :], square).then_inc(K.up("dve_done"), 1)

            for k in range(KT + 1):
                if k < KT:
                    e.wait_ge(sem["x_turned"], K.at("x_turned", k + 1))
                    e.tensor_copy(X[:, k, :], PS[k % 4][:, :]).then_inc(K.up("dve_read"), 1)
                if k:
                    add(k - 1)
            e.wait_ge(sem["vectors_turned"], K.at("vectors_turned", 1))
            e.tensor_copy(VEC[:, :, :], PS[6][:, :].rearrange("p (t r) -> p t r", t=4)).then_inc(K.up("copied_out"), 1)

        def pe(self, e, K):
            e.wait_ge(sem["constants_loaded"], 16 * 14)
            e.wait_ge(sem["tokens_loaded"], 32)
            for k in range(KT):
                if k >= 4:
                    e.wait_ge(sem["dve_read"], K.at("dve_read", k - 3))
                for t in range(4):
                    ins = e.transpose(PS[k % 4][:, t * P:(t + 1) * P], XIN[:, t, k * P:(k + 1) * P], IDENT)
                ins.then_inc(K.up("x_turned"), 1)
            e.wait_ge(sem["vectors_loaded"], K.at("vectors_loaded", 16 * len(VECTORS[13:])))
            for t in range(4):
                ins = e.transpose(PS[6][:, t * P:(t + 1) * P], VROWS[:, t, :], IDENT)
            ins.then_inc(K.up("vectors_turned"), 1)
            for b in range(4):
                K.bank[b] = ("dve_read", K.s("dve_read") + 5 + b)
            for b in range(4, 8):
                K.bank[b] = ("copied_out", K.s("copied_out") + 1)

        def pool(self, e, K):
            pass

    class EarlySides:

        places = (SIDE, EARLY1, EARLY2, EARLY3)

        def sp(self, e, K):
            for j in range(4):
                e.dma_start(self.places[j][:, :, :], rows(wmod[0])[:, :, j * 512:(j + 1) * 512]) \
                    .then_inc(K.up(f"chunk{j}_loaded", 16), 16)

        def act(self, e, K):
            for j in range(4):
                e.wait_ge(sem["side_rows"], K.at("side_rows", j + 1))
                if j:
                    e.wait_ge(sem["side_turned"], K.at("side_turned", j))
                e.activation(MODROW[:, :], PS[4 + 2 * (j % 2)][:, :], ACT.Copy).then_inc(K.up("side_row_copied"), 1)

        def dve(self, e, K):
            e.wait_ge(sem["copied_out"], K.own("copied_out"))
            name, first = bmod[0]
            t, r = place[name]
            for j in range(4):
                e.wait_ge(sem["side_turned"], K.at("side_turned", j + 1))
                bias = VEC[:, t, r + first + 4 * j:r + first + 4 * j + 4].unsqueeze(2).to_broadcast([P, 4, 3])
                e.tensor_tensor(MODT[:, 0, 4 * j:4 * j + 4, :], PS[5][:, 0:12].rearrange("p (q v) -> p q v", v=3), bias,
                                ALU.add).then_inc(K.up("side_added"), 1)

        def pe(self, e, K):
            e.wait_ge(sem["silu_done"], K.at("silu_done"))

            for b in range(4, 7):
                reader, count = K.bank[b]
                e.wait_ge(sem[reader], K.value(reader, count))

            def rows_of(j):
                e.wait_ge(sem[f"chunk{j}_loaded"], 16)
                if j >= 2:
                    e.wait_ge(sem["side_row_copied"], K.at("side_row_copied", j - 1))
                for k in range(KT):
                    g = k % 4
                    ins = e.matmul(PS[4 + 2 * (j % 2)][32 * g:32 * g + 32, :], CC[:, k, :], self.places[j][:, k, :],
                                   start=k < 4, stop=k >= 4)
                ins.then_inc(K.up("side_rows"), 1)

            rows_of(0)
            for j in range(4):
                if j < 3:
                    rows_of(j + 1)
                e.wait_ge(sem["side_row_copied"], K.at("side_row_copied", j + 1))
                if j:
                    e.wait_ge(sem["side_added"], K.at("side_added", j))
                for q in range(4):
                    ins = e.matmul(PS[5][:, 3 * q:3 * q + 3], MODROW[:, q * P:(q + 1) * P], CON[:, C_SEL:C_SEL + 3],
                                   start=True, stop=True)
                ins.then_inc(K.up("side_turned"), 1)
            for b in (4, 6):
                K.bank[b] = ("side_row_copied", K.s("side_row_copied") + 4)
            K.bank[5] = ("side_added", K.s("side_added") + 4)

        def pool(self, e, K):
            pass

    DIMS = {1: "a -> a", 2: "a b -> (a b)", 3: "a b c -> (a b c)"}

    class Lru:

        def sp(self, e, K):
            pass

        pe = sp

        def act(self, e, K):
            e.wait_ge(sem["lambda_done"], K.at("lambda_done"))
            e.wait_ge(sem["act_read"], K.own("act_read"))
            for half in (range(0, 4), range(4, 8)):
                for k in half:
                    e.activation(LT[:, k, :], LA[:, k, :], ACT.Tanh, scale=DER[:, 7, k:k + 1]) \
                        .then_inc(K.up("act_done"), 1)
                e.wait_ge(sem["act_done"], K.own("act_done"))
                for k in half:
                    e.activation(LA[:, k, :], LA[:, k, :], ACT.Exp, scale=DER[:, 6, k:k + 1]) \
                        .then_inc(K.up("decay_done"), 1)
                for k in half:
                    e.wait_ge(sem["decay_done"], K.at("decay_done", k + 1))
                    e.activation(XR[:, k, 0:SEQ], LA[:, k, :], ACT.Square).then_inc(K.up("decay_squared"), 1)
                for k in half:
                    e.wait_ge(sem["one_minus_a2"], K.at("one_minus_a2", k + 1))
                    e.activation(LT[:, k, :], LT[:, k, :], ACT.Sqrt).then_inc(K.up("root_done"), 1)

        def pool(self, e, K):
            for k in range(KT):
                e.wait_ge(sem["act_read"], K.at("act_read", k - 7))
                e.tensor_tensor(GI[:, k, :], GI[:, k, :], XC[:, k, :], ALU.mult).then_inc(K.up("gated_done"), 1)

        def dve(self, e, K):
            for half in (range(0, 4), range(4, 8)):
                for k in half:
                    e.wait_ge(sem["decay_squared"], K.at("decay_squared", k + 1))
                    e.scalar_tensor_tensor(out=LT[:, k, :], in0=XR[:, k, 0:SEQ], scalar=1.0, in1=LT[:, k, :], op0=ALU.add,
                                           op1=ALU.mult).then_inc(K.up("one_minus_a2"), 1)
                for k in half:
                    e.wait_ge(sem["root_done"], K.at("root_done", k + 1))
                    e.wait_ge(sem["gated_done"], K.at("gated_done", k + 1))
                    e.tensor_tensor(GI[:, k, :], GI[:, k, :], LT[:, k, :], ALU.mult).then_inc(K.up("dve_done"), 1)
                    e.wait_ge(sem["dve_done"], K.own("dve_done"))
                    e.tensor_tensor_scan(XC[:, k, :], LA[:, k, :], GI[:, k, :], 0.0, ALU.mult, ALU.add) \
                        .then_inc(K.up("scanned"), 1)

    class LruOut:

        def sp(self, e, K):
            pass

        pe = sp

        def pool(self, e, K):
            for k in range(KT):
                e.wait_ge(sem["scanned"], K.at("scanned", k - 7))
                if k >= 4:
                    e.wait_ge(sem["act_read"], K.at("act_read", k - 7))
                e.tensor_tensor(XC[:, k, :], XC[:, k, :], GB[:, k, :], ALU.mult).then_inc(K.up("gated_done"), 1)

        def act(self, e, K):
            e.wait_ge(sem["products"], K.at("products"))
            for k in range(KT):
                e.wait_ge(sem["gated_done"], K.at("gated_done", k + 1))
                e.activation(AH[:, k, 0:SEQ], XC[:, k, :], ACT.Copy).then_inc(K.up("modulated"), 1)

        def dve(self, e, K):
            for k in range(KT):
                e.wait_ge(sem["modulated"], K.at("modulated", k + 1))
                e.tensor_tensor(AL[:, k, 0:SEQ], XC[:, k, :], AH[:, k, 0:SEQ].bitcast(F32), ALU.subtract) \
                    .then_inc(K.up("input_low"), 1)

    class Conv(Copied):

        def read_act(self, e, K, m):
            i = self.tile0 + m
            e.activation(XR[:, i, 3:3 + SEQ], PS[m][:, 0:SEQ], ACT.Identity, bias=vec("lru_b_in_2", i)) \
                .then_inc(K.up("act_read"), 1)

        def read_dve(self, e, K, m):
            i = self.tile0 + m
            if i == 0:
                e.memset(XR[:, :, 0:3], 0.0).then_inc(K.up("dve_done"), 1)
                e.wait_ge(sem["dve_done"], K.own("dve_done"))
            e.wait_ge(sem["act_read"], K.at("act_read", m + 1))
            xc = XC[:, i, :]
            e.tensor_scalar(xc, XR[:, i, 0:SEQ], vec("lru_conv_w_2", i), vec("lru_conv_b_2", i), ALU.mult, ALU.add) \
                .then_inc(K.up("dve_done"), 1)
            e.wait_ge(sem["dve_done"], K.own("dve_done"))
            for t in range(1, 4):
                e.scalar_tensor_tensor(out=xc, in0=XR[:, i, t:t + SEQ], scalar=vec("lru_conv_w_2", 8 * t + i),
                                       in1=xc, op0=ALU.mult, op1=ALU.add).then_inc(K.up("dve_done"), 1)
                e.wait_ge(sem["dve_done"], K.own("dve_done"))
            e.tensor_copy(Y8H[:, i, :], xc).then_inc(K.up("dve_done"), 1)
            e.wait_ge(sem["dve_done"], K.own("dve_done"))
            e.tensor_tensor(Y8L[:, i, :], xc, Y8H[:, i, :].bitcast(F32), ALU.subtract).then_inc(K.up("hidden_low"), 1)

    class Blocks(Columns):

        kt = 2
        tokens = (0, SEQ)
        ready = ("hidden_low", True)

        def src(self, K, p):
            return rows(self.w[2 * self.u + p])

        def part(self, m, k):
            return 2 * (2 * self.u + m // 2) + k

        def moving(self, m, k, c0, c1):
            i = self.part(m, k)
            return Y8H[:, i, :], Y8L[:, i, :]

    class GateBlocks(Blocks):
        def read_act(self, e, K, m):
            i = 4 * self.u + m
            e.activation(self.dst[:, i, :], PS[m][:, 0:SEQ], ACT.Sigmoid, bias=vec(self.bias, i)) \
                .then_inc(K.up("act_read"), 1)

    class PoolBlocks(Blocks, Residual):
        read = "dddd"
        src = Blocks.src

    class Pooling:

        def sp(self, e, K):
            pass

        pe = sp

        def group(self, e, K, g, done):
            lo, last = 2 * g, 16 + SEQ
            e.wait_ge(sem["x_normed"], K.at("x_normed", lo + 2 - KT))
            a = PA
            for j in range(g + 1):
                lag, o = 1 << j, (PS1, PS2)[j % 2]
                e.tensor_tensor(o[:, lo:lo + 2, 16:last], a[:, lo:lo + 2, 16:last],
                                a[:, lo:lo + 2, 16 - lag:last - lag], ALU.add).then_inc(K.up(done), 1)
                e.wait_ge(sem[done], K.own(done))
                a = o
            inv = PINV[:, g, :].unsqueeze(1).to_broadcast([P, 2, SEQ])
            o = a[:, lo:lo + 2, 16:last]
            e.tensor_tensor(o, o, inv, ALU.mult).then_inc(K.up(done), 1)
            e.wait_ge(sem[done], K.own(done))
            e.tensor_tensor(o, o, PA[:, lo:lo + 2, 16:last], ALU.subtract) \
                .then_inc(K.up("pooled_last" if g == 3 else "pooled"), 1)

        def result(self, g):
            return (PS1, PS2)[g % 2][:, 2 * g:2 * g + 2, 16:16 + SEQ]

        def dve(self, e, K):
            def low(g):
                e.wait_ge(sem["modulated"], K.at("modulated", g + 1))
                for j in range(2):
                    high = Y8H[:, 2 * g + j, :].bitcast(F32)
                    e.tensor_tensor(Y8L[:, 2 * g + j, :], self.result(g)[:, j, :], high, ALU.subtract) \
                        .then_inc(K.up("hidden_low"), 1)

            for buf in (PA, PS1, PS2):
                e.memset(buf[:, :, 0:16], 0.0).then_inc(K.up("dve_done"), 1)
            e.wait_ge(sem["dve_done"], K.own("dve_done"))
            e.wait_ge(sem["constants_loaded"], K.at("constants_loaded"))
            self.group(e, K, 0, "dve_done")
            self.group(e, K, 1, "dve_done")
            low(0)
            self.group(e, K, 2, "dve_done")
            for g in range(1, 4):
                low(g)

        def pool(self, e, K):
            e.wait_ge(sem["dve_done"], K.at("dve_done", 3))
            e.wait_ge(sem["constants_loaded"], K.at("constants_loaded"))
            self.group(e, K, 3, "gated_done")

        def act(self, e, K):
            e.wait_ge(sem["products"], K.at("products"))
            for g in range(4):
                if g < 3:
                    e.wait_ge(sem["pooled"], K.at("pooled", g + 1))
                else:
                    e.wait_ge(sem["pooled_last"], K.at("pooled_last", 1))
                e.activation(Y8H[:, 2 * g:2 * g + 2, :], self.result(g), ACT.Copy).then_inc(K.up("modulated"), 1)

    class Finish:

        def pool(self, e, K):
            pass

        def pe(self, e, K):
            for b in range(4):
                reader, count = K.bank[b]
                e.wait_ge(sem[reader], K.value(reader, count))
            e.wait_ge(sem["x_normed"], K.at("x_normed"))
            for t in range(2):
                for half in range(2):
                    for j in range(4):
                        ins = e.transpose(PS[2 * t + half][:, j * P:(j + 1) * P],
                                          OUTT[:, 4 * half + j, t * P:(t + 1) * P], IDENT)
                    ins.then_inc(K.up("x_turned"), 1)

        def dve(self, e, K):
            for n in range(0, 4, 2):
                e.wait_ge(sem["x_turned"], K.at("x_turned", n + 1))
                e.tensor_copy(OUTS[:, n // 2, 0:512], PS[n][:, :]).then_inc(K.up("copied_out"), 1)

        def act(self, e, K):
            for n in range(1, 4, 2):
                e.wait_ge(sem["x_turned"], K.at("x_turned", n + 1))
                e.activation(OUTS[:, n // 2, 512:1024], PS[n][:, :], ACT.Copy).then_inc(K.up("act_done"), 1)

        def sp(self, e, K):
            for t in range(2):
                e.wait_ge(sem["copied_out"], K.at("copied_out", t + 1))
                e.wait_ge(sem["act_done"], K.at("act_done", t + 1))
                e.dma_start(out[0].rearrange("(t p) d -> p t d", p=P)[:, t, :], OUTS[:, t, :]) \
                    .then_inc(K.up("out_done", 16), 16)
            e.wait_ge(sem["out_done"], K.at("out_done", 32))

    class LruConst:

        def sp(self, e, K):
            pass

        pe = pool = sp

        def dve(self, e, K):
            lam = vec("lru_lambda_2", 0, 8)
            w, z, y, q, m = (DER[:, j, :] for j in (8, 9, 10, 11, 5))
            
            def st(ins):
                ins.then_inc(K.up("dve_done"), 1)
                e.wait_ge(sem["dve_done"], K.own("dve_done"))

            st(e.tensor_scalar(w, lam, -1.0, None, ALU.mult))
            e.tensor_tensor(w, w, lam, ALU.max).then_inc(K.up("lambda_done"), 1)
            e.wait_ge(sem["silu_done"], K.at("silu_done", 1))
            st(e.tensor_scalar(z, w, 2.0, None, ALU.add))
            st(e.reciprocal(z, z))
            st(e.tensor_tensor(z, z, w, ALU.mult))
            st(e.tensor_tensor(y, z, z, ALU.mult))
            st(e.memset(q, 1.0 / 17))
            for n in (15, 13, 11, 9, 7, 5, 3, 1):
                st(e.tensor_tensor(q, q, y, ALU.mult))
                st(e.tensor_scalar(q, q, 1.0 / n, None, ALU.add))
            st(e.tensor_tensor(z, z, q, ALU.mult))
            st(e.tensor_scalar(m, lam, 0.0, None, ALU.min))
            st(e.scalar_tensor_tensor(out=z, in0=z, scalar=-2.0, in1=m, op0=ALU.mult, op1=ALU.add))
            st(e.tensor_scalar(DER[:, 6, :], z, 8.0, None, ALU.mult))
            e.tensor_scalar(DER[:, 7, :], z, -8.0, None, ALU.mult).then_inc(K.up("lambda_done"), 1)
            e.wait_ge(sem["lambda_done"], K.own("lambda_done"))

        def act(self, e, K):
            e.wait_ge(sem["lambda_done"], K.at("lambda_done", 1))
            e.activation(DER[:, 8, :], DER[:, 8, :], ACT.Exp, scale=-1.0).then_inc(K.up("silu_done"), 1)

    def prep_ln(gname, bname, row, alpha, mat, chunk_sc, streams):
        def f(e, K):
            e.tensor_scalar(DER[:, 0, :], vec(gname, row, 8), alpha, None, ALU.mult).then_inc(K.up("dve_done"), 1)
            e.tensor_scalar(DER[:, 1, :], vec(bname, row, 8), alpha, None, ALU.mult).then_inc(K.up("dve_done"), 1)
            if mat is not None:
                e.wait_ge(sem["side_added"], K.own("side_added"))
                for s in range(streams):
                    e.tensor_scalar(DER[:, 2 + s, :], mod(mat, chunk_sc, s), 1.0, 1.0 / alpha, ALU.add, ALU.mult) \
                        .then_inc(K.up("dve_done"), 1)
        return f

    def prep_gain(mat, chunk, streams):
        def f(e, K):
            e.wait_ge(sem["side_added"], K.own("side_added"))
            for s in range(streams):
                e.tensor_scalar(DER[:, 4 + s, :], mod(mat, chunk, s), 1.0, None, ALU.add).then_inc(K.up("dve_done"), 1)
                e.wait_ge(sem["dve_done"], K.own("dve_done"))
        return f

    def prep_rms(gname, row, mat, chunk_sc):
        def f(e, K):
            e.wait_ge(sem["side_added"], K.own("side_added"))
            e.scalar_tensor_tensor(out=DER[:, 2, :], in0=mod(mat, chunk_sc, 2), scalar=1.0,
                                   in1=vec(gname, row, 8), op0=ALU.add, op1=ALU.mult).then_inc(K.up("dve_done"), 1)
            e.wait_ge(sem["dve_done"], K.own("dve_done"))
        return f

    def prep_pool(e, K):
        e.wait_ge(sem["side_added"], K.own("side_added"))
        e.tensor_tensor(DER[:, 3, :], mod(3, 2, 2), vec("pool_scale_2", 0, 8), ALU.mult).then_inc(K.up("dve_done"), 1)
        e.wait_ge(sem["dve_done"], K.own("dve_done"))

    seq = []
    wi = [A["w_in"][l] for l in range(2)]

    def sides(layer):
        return iter(SIDES[layer])

    SIDES = {
        0: [(0, c) for c in range(4, 12)] + [(2, c) for c in range(4)],
        1: [(2, c) for c in range(9, 12)] + [(3, c) for c in range(9)],
    }

    def up_gated(l, tokens, col, h0, per, side, by_k=False):
        return UpGated(by_k=by_k, layer=l, tokens=tokens, col=col, h0=h0, per_turn=per, side=side, ready=("input_low", True))

    def next_side(it):
        s = next(it, None)
        return Side(*s) if s else None

    seq.append(Start())

    for l in range(2):
        N = TOK if l == 0 else SEQ
        streams = N // SEQ
        tok = (0, N)
        it = sides(l)
        if l == 0:
            norm = Norm(tokens=tok, g=lambda k: DER[:, 0, k:k + 1], b=lambda k: DER[:, 1, k:k + 1], split=True,
                        sc=lambda s, k: DER[:, 2 + s, k:k + 1], sh=lambda s, k: mod(0, 0, s, k),
                        prep=prep_ln("ln_in_g", "ln_in_b", 0, ALPHA, 0, 1, 2))
            seq += [Spread(norm), EarlySides(), norm]
        seq.append(LoadTransform())
        seq.append(Copied(w=wi[l], cols=(0, 256), tokens=tok, side=next_side(it), ready=("input_low", True), by_k=True,
                          dst=lambda m, N=N: FT[:, m, 0:N]))
        if l == 0:
            first_unit = seq[-1]
        def merge(b, between=()):
            for half in range(2):
                g0 = 2464 + b * D + half * 512
                seq.append(Copied(w=wi[l], cols=(g0, g0 + 256), tokens=tok, side=next_side(it), func=ACT.Sigmoid,
                                  dst=lambda m, N=N: GATE[:, m, 0:N]))
                if half == 0:
                    seq.extend(between)
                seq.append(Branch(w=A["w_branch"][l][b], cols=(half * 512, half * 512 + 256), tokens=tok, b=b,
                                  half=half, ready=("branch_low", False)))

        merge(0, [Fourier(streams)])
        seq.append(Copied(w=wi[l], cols=(512, 768), tokens=tok, side=next_side(it), scale=NA_SCALE,
                          dst=lambda m, N=N: NQ[:, m, 0:N]))
        seq.append(LoadRpb(l))
        seq.append(Copied(w=wi[l], cols=(1024, 1280), side=next_side(it), dst=lambda m: NK[:, m, :]))
        seq.append(Bias())
        seq.append(Values(w=wi[l], cols=(1536, 1792), side=next_side(it)))
        seq.append(Attention("na", streams))
        merge(1)
        small = Compressed(w=wi[l], cols=(2048, 2304), offs=(0, P, 0, 64), tokens=tok,
                       dst=lambda m, N=N: (CQ[:, 0, 0:N], CQ[:, 1, 0:N], CKV[:, :], KR[:, :])[m])
        seq.append(LoadLatentWeights(l))
        if l == 1:
            seq.append(LruConst())
        seq.append(small)
        seq.append(Latent(l, N))
        seq.append(Attention("mla", streams))
        merge(2)
        for half in range(2):
            seq.append(Residual(w=A["w_out"][l], cols=(half * 512, half * 512 + 256), tokens=tok, rhs=(HH, HL),
                                ready=("hidden_low", True), late=4 if half == 0 else 0, side=next_side(it), tile0=4 * half, first=half == 0,
                                scale=lambda s, i: DER[:, 4 + s, i:i + 1], prep=prep_gain(l, 2, streams) if half == 0 else None))
        seq.append(Norm(tokens=tok, g=lambda k: DER[:, 0, k:k + 1], b=lambda k: DER[:, 1, k:k + 1],
                        sc=lambda s, k: DER[:, 2 + s, k:k + 1], sh=lambda s, k, l=l: mod(l, 3, s, k),
                        prep=prep_ln("ln1_g", "ln1_b", 8 * l, ALPHA, l, 4, streams)))
        assert next(it, None) is None, "a modulation chunk has no place"

        def down(krow, kt, half, per, side, last):
            return Down(w=A["w_ffn_down"][l], cols=(half * 512, half * 512 + 256), tokens=tok, krow=krow, kt=kt,
                        rhs_count=kt, per_turn=per, side=side, tile0=4 * half, first=half == 0, stats=last, late=0 if half else 2,
                        scale=lambda s, i: DER[:, 4 + s, i:i + 1],
                        prep=prep_gain(l, 5, streams) if half == 0 else None)

        hosted = [(2, c) for c in range(4, 9)] if l == 0 else [(3, 9), (3, 10), (3, 11)]
        hosted = [Side(*c) for c in hosted] + [None] * (5 - len(hosted))
        seq += [up_gated(l, tok, 2048 + 256 * u, 2 * u, 0, hosted[u], by_k=u == 0) for u in range(3)]
        seq += [down(16, 6, half, 0, hosted[3 + half], False) for half in range(2)]
        body = [up_gated(l, tok, 256 * u, 2 * u, 1024, Side(1, u, 6) if l == 0 else None) for u in range(4)]
        body += [down(0, 8, half, 8, Side(1, 4 + half, 6) if l == 0 else None, True) for half in range(2)]
        seq.append(("loop", 2, body))
        final = l == 1
        seq.append(Norm(tokens=tok, g=lambda k: DER[:, 0, k:k + 1], b=lambda k: DER[:, 1, k:k + 1],
                        sc=lambda s, k: DER[:, 2 + s, k:k + 1], sh=lambda s, k: mod(1, 0, s, k),
                        to=None if final else "a", stats=final,
                        prep=prep_ln("ln2_g", "ln2_b", 8 * l, 1.0 if final else ALPHA, None if final else 1, 1, 2)))

    lat = (0, SEQ)

    def rms(gname, row, mat, chunk, **kw):
        return Norm(tokens=lat, mean=False, write_x=False, eps=RMS_EPS, sc=lambda s, k: DER[:, 2, k:k + 1],
                    sh=lambda s, k: mod(mat, chunk, 2, k), prep=prep_rms(gname, row, mat, chunk + 1), **kw)

    def mlp(layer):
        w1, w2 = A["ffn_w1_2"][layer], A["ffn_w2_2"][layer]

        def part(base, per, first, last=False):
            units = [UpSquared(by_k=first and u == 0, w=w1, cols=(base * P + 512 * u, base * P + 512 * u + 256), per_turn=per * P, h0=4 * u,
                               ready=("input_low", True)) for u in range(2)]
            units += [Down(w=w2, cols=(half * 512, half * 512 + 256), tokens=lat, krow=base, kt=8, per_turn=per,
                           tile0=4 * half, first=half == 0, stats=last, mean=False, rhs_count=8,
                           late=0 if half else 4,
                           scale=lambda s, i: mod(2 + layer, 5, 2, i)) for half in range(2)]
            return units

        seq.extend(part(0, 0, True))
        seq.append(("loop", 2, part(8, 8, False)))
        seq.extend(part(24, 0, False, True))

    seq.append(rms("norm_mix_g_2", 0, 2, 0, summed=True))
    seq += [Conv(w=A["lru_w_in_2"][0], cols=(half * 512, half * 512 + 256), tokens=lat, tile0=4 * half,
                 ready=("input_low", True), by_k=half == 0) for half in range(2)]
    gelu = [Gelu(w=A["lru_w_y_2"][0], cols=(half * 512, half * 512 + 256), tokens=lat, tile0=4 * half)
            for half in range(2)]
    seq.append(gelu[0])
    seq += [GateBlocks(w=A["lru_w_a_2"][0], u=u, dst=LA, bias="lru_b_a_2") for u in range(2)]
    seq += [GateBlocks(w=A["lru_w_x_2"][0], u=u, dst=GI, bias="lru_b_x_2") for u in range(2)]
    seq += [Lru(), gelu[1], LruOut()]
    seq += [Residual(w=A["lru_w_out_2"][0], cols=(half * 512, half * 512 + 256), tokens=lat, tile0=4 * half,
                     first=half == 0, mean=False, bias="lru_b_out_2", ready=("input_low", True), by_k=half == 0,
                     scale=lambda s, i: mod(2, 2, 2, i)) for half in range(2)]
    seq.append(rms("norm_ffn_g_2", 0, 2, 3))
    mlp(0)
    seq.append(rms("norm_mix_g_2", 8, 3, 0, to="pool"))
    seq.append(LoadWindows())
    seq.append(Pooling())
    pool_units = [PoolBlocks(w=A["pool_w_2"][0], u=u, tile0=4 * u, first=u == 0, mean=False, prep=prep_pool if u == 0 else None,
                             scale=lambda s, i: DER[:, 3, i:i + 1]) for u in range(2)]
    seq += pool_units
    seq.append(rms("norm_ffn_g_2", 8, 3, 3))
    mlp(1)
    seq.append(Norm(tokens=lat, mean=False, write_x=False, eps=RMS_EPS, to="out", g=lambda k: vec("final_norm_g_2", k)))
    seq.append(Finish())

    groups = []
    for s in seq:
        if isinstance(s, tuple):
            groups.append((s[1], s[2]) if s[0] == "loop" else (1, s[1]))
        else:
            groups.append((1, [s]))
    units = [s for turns, g in groups for s in g if isinstance(s, Unit)]
    for a, b in zip(units, units[1:]):
        a.nxt = b
    groups.insert(2, (1, [First(first_unit)]))
    write_programs(groups, sem, nc, stack)


ENGINES = ("sp", "act", "dve", "pe", "pool")


def program_of(section, engine):
    return {"sp": section.sp, "act": section.act, "dve": section.dve, "pe": section.pe, "pool": section.pool}[engine]


def after_turns(bank, begin, stride, turns):
    return {b: (reader, v + stride[reader] * (turns - 1) if v > begin[reader] else v)
            for b, (reader, v) in bank.items()}


def count_signals(groups, sems):
    dry = {n: Counts(Quiet(), sems, OWN[n], True) for n in ENGINES}
    now = {n: 0 for n in sems}
    starts, strides, banks = {}, [], []
    for gi, (turns, sections) in enumerate(groups):
        begin = dict(now)
        for si, section in enumerate(sections):
            starts[gi, si] = dict(now)
            for engine in ENGINES:
                dry[engine].start = starts[gi, si]
                program_of(section, engine)(dry[engine].eng, dry[engine])
            now = {n: dry[engine].count[n] for engine in ENGINES for n in OWN[engine]}
        stride = {n: now[n] - begin[n] for n in now}
        strides.append(stride)
        banks.append(dict(dry["pe"].bank))
        now = {n: begin[n] + stride[n] * turns for n in now}
        for engine in ENGINES:
            dry[engine].count = {n: now[n] for n in OWN[engine]}
        dry["pe"].bank = after_turns(dry["pe"].bank, begin, stride, turns)
    return starts, strides, banks


def write_programs(groups, sems, nc, stack):
    starts, strides, banks = count_signals(groups, sems)

    def program(engine, eng):
        K = Counts(eng, sems, OWN[engine])
        for gi, (turns, sections) in enumerate(groups):
            begin, stride = starts[gi, 0], strides[gi]
            if turns == 1:
                for si, section in enumerate(sections):
                    K.start = starts[gi, si]
                    program_of(section, engine)(eng, K)
            elif any(stride[n] for n in K.names):
                if engine == "pe":
                    for b, (reader, v) in sorted(banks[gi].items()):
                        if v > begin[reader]:
                            before, count = K.bank[b]
                            eng.wait_ge(sems[before], count)
                            K.bank[b] = (reader, v - stride[reader])
                with eng.Fori(0, turns) as turn:
                    K.turn, K.stride = turn, stride
                    for si, section in enumerate(sections):
                        K.start = starts[gi, si]
                        program_of(section, engine)(eng, K)
                    K.turn, K.stride = None, {}
                K.count = {n: begin[n] + stride[n] * turns for n in K.names}
                K.bank = after_turns(K.bank, begin, stride, turns)

    block = stack.enter_context(nc.Block())

    @block.sync
    def _(sp):
        program("sp", sp)

    @block.scalar
    def _(act):
        program("act", act)

    @block.vector
    def _(dve):
        program("dve", dve)

    @block.tensor
    def _(pe):
        program("pe", pe)

    @block.gpsimd
    def _(pool):
        program("pool", pool)

    stack.close()


def kernel(**inputs):
    import concourse.bacc as bacc
    from concourse.bass_utils import run_bass_kernel_spmd

    nc = bacc.Bacc("TRN2", target_bir_lowering=False, num_devices=1)
    arrays, aps = {}, {}
    for name in INPUTS:
        a = np.asarray(inputs[name])
        if name == "na_rpb":
            a = a[:, :, ::-1, ::-1]
        a = np.ascontiguousarray(a)
        arrays[f"in_{name}"] = a
        aps[name] = nc.dram_tensor(f"in_{name}", a.shape, mybir.dt.from_np(a.dtype), kind="ExternalInput").ap()
    arrays["in_constants"] = constants()
    const = nc.dram_tensor("in_constants", (P, C_ALL), F32, kind="ExternalInput").ap()
    out = nc.dram_tensor("out", (1, SEQ, D), F32, kind="ExternalOutput").ap()
    build(nc, aps, out, const)
    r = run_bass_kernel_spmd(nc, [arrays], core_ids=[0])
    return np.asarray(r.results[0]["out"])
```
